# Optimizing a Trainium2 kernel written in Bass

```python
import math
import jax, jax.numpy as jnp
from jax import lax
import numpy as np

D_MODEL = 1024
BATCH = 1
SEQ = 1024
DEPTH = 1

GLA_HEADS = 4
GLA_DK = 64
GLA_DV = 128
GLA_QK_WIDTH = GLA_HEADS * GLA_DK
GLA_WIDTH = GLA_HEADS * GLA_DV
GATE_RANK = 16
GATE_NORMALIZER = 16.0
CHUNK = 64
CONV_WIDTH = D_MODEL // 2
CONV_GROUPS = 8
CONV_K = 3
MIX_WIDTH = GLA_WIDTH + CONV_WIDTH
D_FF = int(math.ceil(8 * D_MODEL / 3 / 256) * 256)
NORM_EPS = 1e-6

COL_Q = GLA_QK_WIDTH
COL_K = GLA_QK_WIDTH
COL_V = GLA_WIDTH
COL_G = GLA_WIDTH
COL_A = GATE_RANK
COL_CB = CONV_WIDTH
COL_CC = CONV_WIDTH
COL_CH = CONV_WIDTH
IN_COLS = COL_Q + COL_K + COL_V + COL_G + COL_A + COL_CB + COL_CC + COL_CH


def rmsnorm(x, g):
    xf = x.astype(jnp.float32)
    y = xf * lax.rsqrt(jnp.mean(xf * xf, axis=-1, keepdims=True) + NORM_EPS)
    return (y * g.astype(jnp.float32)).astype(x.dtype)

def gla_chunked(q, k, v, log_a):
    bsz, seq, heads, dk = q.shape
    dv = v.shape[-1]
    n_chunks = seq // CHUNK

    def to_chunks(t):
        return t.astype(jnp.float32).reshape(bsz, n_chunks, CHUNK, heads, t.shape[-1]).transpose(1, 0, 3, 2, 4)

    q, k, v, log_a = to_chunks(q), to_chunks(k), to_chunks(v), to_chunks(log_a)
    b = jnp.cumsum(log_a, axis=-2)
    b_last = b[..., -1:, :]
    q_i = q * jnp.exp(b)
    k_i = k * jnp.exp(-b)
    k_s = k * jnp.exp(b_last - b)

    causal = jnp.tril(jnp.ones((CHUNK, CHUNK), dtype=bool))
    scores = jnp.einsum('nbhck,nbhsk->nbhcs', q_i, k_i)
    scores = jnp.where(causal, scores, 0.0)
    o_intra = jnp.einsum('nbhcs,nbhsv->nbhcv', scores, v)

    chunk_kv = jnp.einsum('nbhsk,nbhsv->nbhkv', k_s, v)
    chunk_decay = jnp.exp(b_last[..., 0, :])

    def step(state, inp):
        dec, kv_c = inp
        return dec[..., None] * state + kv_c, state

    state0 = jnp.zeros((bsz, heads, dk, dv), jnp.float32)
    _, state_prev = lax.scan(step, state0, (chunk_decay, chunk_kv))
    o_inter = jnp.einsum('nbhck,nbhkv->nbhcv', q_i, state_prev)

    o = o_intra + o_inter
    return o.transpose(1, 0, 3, 2, 4).reshape(bsz, seq, heads, dv)

def causal_depthwise_conv(u, w):
    seq = u.shape[1]
    u_pad = jnp.pad(u, ((0, 0), (CONV_K - 1, 0), (0, 0)))
    y = w[0] * u_pad[:, 0:seq]
    for j in range(1, CONV_K):
        y = y + w[j] * u_pad[:, j:j + seq]
    return y

def first_inputs(seed: int = 0) -> dict:
    key = jax.random.key(seed)
    ks = jax.random.split(key, 16)
    f32 = jnp.float32
    n = lambda k, shape, scale: (jax.random.normal(k, shape, f32) * scale)
    return {
        "x": n(ks[0], (BATCH, SEQ, D_MODEL), 1.0),
        "norm1_g": 1.0 + n(ks[1], (DEPTH, D_MODEL), 0.02),
        "w_in": n(ks[2], (DEPTH, D_MODEL, IN_COLS), D_MODEL ** -0.5),
        "w_gate_up": n(ks[3], (DEPTH, GATE_RANK, GLA_QK_WIDTH), GATE_RANK ** -0.5),
        "b_gate": n(ks[4], (DEPTH, GLA_QK_WIDTH), 0.01),
        "gla_norm_g": 1.0 + n(ks[5], (DEPTH, GLA_DV), 0.02),
        "conv_w": n(ks[6], (DEPTH, CONV_K, CONV_WIDTH), CONV_K ** -0.5),
        "w_out": n(ks[7], (DEPTH, MIX_WIDTH, D_MODEL), MIX_WIDTH ** -0.5),
        "norm2_g": 1.0 + n(ks[8], (DEPTH, D_MODEL), 0.02),
        "w_ffn_gate": n(ks[9], (DEPTH, D_MODEL, D_FF), D_MODEL ** -0.5),
        "w_ffn_up": n(ks[10], (DEPTH, D_MODEL, D_FF), D_MODEL ** -0.5),
        "w_ffn_down": n(ks[11], (DEPTH, D_FF, D_MODEL), D_FF ** -0.5),
        "norm_f_g": 1.0 + n(ks[12], (D_MODEL,), 0.02),
    }

def first_block(x, norm1_g, w_in, w_gate_up, b_gate, gla_norm_g, conv_w, w_out,
              norm2_g, w_ffn_gate, w_ffn_up, w_ffn_down, norm_f_g):
    bsz, seq, _ = x.shape
    splits = np.cumsum([COL_Q, COL_K, COL_V, COL_G, COL_A, COL_CB, COL_CC])
    for l in range(DEPTH):
        h = rmsnorm(x, norm1_g[l])
        proj = h @ w_in[l]
        p_q, p_k, p_v, p_g, p_a, c_b, c_c, c_h = jnp.split(proj, splits, axis=-1)

        q = p_q.reshape(bsz, seq, GLA_HEADS, GLA_DK) * (GLA_DK ** -0.5)
        k = p_k.reshape(bsz, seq, GLA_HEADS, GLA_DK)
        v = p_v.reshape(bsz, seq, GLA_HEADS, GLA_DV)
        gate_logits = (p_a @ w_gate_up[l] + b_gate[l]).astype(jnp.float32)
        log_a = (jax.nn.log_sigmoid(gate_logits) / GATE_NORMALIZER).reshape(bsz, seq, GLA_HEADS, GLA_DK)
        o = gla_chunked(q, k, v, log_a)
        o = rmsnorm(o, gla_norm_g[l]).astype(x.dtype)
        o = o * jax.nn.silu(p_g.reshape(bsz, seq, GLA_HEADS, GLA_DV))
        o_gla = o.reshape(bsz, seq, GLA_WIDTH)

        u = c_c * c_h
        o_conv = c_b * causal_depthwise_conv(u, conv_w[l])

        mixed = jnp.concatenate([o_gla, o_conv], axis=-1) @ w_out[l]
        x = x + mixed

        h2 = rmsnorm(x, norm2_g[l])
        ffn = (jax.nn.silu(h2 @ w_ffn_gate[l]) * (h2 @ w_ffn_up[l])) @ w_ffn_down[l]
        x = x + ffn
    return rmsnorm(x, norm_f_g)


CHUNK_2 = 128
A_WIDTH = D_MODEL
A_GROUPS = 8
A_GROUP_DIM = A_WIDTH // A_GROUPS
N_HEADS = 16
HEAD_DIM = 64
B_WIDTH = N_HEADS * HEAD_DIM
DILATED_PATTERNS = ((128, 1), (512, 4), (2048, 16))
BLOCK = 128
N_BRANCHES = 2
EPS = 1e-6
NEG_INF = -1e30
IN_COLS_2 = 3 * A_WIDTH + 4 * B_WIDTH + N_BRANCHES * D_MODEL


def rmsnorm_2(x, g):
    xf = x.astype(jnp.float32)
    y = xf * lax.rsqrt(jnp.mean(xf * xf, axis=-1, keepdims=True) + EPS)
    return (y * g.astype(jnp.float32)).astype(x.dtype)

def chunked_spatial_gating(u, v, w_s, b_s, g_v):
    Bn, S, _ = v.shape
    v = rmsnorm_2(v, g_v)
    vc = v.reshape(Bn, S // CHUNK_2, CHUNK_2, A_GROUPS, A_GROUP_DIM)
    causal = jnp.tril(jnp.ones((CHUNK_2, CHUNK_2), dtype=bool))
    w = jnp.where(causal[None], w_s, 0).astype(v.dtype)
    mixed = jnp.einsum('gts,bcsgd->bctgd', w, vc) + b_s.T[None, None, :, :, None]
    return u * mixed.reshape(Bn, S, A_WIDTH)

def dilated_pattern(q, k, v, slopes, window, dilation):
    Bn, H, S, Dh = q.shape
    L = S // dilation
    nback = window // dilation
    nb = -(-L // BLOCK)
    pad = nb * BLOCK - L

    def to_blocks(t):
        t = t.reshape(Bn, H, L, dilation, Dh).transpose(0, 1, 3, 2, 4)
        t = jnp.pad(t, ((0, 0), (0, 0), (0, 0), (0, pad), (0, 0)))
        return t.reshape(Bn, H, dilation, nb, BLOCK, Dh)

    qb, kb, vb = to_blocks(q), to_blocks(k), to_blocks(v)

    def with_prev(t):
        prev = jnp.pad(t, ((0, 0), (0, 0), (0, 0), (1, 0), (0, 0), (0, 0)))[:, :, :, :-1]
        return jnp.concatenate([prev, t], axis=4)

    kw, vw = with_prev(kb), with_prev(vb)
    qpos = jnp.arange(BLOCK)[:, None] + BLOCK
    kpos = jnp.arange(2 * BLOCK)[None, :]
    dist = qpos - kpos
    key_idx = (jnp.arange(nb)[:, None, None] - 1) * BLOCK + kpos[None]
    valid = (dist >= 0) & (dist <= nback) & (key_idx >= 0)

    s = jnp.einsum('bhrnqd,bhrnkd->bhrnqk', qb, kw) * (Dh ** -0.5)
    s = s - slopes[None, :, None, None, None, None] * (dist * dilation).astype(jnp.float32)
    s = jnp.where(valid[None, None, None], s, NEG_INF)
    m = jnp.max(s, axis=-1)
    p = jnp.exp(s - m[..., None])
    l = jnp.sum(p, axis=-1)
    o = jnp.einsum('bhrnqk,bhrnkd->bhrnqd', p, vw) / l[..., None]

    def from_blocks(t):
        t = t.reshape(Bn, H, dilation, nb * BLOCK, *t.shape[5:])[:, :, :, :L]
        t = jnp.moveaxis(t, 2, 3)
        return t.reshape(Bn, H, S, *t.shape[4:])

    return from_blocks(o), from_blocks(m), from_blocks(l)

def dilated_attention(q, k, v):
    Bn, S, _ = q.shape
    heads = lambda t: t.astype(jnp.float32).reshape(Bn, S, N_HEADS, HEAD_DIM).transpose(0, 2, 1, 3)
    qh, kh, vh = heads(q), heads(k), heads(v)
    slopes = 2.0 ** (-8.0 * jnp.arange(1, N_HEADS + 1, dtype=jnp.float32) / N_HEADS)
    outs = [dilated_pattern(qh, kh, vh, slopes, w, d) for (w, d) in DILATED_PATTERNS]
    m_all = jnp.max(jnp.stack([m for (_, m, _) in outs]), axis=0)
    alphas = [l * jnp.exp(m - m_all) for (_, m, l) in outs]
    num = sum(a[..., None] * o for a, (o, _, _) in zip(alphas, outs))
    o = num / sum(alphas)[..., None]
    return o.transpose(0, 2, 1, 3).reshape(Bn, S, B_WIDTH).astype(q.dtype)

def second_inputs(seed: int = 0) -> dict:
    key = jax.random.key(seed)
    ks = jax.random.split(key, 10)
    f32 = jnp.float32
    x = jax.random.normal(ks[0], (BATCH, SEQ, D_MODEL), f32)
    g_norm = 1.0 + 0.05 * jax.random.normal(ks[1], (DEPTH, D_MODEL), f32)
    w_in = jax.random.normal(ks[2], (DEPTH, D_MODEL, IN_COLS_2), f32) * D_MODEL ** -0.5
    w_s = jax.random.normal(ks[3], (DEPTH, A_GROUPS, CHUNK_2, CHUNK_2), f32) * CHUNK_2 ** -0.5
    b_s = 1.0 + 0.1 * jax.random.normal(ks[4], (DEPTH, A_GROUPS, CHUNK_2), f32)
    g_v = 1.0 + 0.05 * jax.random.normal(ks[5], (DEPTH, A_WIDTH), f32)
    w_proj_a = jax.random.normal(ks[6], (DEPTH, A_WIDTH, D_MODEL), f32) * A_WIDTH ** -0.5
    w_proj_b = jax.random.normal(ks[7], (DEPTH, B_WIDTH, D_MODEL), f32) * B_WIDTH ** -0.5
    w_out = jax.random.normal(ks[8], (DEPTH, D_MODEL, D_MODEL), f32) * D_MODEL ** -0.5
    g_final = 1.0 + 0.05 * jax.random.normal(ks[9], (D_MODEL,), f32)
    return {"x": x, "g_norm": g_norm, "w_in": w_in, "w_s": w_s, "b_s": b_s, "g_v": g_v,
            "w_proj_a": w_proj_a, "w_proj_b": w_proj_b, "w_out": w_out, "g_final": g_final}

def second_block(x, g_norm, w_in, w_s, b_s, g_v, w_proj_a, w_proj_b, w_out, g_final):
    splits = [A_WIDTH, 2 * A_WIDTH, 3 * A_WIDTH,
              3 * A_WIDTH + B_WIDTH, 3 * A_WIDTH + 2 * B_WIDTH,
              3 * A_WIDTH + 3 * B_WIDTH, 3 * A_WIDTH + 4 * B_WIDTH]
    for layer in range(DEPTH):
        h = rmsnorm_2(x, g_norm[layer])
        proj = h @ w_in[layer]
        a_u, a_v, a_gate, q, k, v, b_gate, gate_logits = jnp.split(proj, splits, axis=-1)
        y_a = chunked_spatial_gating(jax.nn.gelu(a_u), jax.nn.gelu(a_v),
                                     w_s[layer], b_s[layer], g_v[layer]) * jax.nn.silu(a_gate)
        y_b = dilated_attention(q, k, v) * jax.nn.silu(b_gate)
        g_a, g_b = jnp.split(jax.nn.sigmoid(gate_logits), N_BRANCHES, axis=-1)
        merged = g_a * (y_a @ w_proj_a[layer]) + g_b * (y_b @ w_proj_b[layer])
        x = x + merged @ w_out[layer]
    return rmsnorm_2(x, g_final)


def setup_inputs(seed=0):
    out = dict(first_inputs(seed))
    for name, value in second_inputs(seed + 1).items():
        if name != "x":
            out[name + "_2"] = value
    return out


def reference(
    x, norm1_g, w_in, w_gate_up, b_gate, gla_norm_g, conv_w, w_out, norm2_g, w_ffn_gate,
    w_ffn_up, w_ffn_down, norm_f_g, g_norm_2, w_in_2, w_s_2, b_s_2, g_v_2, w_proj_a_2,
    w_proj_b_2, w_out_2, g_final_2,
):
    x = first_block(
        x, norm1_g, w_in, w_gate_up, b_gate, gla_norm_g, conv_w, w_out, norm2_g, w_ffn_gate,
        w_ffn_up, w_ffn_down, norm_f_g,
    )
    return second_block(
        x, g_norm_2, w_in_2, w_s_2, b_s_2, g_v_2, w_proj_a_2, w_proj_b_2, w_out_2, g_final_2,
    )


_drawn_inputs = setup_inputs


def setup_inputs(seed=0):
    import zlib

    import numpy as np

    out = dict(_drawn_inputs(seed))
    spreads = {}
    factors = {'b_gate': 8.0,
     'gla_norm_g': 6.447,
     'norm2_g': 4.673,
     'norm_f_g': 2.711,
     'b_s_2': 8.289,
     'g_v_2': 24.472}
    for name, (base, spread) in spreads.items():
        noise = np.random.default_rng([zlib.crc32(name.encode()), seed]).standard_normal(out[name].shape)
        drawn = base * np.exp(spread * noise) if base else spread * noise
        out[name] = __import__('jax').numpy.asarray(drawn.astype(out[name].dtype))
    for name, factor in factors.items():
        out[name] = (out[name] * factor).astype(out[name].dtype)
    return out
```

```python
import concourse.bass as bass
from concourse import mybir
from contextlib import ExitStack
import numpy as np

P = 128
D = 1024
S = 1024
KT = D // P
HALF = 512
EPS = 1e-6
GLA_HEADS, DK, DV, CHUNK, RANK = 4, 64, 128, 64, 16
NCH = S // CHUNK
NBLK = S // P
D_FF = 2816
HEADS, DH = 16, 64
PAIRS = HEADS // 2

U_A = 0
U_Q, U_K, U_V, U_G = 1, 3, 5, 9
U_CONV = 13
U_OUT = 25
FFN = [(33, 8, 49), (57, 8, 73), (81, 6, 93)]
U_AV = 101
U_QKV = 109
U_AU = 133
U_ATT = 141
U_PA, U_PB, U_WO = 173, 181, 189
UNITS = 197

V_G1, V_BG, V_GN, V_CW, V_G2, V_GF, V_H2, V_GV, V_FIN, V_SL = 0, 8, 10, 11, 23, 31, 39, 47, 55, 63
VECS = V_SL + HEADS


class Unit:

    def __init__(self, c, reg=None, a=0):
        self.c, self.reg, self.a = c, reg, a

    def plus(self, n):
        return Unit(self.c + n, self.reg, self.a)

    @property
    def slot(self):
        return self.c % 2

    def count(self, n=0):
        return self.c + n if self.reg is None else self.reg * self.a + (self.c + n)

    def turn(self, scale, n):
        k = scale * (self.c // 2 + n)
        return k if self.reg is None else self.reg * (scale * self.a // 2) + k


def mixed_tile(k):
    return U_V + k if k < 4 else (13, 14, 15, 19)[k - 4]


def two_blocks(nc, xT, weights, vecs, gate_up, mix_w, mix_b, dist, logm, ident, out):
    f32, f32r = mybir.dt.float32, mybir.dt.float32r
    ALU = mybir.AluOpType
    ACT = mybir.ActivationFunctionType

    ctx = ExitStack()
    with ctx:
        at = {}
        top = (nc.sbuf_base + 63) // 64 * 64

        def place(name, cols, dt=f32, offset=None, rows=P):
            nonlocal top
            shape = [rows] + (list(cols) if isinstance(cols, (list, tuple)) else [cols])
            size = 4 * int(np.prod(shape[1:]))
            if offset is None:
                offset, top = top, top + (size + 63) // 64 * 64
            at[name] = offset
            return nc.alloc_sbuf_tensor_at(name, shape, dt, offset=offset)

        XH = place("x_hi", [KT, S], f32r)
        XL = place("x_lo", [KT, S], f32r)
        WR = place("w_raw", [2, KT, P])
        WH = place("w_hi", [2, KT, P], f32r)
        WL = place("w_lo", [2, KT, P], f32r)
        VEC = place("vectors", VECS)
        IDN = place("identity", P)
        ONES = place("ones", P)
        R = place("rstd", S)
        GG = place("gain_product", KT)
        DEC = place("chunk_decay", [2, NCH])
        STAT = place("softmax_stats", [4, 4])
        WGU = place("gate_up_w", 2 * P, rows=RANK)
        XR = place("residual", [KT, S])
        WK = place("work", [20, S])
        wk, xr = at["work"], at["residual"]
        TMP = 16
        MH = place("m_hi", [8, S], f32r, wk)
        ML = place("m_lo", [8, S], f32r, wk + 8 * 4 * S)
        xo = at["x_hi"]
        VTOK = place("gla_v_tokens", [NBLK, GLA_HEADS * DV], f32, xo)
        KTOK = place("gla_k_tokens", [NBLK, GLA_HEADS * DK], f32, xo + 16384)
        ST = place("gla_states", [2, NCH, DV], f32, xo + 24576)
        SC = place("gla_scores", [2, NBLK, P], f32, xo + 40960)
        KS = place("gla_k_s", [2, S], f32, xo + 49152)
        RESET = place("gla_scan_reset", S, f32, xo + 57344)
        GSQ = place("gla_squares", S, f32, xo + 61440)
        Q2 = place("att_q", S, f32, xr)
        K2 = place("att_k", S, f32, xr + 4096)
        VT = place("att_v", S, f32, xr + 8192)
        QS = place("att_q_split", S, f32r, xr + 12288)
        KH = place("att_k_hi", S, f32r, xr + 16384)
        KL = place("att_k_lo", S, f32r, xr + 20480)
        VHL = place("att_v_split", [2, NBLK, P], f32r, xr + 24576)
        DIST = place("distances", S, f32, wk)
        LOGM = place("log_counts", S, f32, wk + 4096)
        BH = place("att_bias", S, f32, wk + 8192)
        PH = place("att_p_hi", [2, HALF], f32r, wk + 12288)
        PL = place("att_p_lo", [2, HALF], f32r, wk + 16384)
        Y = place("att_y", S, f32, wk + 20480)
        MXL = place("att_mixed", S, f32, wk + 24576)
        SBG = place("att_b_gate", S, f32, wk + 28672)
        GAB = place("att_gates", [2, S], f32, wk + 32768)
        OT = place("att_o_half", HALF, f32, wk + 40960)
        PB = place("att_p", [4, S], f32, wk + TMP * 4096)

        def psum(name, shape):
            return ctx.enter_context(nc.psum_tensor(name, shape, f32))

        PD = psum("dense", [P, 2, S])
        PA = psum("aux", [P, 4, HALF])

        def dram(name, n):
            return nc.dram_tensor(name, (n, P, S), f32, kind="Internal").ap()

        d_x, d_qkv, d_mix = dram("kept_x", KT), dram("kept_qkv", 3 * KT), dram("kept_mixed", KT)
        d_ya, d_yb = dram("kept_ya", KT), dram("kept_yb", KT)
        d_ga, d_gb = dram("kept_ga", KT), dram("kept_gb", KT)

        def sem(name):
            return ctx.enter_context(nc.semaphore(name))

        x_in = [sem(f"x_in{k}") for k in range(KT)]
        vec_in, tab_in, gat_in = sem("vec_in"), sem("tab_in"), sem("gat_in")
        consts = sem("consts")
        w_raw = [sem("w_raw0"), sem("w_raw1")]
        w_hi, w_lo, mm_done, evac = sem("w_hi"), sem("w_lo"), sem("mm_done"), sem("evac")
        xh, x_ready = sem("xh"), sem("x_ready")
        sq, acc, ss, rr, rs = sem("sq"), sem("acc"), sem("ss"), sem("rr"), sem("rs")
        xr_scaled = sem("xr_scaled")
        cv = sem("conv_step")
        s_t, m_t, mh, m_ready = sem("silu_done"), sem("m_t"), sem("mh"), sem("m_ready")
        z_mm, z_abs, z_add, ga, gd = sem("z_mm"), sem("z_abs"), sem("z_add"), sem("gla_act"), sem("gla_dve")
        g_tp, g_tc, kv_mm, st_c = sem("g_tp"), sem("g_tc"), sem("kv_mm"), sem("state_c")
        g_const, sc_mm, sc_cp, sc_sel, o_mm = sem("g_const"), sem("sc_mm"), sem("sc_cp"), sem("sc_sel"), sem("o_mm")
        o_cp, o_sq, o_ss, o_rr, o_rs = sem("o_cp"), sem("o_sq"), sem("o_ss"), sem("o_rr"), sem("o_rs")
        g_silu, g_out = sem("g_silu"), sem("g_out")
        av_t, av_g, avn, v_tp, v_tc, mix_mm, mixed = (sem(n) for n in
            ("av_t", "av_g", "avn", "v_tp", "v_tc", "mix_mm", "mixed"))
        w_sel = sem("w_sel")
        sp_x, sp_mx, sp_t = sem("sp_x"), sem("sp_mx"), [sem("sp_t0"), sem("sp_t1")]
        au_g, mx_upd = sem("au_g"), sem("mx_upd")
        q_in, k_in, v_in, mx_in = sem("q_in"), sem("k_in"), sem("v_in"), sem("mx_in")
        q_hi, k_hi, q_lo, k_lo, bias = sem("q_hi"), sem("k_hi"), sem("q_lo"), sem("k_lo"), sem("bias")
        vt_tp, v_hi, v_lo = sem("vt_tp"), sem("v_hi"), sem("v_lo")
        s_ready, ttr, ex, rl, pn = sem("s_ready"), sem("ttr"), sem("ex"), sem("rl"), sem("pn")
        t_ready, ph, pl, pv, o_half, yh = (sem(n) for n in ("t_ready", "ph", "pl", "pv", "o_half", "yh"))
        g_act, ya_up, yb_up = sem("gate_act"), sem("ya_up"), sem("yb_up")
        sp_ya = sem("sp_ya")
        ld = [sem("ld0"), sem("ld1")]
        m1 = sem("merged")
        fin, outs = sem("fin"), sem("outs")
        turns = sem("turns")

        def vec(c, n=1):
            return VEC[:, c:c + n]

        def one(t):
            return t.rearrange("p a n -> p (a n)")

        SQ_NORM2, SQ_F, SQ_V, SQ_END = 8, 16, 32, 40
        LD_YA, LD_YB, LD_GB, LD_X = 0, 8, 24, 32
        GD_PAIR = (0, 8)

        block = ctx.enter_context(nc.Block())

        @block.sync
        def _(sp):
            def load(u):
                if u.c >= 2:
                    sp.wait_ge(w_lo, u.count(-1))
                sp.dma_start(WR[:, u.slot].rearrange("p k c -> p (k c)"),
                             weights[u.count()]).then_inc(w_raw[u.slot], 16)

            def loads(c, n):
                if n >= 2:
                    with sp.Fori(0, n // 2) as i:
                        load(Unit(c, i, 2))
                        load(Unit(c + 1, i, 2))
                if n % 2:
                    load(Unit(c + n - 1))

            sp.dma_start(VEC[:], vecs).then_inc(vec_in, 16)
            for k in range(KT):
                sp.dma_start(XR[:, k], xT[k]).then_inc(x_in[k], 16)
                if k < 2:
                    load(Unit(k))
            sp.dma_start(WGU[:], gate_up).then_inc(tab_in, 16)
            sp.dma_start(IDN[:], ident).then_inc(tab_in, 16)
            loads(2, U_AV + 4 - 2)
            sp.dma_start(WK[:, 10], mix_w).then_inc(gat_in, 16)
            sp.dma_start(WK[:, 11], mix_b).then_inc(gat_in, 16)
            loads(U_AV + 4, U_ATT + 2 - U_AV - 4)

            sp.wait_ge(sp_x, 16 * KT)
            sp.wait_ge(sp_mx, 16 * KT)
            for t in range(2):
                sp.wait_ge(sp_t[t], 16 * 12)
            sp.wait_ge(mm_done, U_ATT)
            sp.dma_start(DIST[:], dist).then_inc(tab_in, 16)
            sp.dma_start(LOGM[:], logm).then_inc(tab_in, 16)

            def load_qk(j, h, first):
                if not first:
                    sp.wait_ge(q_lo, 2 * j + h)
                    sp.wait_ge(k_lo, 2 * j + h)
                for t, sm, c in ((Q2, q_in, 0), (K2, k_in, 1)):
                    src = d_qkv[3 * j + c, h * DH:(h + 1) * DH, :]
                    sp.dma_start(t[0:DH], src).then_inc(sm, 16)
                    sp.dma_start(t[DH:P], src).then_inc(sm, 16)

            def load_v(j, first):
                if not first:
                    sp.wait_ge(vt_tp, 2 * j)
                sp.dma_start(VT[:], d_qkv[3 * j + 2]).then_inc(v_in, 16)

            def load_mixed(j):
                sp.wait_ge(sp_ya, 16 * j + 16)
                sp.dma_start(MXL[:], d_mix[j + 1]).then_inc(mx_in, 16)

            load_qk(0, 0, True)
            load_v(0, True)
            sp.dma_start(MXL[:], d_mix[0]).then_inc(mx_in, 16)
            with sp.Fori(0, PAIRS - 1) as j:
                load_qk(j, 1, False)
                load(Unit(U_ATT + 2, j, 4))
                load(Unit(U_ATT + 3, j, 4))
                load_v(j + 1, False)
                load_mixed(j)
                load(Unit(U_ATT + 4, j, 4))
                load_qk(j + 1, 0, False)
                load(Unit(U_ATT + 5, j, 4))
            load_qk(PAIRS - 1, 1, False)
            for m in range(4):
                load(Unit(U_ATT + 4 * (PAIRS - 1) + 2 + m))

            n = 0

            used = []

            def fetch(src, by, count):
                nonlocal n
                if n >= 2:
                    sp.wait_ge(*used[n - 2])
                used.append((by, count))
                sp.dma_start(WK[:, TMP + n % 2], src).then_inc(ld[n % 2], 16)
                n += 1

            sp.wait_ge(sp_ya, 16 * KT)
            sp.wait_ge(mm_done, U_PA)
            sp.wait_ge(yh, 4 * PAIRS)
            for k in range(KT):
                fetch(d_ya[k], x_ready, 32 + k + 1)
            sp.wait_ge(sp_x, 16 * 2 * KT)
            for t in range(2):
                sp.wait_ge(sp_t[t], 16 * (12 + KT))
            for k in range(KT):
                fetch(d_yb[k], m_ready, 22 + k + 1)
                load(Unit(U_PA + k + 2))
                fetch(d_ga[k], evac, U_PA + k + 1)
            for k in range(KT):
                load(Unit(U_PB + k + 2))
                fetch(d_gb[k], evac, U_PB + k + 1)
            for k in range(KT):
                if U_WO + k + 2 < UNITS:
                    load(Unit(U_WO + k + 2))
                fetch(d_x[k], evac, U_WO + k + 1)
            for k in range(KT):
                sp.wait_ge(fin, k + 1)
                sp.dma_start(out[k], XR[:, k]).then_inc(outs, 16)
            sp.wait_ge(outs, 16 * KT)

        @block.gpsimd
        def _(pool):
            def split(u):
                pool.wait_ge(w_hi, u.count(1))
                pool.tensor_tensor(WL[:, u.slot], WR[:, u.slot], WH[:, u.slot].bitcast(f32),
                                   ALU.subtract).then_inc(w_lo, 1)

            def splits(c, n):
                if n >= 2:
                    with pool.Fori(0, n // 2) as i:
                        split(Unit(c, i, 2))
                        split(Unit(c + 1, i, 2))
                if n % 2:
                    split(Unit(c + n - 1))

            pool.memset(ONES[:], 1.0).then_inc(consts, 1)
            splits(0, U_OUT + 2)
            pool.wait_ge(mm_done, U_OUT)
            pool.memset(RESET[:], 1.0).then_inc(g_const, 1)
            pool.wait_ge(g_const, 1)
            pool.memset(RESET[:].rearrange("p (c t) -> p c t", t=CHUNK)[:, :, 0:1], 0.0).then_inc(g_const, 1)
            for s in range(2):
                pool.memset(SC[:, s], 0.0).then_inc(g_const, 1)
            for h in range(GLA_HEADS):
                pool.wait_ge(sc_cp, h + 1)
                pool.affine_select(out=SC[:, h % 2], in_=SC[:, h % 2], compare_op=ALU.is_ge, fill=0.0,
                                   base=0, pattern=[[0, NBLK], [1, P]], channel_multiplier=-1
                                   ).then_inc(sc_sel, 1)
            splits(U_OUT + 2, U_AV + 4 - U_OUT - 2)
            pool.wait_ge(gat_in, 32)
            w3 = WK[:, 10].rearrange("p (g t) -> p g t", t=P)
            pool.affine_select(out=w3, in_=w3, compare_op=ALU.is_ge, fill=0.0, base=0,
                               pattern=[[0, KT], [1, P]], channel_multiplier=-1).then_inc(w_sel, 1)
            splits(U_AV + 4, UNITS - U_AV - 4)

        @block.tensor
        def _(pe):
            def unit(u, H=XH, L=XL, nk=KT, ready=None, between=None):
                pe.wait_ge(w_hi, u.count(1))
                pe.wait_ge(w_lo, u.count(1))
                if u.c >= 2:
                    pe.wait_ge(evac, u.count(-1))
                for t in range(2):
                    dst = PD[:, u.slot, t * HALF:(t + 1) * HALF]
                    for k in range(nk):
                        if ready and t == 0:
                            pe.wait_ge(ready[0], ready[1] + k + 1)
                        tok = slice(t * HALF, (t + 1) * HALF)
                        pe.matmul(dst, WH[:, u.slot, k], H[:, k, tok], start=(k == 0), stop=False)
                        pe.matmul(dst, WH[:, u.slot, k], L[:, k, tok], start=False, stop=False)
                        last = pe.matmul(dst, WL[:, u.slot, k], H[:, k, tok], start=False, stop=(k == nk - 1))
                        if t == 1 and k == nk - 1:
                            last.then_inc(mm_done, 1)
                        if between:
                            between(t * nk + k)

            def units(c, n, **kw):
                if n >= 2:
                    with pe.Fori(0, n // 2) as i:
                        unit(Unit(c, i, 2), **kw)
                        unit(Unit(c + 1, i, 2), **kw)
                if n % 2:
                    unit(Unit(c + n - 1), **kw)

            def column_sums(count, src, bank=0):
                pe.wait_ge(acc, count)
                for t in range(2):
                    last = pe.matmul(PA[:, bank + t], ONES[:], src[:, t * HALF:(t + 1) * HALF],
                                     start=True, stop=True)
                last.then_inc(ss, 1)

            pe.wait_ge(consts, 1)
            unit(Unit(0), ready=(x_ready, 0))
            column_sums(8, WK[:, TMP + 2])
            unit(Unit(1))
            units(2, 23)

            pe.wait_ge(tab_in, 32)
            pe.wait_ge(evac, 25)
            for j in range(2):
                for t in range(2):
                    last = pe.matmul(PA[:, 2 * j + t], WGU[:, j * P:(j + 1) * P],
                                     WK[0:RANK, 0, t * HALF:(t + 1) * HALF], start=True, stop=True)
                last.then_inc(z_mm, 1)
            pe.wait_ge(z_add, 2)
            pe.wait_ge(z_abs, 2)
            n = 0
            for src, ready in [(WK[:, U_V + h], None) for h in range(GLA_HEADS)] + \
                              [(KS[:, j], j) for j in range(2)]:
                if ready is not None:
                    pe.wait_ge(gd, GD_PAIR[ready] + 6)
                for q in range(2):
                    if n >= 4:
                        pe.wait_ge(g_tc, n - 3)
                    for b in range(4):
                        last = pe.transpose(PA[:, n % 4, b * P:(b + 1) * P],
                                            src[:, (4 * q + b) * P:(4 * q + b + 1) * P], IDN[:])
                    last.then_inc(g_tp, 1)
                    n += 1
            pe.wait_ge(g_tc, 12)
            for j in range(2):
                if j:
                    pe.wait_ge(st_c, NCH - 1)
                for c in range(NCH):
                    half, blk, col = c % 2, c // 2, (c // 2) % 4 * DV
                    rows = slice(CHUNK * half, CHUNK * (half + 1))
                    for p in range(2):
                        h = 2 * j + p
                        last = pe.matmul(PA[p * DK:(p + 1) * DK, 2 * half + blk // 4, col:col + DV],
                                         KTOK[rows, blk, h * DK:(h + 1) * DK],
                                         VTOK[rows, blk, h * DV:(h + 1) * DV], start=True, stop=True)
                    if c % 8 == 7:
                        last.then_inc(kv_mm, 1)

            def scores(h):
                rows = slice(h % 2 * DK, (h % 2 + 1) * DK)
                if h:
                    pe.wait_ge(sc_cp, h)
                for b in range(NBLK):
                    tok = slice(b * P, (b + 1) * P)
                    last = pe.matmul(PA[:, b // 4, b % 4 * P:(b % 4 + 1) * P], WK[rows, U_K + h // 2, tok],
                                     WK[rows, U_Q + h // 2, tok], start=True, stop=True)
                last.then_inc(sc_mm, 1)

            pe.wait_ge(st_c, 2 * (NCH - 1))
            pe.wait_ge(gd, GD_PAIR[1] + 7)
            scores(0)
            for h in range(GLA_HEADS):
                if h + 1 < GLA_HEADS:
                    scores(h + 1)
                rows = slice(h % 2 * DK, (h % 2 + 1) * DK)
                pe.wait_ge(sc_sel, h + 1)
                if h:
                    pe.wait_ge(o_cp, h)
                for b in range(NBLK):
                    bank, col = 2 + b // 4, b % 4 * P
                    pe.matmul(PA[:, bank, col:col + P], VTOK[:, b, h * DV:(h + 1) * DV], SC[:, h % 2, b],
                              start=True, stop=False)
                    for c in (2 * b, 2 * b + 1):
                        last = pe.matmul(PA[:, bank, col + c % 2 * CHUNK:col + (c % 2 + 1) * CHUNK],
                                         ST[rows, h // 2, c], WK[rows, U_Q + h // 2, c * CHUNK:(c + 1) * CHUNK],
                                         start=False, stop=(c % 2 == 1))
                last.then_inc(o_mm, 1)
                pe.wait_ge(o_sq, h + 1)
                if h >= 2:
                    pe.wait_ge(o_rr, h - 1)
                for t in range(2):
                    last = pe.matmul(PD[:, h % 2, t * HALF:(t + 1) * HALF], ONES[:],
                                     GSQ[:, t * HALF:(t + 1) * HALF], start=True, stop=True)
                last.then_inc(o_ss, 1)

            unit(Unit(U_OUT), ready=(x_ready, 8))
            units(U_OUT + 1, 7)
            for n, (first, tiles, down) in enumerate(FFN):
                if n == 0:
                    unit(Unit(first), ready=(x_ready, 16))
                    column_sums(16, WK[:, TMP + 2])
                    unit(Unit(first + 1))
                    units(first + 2, 2 * tiles - 2)
                else:
                    units(first, 2 * tiles)
                unit(Unit(down), H=MH, L=ML, nk=tiles, ready=(m_ready, 8 * n))
                units(down + 1, 7, H=MH, L=ML, nk=tiles)

            unit(Unit(U_AV), ready=(x_ready, 24))
            column_sums(31, WK[:, TMP + 2])
            column_sums(32, WK[:, TMP + 3], 2)
            units(U_AV + 1, 7)
            units(U_QKV, 2)
            column_sums(SQ_V + 8, WK[:, TMP + 2])
            units(U_QKV + 2, 4)

            def gating_transposes(g):
                pe.wait_ge(avn, g + 1)
                if g:
                    pe.wait_ge(v_tc, 2 * g)
                for b in range(NBLK):
                    last = pe.transpose(PA[:, b // 4, b % 4 * P:(b % 4 + 1) * P],
                                        WK[:, g, b * P:(b + 1) * P], IDN[:])
                    if b % 4 == 3:
                        last.then_inc(v_tp, 1)

            pe.wait_ge(w_sel, 1)
            gating_transposes(0)
            for g in range(KT):
                if g + 1 < KT:
                    gating_transposes(g + 1)
                pe.wait_ge(v_tc, 2 * g + 2)
                if g:
                    pe.wait_ge(mixed, g)
                for b in range(NBLK):
                    last = pe.matmul(PA[:, 2 + b // 4, b % 4 * P:(b % 4 + 1) * P],
                                     WK[:, 8 + g % 2, b * P:(b + 1) * P], WK[:, 10, g * P:(g + 1) * P],
                                     start=True, stop=True)
                last.then_inc(mix_mm, 1)
            units(U_QKV + 6, 18)
            units(U_AU, 8)

            with pe.Fori(0, PAIRS) as j:
                for m in range(4):
                    h, sb = m // 2, m % 2
                    if m == 0:
                        pe.wait_ge(v_in, 16 * j + 16)
                        for q in range(2):
                            for b in range(4):
                                last = pe.transpose(PA[:, q, b * P:(b + 1) * P],
                                                    VT[:, (4 * q + b) * P:(4 * q + b + 1) * P], IDN[:])
                            last.then_inc(vt_tp, 1)
                    chunks = [(i, c, min(HALF, (i + 1) * P - c)) for i in range(4 * sb, 4 * sb + 4)
                              for c in range(0, (i + 1) * P, HALF)]
                    base = 12 * h + 4 * sb
                    start_at = 7 if sb == 0 else 2

                    def score_chunk(n):
                        if not 0 <= n < len(chunks):
                            return
                        i, c, w = chunks[n]
                        if n == 0 and sb == 0:
                            pe.wait_ge(q_lo, 2 * j + h + 1)
                            pe.wait_ge(k_lo, 2 * j + h + 1)
                            if m == 0:
                                pe.wait_ge(v_lo, 2 * j + 2)
                        if n >= 3:
                            pe.wait_ge(ttr, 24 * j + base + n - 2)
                        dst = PA[:, n % 3, 0:w]
                        pe.matmul(dst, QS[:, i * P:(i + 1) * P], KH[:, c:c + w], start=True, stop=False)
                        pe.matmul(dst, QS[:, i * P:(i + 1) * P], KL[:, c:c + w], start=False, stop=True
                                  ).then_inc(s_ready, 1)

                    unit(Unit(U_ATT + m, j, 4), between=lambda g: score_chunk(g - start_at))

                    nj = 4 * sb + 4

                    def turn_p(k):
                        if k == 0:
                            pe.wait_ge(pn, 16 * j + 4 * m + 4)
                        for b in range(max(0, k - 4 * sb), 4):
                            last = pe.transpose(PA[:, k % 3, b * P:(b + 1) * P], PB[:, b, k * P:(k + 1) * P],
                                                IDN[:])
                        last.then_inc(t_ready, 1)

                    turn_p(0)
                    turn_p(1)
                    for k in range(nj):
                        if k + 2 < nj:
                            turn_p(k + 2)
                        pe.wait_ge(pl, 24 * j + base + k + 1)
                        if k == 0 and m:
                            pe.wait_ge(yh, 4 * j + m)
                        lo = max(0, k - 4 * sb) * P
                        dst = PA[:, 3, lo:HALF]
                        pe.matmul(dst, VHL[:, h, k], PH[:, k % 2, lo:HALF], start=(k == 0), stop=False)
                        pe.matmul(dst, VHL[:, h, k], PL[:, k % 2, lo:HALF], start=False, stop=(k == nj - 1)
                                  ).then_inc(pv, 1)

            unit(Unit(U_PA), ready=(x_ready, 32))
            units(U_PA + 1, 7)
            unit(Unit(U_PB), H=MH, L=ML, ready=(m_ready, 22))
            units(U_PB + 1, 7, H=MH, L=ML)
            unit(Unit(U_WO), ready=(x_ready, 40))
            units(U_WO + 1, 7)
            column_sums(SQ_END + 8, WK[:, 0])

        @block.scalar
        def _(act):
            def split(u):
                if u.reg is None and u.c >= UNITS:
                    return
                act.wait_ge(w_raw[u.slot], u.turn(16, 1))
                if u.c >= 2:
                    act.wait_ge(mm_done, u.count(-1))
                act.copy(WH[:, u.slot], WR[:, u.slot]).then_inc(w_hi, 1)

            def splits(c, n):
                if n >= 2:
                    with act.Fori(0, n // 2) as i:
                        split(Unit(c, i, 2))
                        split(Unit(c + 1, i, 2))
                if n % 2:
                    split(Unit(c + n - 1))

            def square(src, n, scale=1.0):
                if n >= 2:
                    act.wait_ge(acc, n - 1)
                act.activation(WK[:, TMP + n % 2], src, ACT.Square, scale=scale).then_inc(sq, 1)

            def root(n, src, dst=R[:]):
                act.wait_ge(rr, n)
                act.activation(dst, src, ACT.Sqrt).then_inc(rs, 1)

            act.wait_ge(vec_in, 16)
            for k in range(KT):
                act.wait_ge(x_in[k], 16)
                act.activation(XH[:, k], XR[:, k], ACT.Copy, scale=vec(V_G1 + k)).then_inc(xh, 1)
                if k < 2:
                    split(Unit(k))
                square(XR[:, k], k)
            root(1, WK[:, TMP + 3])
            splits(2, 25)
            n = 0

            def step(ins):
                nonlocal n
                n += 1
                ins.then_inc(ga, 1)

            act.wait_ge(z_mm, 2)
            act.activation(WK[:, TMP + 1], one(PA[:, 0:2]), ACT.Abs, bias=vec(V_BG)).then_inc(z_abs, 1)
            for j in range(2):
                Z, E, B = WK[:, TMP], WK[:, TMP + 1], WK[:, TMP + 2]
                if j:
                    act.wait_ge(gd, GD_PAIR[0] + 6)
                    act.activation(E, GSQ[:], ACT.Copy).then_inc(ga, 1)
                    n += 1
                    act.wait_ge(ga, n)
                else:
                    act.activation(GSQ[:], one(PA[:, 2:4]), ACT.Abs, bias=vec(V_BG + 1)).then_inc(z_abs, 1)
                    act.wait_ge(z_abs, 2)
                step(act.activation(E, E, ACT.Exp, scale=-1.0))
                act.wait_ge(ga, n)
                step(act.activation(E, E, ACT.Ln, bias=1.0))
                act.wait_ge(gd, GD_PAIR[j] + 2)
                step(act.activation(E, B, ACT.Exp, scale=1.0 / 16))
                act.wait_ge(ga, n)
                step(act.activation(Z, B, ACT.Exp, scale=-1.0 / 16))
                act.wait_ge(gd, GD_PAIR[j] + 5)
                step(act.activation(E, E, ACT.Exp, scale=1.0 / 16))
            for i in range(12):
                act.wait_ge(g_tp, i + 1)
                q = i % 2
                if i < 8:
                    dst = VTOK[:, 4 * q:4 * q + 4, i // 2 * P:(i // 2 + 1) * P]
                else:
                    dst = KTOK[:, 4 * q:4 * q + 4, (i - 8) // 2 * P:((i - 8) // 2 + 1) * P]
                act.copy(dst, PA[:, i % 4].rearrange("p (b f) -> p b f", f=P)).then_inc(g_tc, 1)
            for h in range(GLA_HEADS):
                act.activation(WK[:, U_G + h], WK[:, U_G + h], ACT.Silu).then_inc(g_silu, 1)
            for h in range(GLA_HEADS):
                act.wait_ge(o_mm, h + 1)
                if h:
                    act.wait_ge(o_ss, h)
                act.copy(WK[:, U_V + h], one(PA[:, 2:4])).then_inc(o_cp, 1)
                act.wait_ge(o_cp, h + 1)
                act.activation(GSQ[:], WK[:, U_V + h], ACT.Square).then_inc(o_sq, 1)
                act.wait_ge(o_rr, h + 1)
                act.activation(WK[:, TMP], WK[:, TMP], ACT.Sqrt).then_inc(o_rs, 1)

            def hi_part(k, src, scale=None):
                if scale is None:
                    act.copy(XH[:, k], src).then_inc(xh, 1)
                else:
                    act.activation(XH[:, k], src, ACT.Copy, scale=scale).then_inc(xh, 1)

            act.wait_ge(o_ss, GLA_HEADS)
            for k in range(KT):
                if k < 4:
                    act.wait_ge(g_out, k + 1)
                hi_part(k, WK[:, mixed_tile(k)])
            for k in range(KT):
                split(Unit(U_OUT + k + 2))
                act.wait_ge(evac, U_OUT + k + 1)
                square(XR[:, k], SQ_NORM2 + k)
            for k in range(KT):
                hi_part(k, XR[:, k], vec(V_G2 + k))
            root(2, WK[:, TMP + 3])

            act.preload_act_table(ACT.Silu)
            for n, (first, tiles, down) in enumerate(FFN):
                with act.Fori(0, tiles) as i:
                    u = Unit(first, i, 2)
                    split(u.plus(2))
                    act.wait_ge(evac, u.count(1))
                    act.activation(WK[:, TMP + 1], WK[:, TMP], ACT.Silu).then_inc(s_t, 1)
                    split(u.plus(3))
                    act.wait_ge(m_t, i + (8 * n + 1))
                    act.copy(MH[:, i], WK[:, TMP + 3]).then_inc(mh, 1)
                if n < 2:
                    splits(down + 2, 8)
                else:
                    for k in range(8):
                        split(Unit(down + 2 + k))
                        act.wait_ge(evac, down + k + 1)
                        square(XR[:, k], SQ_F + 2 * k)
                        square(XR[:, k], SQ_F + 2 * k + 1, vec(V_GF + k))

            act.wait_ge(gd, GD_PAIR[1] + 8)
            for k in range(KT):
                hi_part(k, XR[:, k], GG[:, k:k + 1])
            act.wait_ge(rr, 4)
            act.activation(R[:], WK[:, 8], ACT.Sqrt).then_inc(rs, 1)
            act.activation(WK[:, 9], WK[:, TMP + 3], ACT.Sqrt).then_inc(rs, 1)
            for k in range(KT):
                split(Unit(U_AV + k + 2))
                act.wait_ge(evac, U_AV + k + 1)
                act.activation(WK[:, k], WK[:, 12 + k % 2], ACT.Gelu_apprx_tanh).then_inc(av_g, 1)
                act.wait_ge(av_g, k + 1)
                square(WK[:, k], SQ_V + k)
                act.wait_ge(xr_scaled, k + 1)
                act.dma_start(d_x[k], XR[:, k]).then_inc(sp_x, 16)

            def keep(u, t):
                act.wait_ge(evac, u.count(1))
                act.dma_start(d_qkv[u.count(-U_QKV)], WK[:, 12 + t]).then_inc(sp_t[t], 16)

            def keeps(c, n):
                with act.Fori(0, n // 2) as i:
                    for s in range(2):
                        u = Unit(c + s, i, 2)
                        split(u.plus(2))
                        keep(u, s)

            keeps(U_QKV, 2)
            root(5, WK[:, TMP + 3], WK[:, TMP + 3])
            keeps(U_QKV + 2, 4)
            for g in range(KT):
                if g >= 2:
                    act.wait_ge(mix_mm, g - 1)
                for q in range(2):
                    act.wait_ge(v_tp, 2 * g + q + 1)
                    act.copy(WK[:, 8 + g % 2, q * HALF:(q + 1) * HALF], PA[:, q]).then_inc(v_tc, 1)
            keeps(U_QKV + 6, 18)
            act.preload_act_table(ACT.Gelu_apprx_tanh)
            for k in range(KT):
                u = Unit(U_AU + k)
                split(u.plus(2))
                act.wait_ge(evac, u.count(1))
                act.activation(WK[:, 14 + k % 2], WK[:, 12 + k % 2], ACT.Gelu_apprx_tanh).then_inc(au_g, 1)
                act.wait_ge(mx_upd, k + 1)
                act.dma_start(d_mix[k], WK[:, k]).then_inc(sp_mx, 16)

            with act.Fori(0, PAIRS) as j:
                for m in range(4):
                    h, sb = m // 2, m % 2
                    base = 12 * h + 4 * sb
                    u = Unit(U_ATT + m, j, 4)
                    if sb == 0:
                        act.wait_ge(q_in, 64 * j + 32 * h + 32)
                        act.activation(QS[:], Q2[:], ACT.Copy, scale=DH ** -0.5).then_inc(q_hi, 1)
                        act.wait_ge(k_in, 64 * j + 32 * h + 32)
                        act.copy(KH[:], K2[:]).then_inc(k_hi, 1)
                        if m == 0:
                            for q in range(2):
                                act.wait_ge(vt_tp, 2 * j + q + 1)
                                act.copy(VHL[:, :, 4 * q:4 * q + 4, 0:DH].rearrange("p h b d -> p b h d"),
                                         PA[:, q].rearrange("p (b h d) -> p b h d", h=2, d=DH)
                                         ).then_inc(v_hi, 1)
                    for b in range(4):
                        w = (4 * sb + b + 1) * P
                        act.wait_ge(ttr, 24 * j + base + (b + 1) * (sb + 1))
                        act.activation(PB[:, b, 0:w], PB[:, b, 0:w], ACT.Exp, scale=-1.0,
                                       bias=STAT[:, 1, b:b + 1], accum_out=STAT[:, 2, b:b + 1]).then_inc(ex, 1)
                    for k in range(4 * sb + 4):
                        lo = max(0, k - 4 * sb) * P
                        act.wait_ge(t_ready, 24 * j + base + k + 1)
                        if k >= 2:
                            act.wait_ge(pv, 24 * j + base + k - 1)
                        act.copy(PH[:, k % 2, lo:HALF], PA[:, k % 3, lo:HALF]).then_inc(ph, 1)
                    act.wait_ge(pv, 24 * j + base + 4 * sb + 4)
                    act.copy(OT[0:DH], PA[DH:P, 3]).then_inc(o_half, 1)
                    split(u.plus(2))
                    act.wait_ge(evac, u.count(1))
                    if m == 0:
                        act.activation(WK[:, 14], WK[:, 12 + u.slot], ACT.Silu).then_inc(g_act, 1)
                        act.wait_ge(ya_up, j + 1)
                        act.dma_start(d_ya[j], MXL[:]).then_inc(sp_ya, 16)
                    elif m == 1:
                        act.activation(SBG[:], WK[:, 12 + u.slot], ACT.Silu).then_inc(g_act, 1)
                    else:
                        t = m - 2
                        act.wait_ge(sp_t[t], 16 * j + 16 * 12)
                        act.activation(GAB[:, t], WK[:, 12 + u.slot], ACT.Sigmoid).then_inc(g_act, 1)
                        act.wait_ge(g_act, 4 * j + m + 1)
                        act.dma_start((d_ga, d_gb)[t][j], GAB[:, t]).then_inc(sp_t[t], 16)
                act.wait_ge(yb_up, j + 1)
                act.dma_start(d_yb[j], Y[:]).then_inc(sp_x, 16)

            def loaded(n):
                act.wait_ge(ld[n % 2], 16 * (n // 2 + 1))

            act.wait_ge(mm_done, U_PA)
            for k in range(KT):
                loaded(LD_YA + k)
                hi_part(k, WK[:, TMP + k % 2])
            for k in range(KT):
                n = LD_YB + 2 * k
                loaded(n)
                if k == 0:
                    for t in range(2):
                        act.wait_ge(sp_t[t], 16 * (12 + KT))
                    act.wait_ge(sp_x, 16 * 2 * KT)
                act.copy(MH[:, k], WK[:, TMP + n % 2]).then_inc(mh, 1)
                split(Unit(U_PA + k + 2))
            for k in range(KT):
                split(Unit(U_PB + k + 2))
                act.wait_ge(m1, k + 1)
                hi_part(k, XR[:, k])
            for k in range(KT):
                split(Unit(U_WO + k + 2))
                act.wait_ge(evac, U_WO + k + 1)
                n = SQ_END + k
                if k >= 2:
                    act.wait_ge(acc, n - 1)
                act.activation(WK[:, 2 + n % 2], XR[:, k], ACT.Square).then_inc(sq, 1)
            root(6, WK[:, 1])

        @block.vector
        def _(dve):
            def lo_part(k, src, n, scale=None, H=XH, L=XL, made=xh, ready=x_ready):
                dve.wait_ge(made, n)
                if scale is None:
                    dve.tensor_tensor(L[:, k], src, H[:, k].bitcast(f32), ALU.subtract).then_inc(ready, 1)
                else:
                    dve.scalar_tensor_tensor(L[:, k], src, scale, H[:, k].bitcast(f32),
                                             ALU.mult, ALU.subtract).then_inc(ready, 1)

            def add_square(n, first, dst, src=None):
                src = WK[:, TMP + n % 2] if src is None else src
                dve.wait_ge(sq, n + 1)
                if first:
                    dve.tensor_copy(dst, src).then_inc(acc, 1)
                else:
                    dve.wait_ge(acc, n)
                    dve.tensor_tensor(dst, dst, src, ALU.add).then_inc(acc, 1)

            def mean_recip(n_ss, n_rr, dst, width, bank=0):
                dve.wait_ge(ss, n_ss)
                dve.tensor_scalar(dst, one(PA[:, bank:bank + 2]), 1.0 / width, EPS, ALU.mult, ALU.add
                                  ).then_inc(cv, 1)
                nonlocal_cv[0] += 1
                dve.wait_ge(cv, nonlocal_cv[0])
                dve.reciprocal(dst, dst).then_inc(rr, 1)

            nonlocal_cv = [0]

            def chain(ins):
                nonlocal_cv[0] += 1
                ins.then_inc(cv, 1)
                dve.wait_ge(cv, nonlocal_cv[0])

            def scaled(u, dst):
                dve.wait_ge(mm_done, u.count(1))
                return dve.tensor_tensor(dst, PD[:, u.slot], R[:], ALU.mult).then_inc(evac, 1)

            dve.wait_ge(vec_in, 16)
            for k in range(KT):
                lo_part(k, XR[:, k], k + 1, vec(V_G1 + k))
                add_square(k, k == 0, WK[:, TMP + 2])
            mean_recip(1, 1, WK[:, TMP + 3], D)
            dve.wait_ge(rs, 1)
            for u in range(U_CONV):
                scaled(Unit(u), WK[:, u])
            for c in range(4):
                U = U_CONV + 3 * c
                T, A, O = WK[:, TMP], WK[:, TMP + 1], WK[:, mixed_tile(4 + c)]
                scaled(Unit(U), T)
                dve.wait_ge(evac, U + 1)
                dve.wait_ge(mm_done, U + 2)
                dve.tensor_tensor(T, PD[:, (U + 1) % 2], T, ALU.mult).then_inc(evac, 1)
                dve.wait_ge(evac, U + 2)
                chain(dve.tensor_tensor(A, T, R[:], ALU.mult))
                w = [vec(V_CW + 3 * c + t) for t in range(3)]
                chain(dve.tensor_scalar(O, A, w[2], None, ALU.mult))
                chain(dve.scalar_tensor_tensor(O[:, 1:S], A[:, 0:S - 1], w[1], O[:, 1:S], ALU.mult, ALU.add))
                chain(dve.scalar_tensor_tensor(O[:, 2:S], A[:, 0:S - 2], w[0], O[:, 2:S], ALU.mult, ALU.add))
                scaled(Unit(U + 2), T)
                dve.wait_ge(evac, U + 3)
                chain(dve.tensor_tensor(O, T, O, ALU.mult))

            n = 0

            def step(ins):
                nonlocal n
                n += 1
                ins.then_inc(gd, 1)

            dve.wait_ge(g_const, 4)
            dve.wait_ge(z_abs, 2)
            Z, E, B = WK[:, TMP], WK[:, TMP + 1], WK[:, TMP + 2]
            dve.tensor_scalar(Z, one(PA[:, 0:2]), vec(V_BG), None, ALU.add).then_inc(z_add, 1)
            dve.tensor_scalar(KS[:, 1], one(PA[:, 2:4]), vec(V_BG + 1), None, ALU.add).then_inc(z_add, 1)
            for j in range(2):
                q, k = WK[:, U_Q + j], WK[:, U_K + j]
                ga0 = 5 * j + j
                dve.wait_ge(z_add, 2)
                assert n == (0, 7)[j]
                if j:
                    dve.wait_ge(gd, n)
                    step(dve.tensor_copy(Z, KS[:, 1]))
                    dve.wait_ge(gd, n)
                dve.wait_ge(ga, ga0 + 2)
                step(dve.scalar_tensor_tensor(Z, Z, 0.0, E, ALU.min, ALU.subtract))
                dve.wait_ge(gd, n)
                step(dve.tensor_tensor_scan(B, RESET[:], Z, 0.0, ALU.mult, ALU.add))
                dve.wait_ge(ga, ga0 + 3)
                step(dve.scalar_tensor_tensor(q, q, DK ** -0.5, E, ALU.mult, ALU.mult))
                step(dve.tensor_copy(DEC[:, j], E.rearrange("p (c t) -> p c t", t=CHUNK)[:, :, CHUNK - 1]))
                dve.wait_ge(gd, n)
                b3 = B.rearrange("p (c t) -> p c t", t=CHUNK)
                step(dve.tensor_tensor(E.rearrange("p (c t) -> p c t", t=CHUNK),
                                       b3[:, :, CHUNK - 1:CHUNK].to_broadcast([P, NCH, CHUNK]), b3,
                                       ALU.subtract))
                dve.wait_ge(ga, ga0 + 5)
                step(dve.tensor_tensor(KS[:, j], k, E, ALU.mult))
                dve.wait_ge(gd, n)
                step(dve.tensor_tensor(k, k, Z, ALU.mult))
            assert n == GD_PAIR[1] + 7
            for j in range(2):
                chain(dve.memset(ST[:, j, 0], 0.0))
                for c in range(NCH - 1):
                    if c % 8 == 0:
                        dve.wait_ge(kv_mm, 2 * j + c // 8 + 1)
                    if c:
                        dve.wait_ge(st_c, (NCH - 1) * j + c)
                    half, blk = c % 2, c // 2
                    dve.scalar_tensor_tensor(ST[:, j, c + 1], ST[:, j, c], DEC[:, j, c:c + 1],
                                             PA[:, 2 * half + blk // 4, blk % 4 * DV:(blk % 4 + 1) * DV],
                                             ALU.mult, ALU.add).then_inc(st_c, 1)
            for h in range(GLA_HEADS + 1):
                if h < GLA_HEADS:
                    dve.wait_ge(sc_mm, h + 1)
                    if h >= 2:
                        dve.wait_ge(o_mm, h - 1)
                    ps = PA[:, 0:2].rearrange("p a (b t) -> p (a b) t", t=P)
                    for half in range(2):
                        rows = slice(half * CHUNK, (half + 1) * CHUNK)
                        last = dve.tensor_copy(SC[rows, h % 2, :, rows], ps[rows, :, rows])
                    last.then_inc(sc_cp, 1)
                if h:
                    g = h - 1
                    T, O = WK[:, TMP], WK[:, U_V + g]
                    dve.wait_ge(o_ss, g + 1)
                    if g:
                        dve.wait_ge(g_out, g)
                    chain(dve.tensor_scalar(T, PD[:, g % 2], 1.0 / DV, EPS, ALU.mult, ALU.add))
                    dve.reciprocal(T, T).then_inc(o_rr, 1)
                    dve.wait_ge(g_silu, GLA_HEADS)
                    chain(dve.tensor_tensor(O, O, WK[:, U_G + g], ALU.mult))
                    dve.wait_ge(o_rs, g + 1)
                    dve.scalar_tensor_tensor(O, O, vec(V_GN), T, ALU.mult, ALU.mult).then_inc(g_out, 1)

            for k in range(KT):
                lo_part(k, WK[:, mixed_tile(k)], 8 + k + 1)

            def add_to_residual(u, k):
                dve.wait_ge(mm_done, u.count(1))
                dve.tensor_tensor(XR[:, k], PD[:, u.slot], XR[:, k], ALU.add).then_inc(evac, 1)

            for k in range(KT):
                add_to_residual(Unit(U_OUT + k), k)
                add_square(SQ_NORM2 + k, k == 0, WK[:, TMP + 2])
            for k in range(KT):
                lo_part(k, XR[:, k], 16 + k + 1, vec(V_G2 + k))
            mean_recip(2, 2, WK[:, TMP + 3], D)
            dve.wait_ge(rs, 2)

            for n, (first, tiles, down) in enumerate(FFN):
                with dve.Fori(0, tiles) as i:
                    u = Unit(first, i, 2)
                    scaled(u, WK[:, TMP])
                    scaled(u.plus(1), WK[:, TMP + 2])
                    dve.wait_ge(evac, u.count(2))
                    dve.wait_ge(s_t, i + (8 * n + 1))
                    dve.tensor_tensor(WK[:, TMP + 3], WK[:, TMP + 1], WK[:, TMP + 2], ALU.mult).then_inc(m_t, 1)
                    dve.wait_ge(mh, i + (8 * n + 1))
                    dve.tensor_tensor(ML[:, i], WK[:, TMP + 3], MH[:, i].bitcast(f32), ALU.subtract
                                      ).then_inc(m_ready, 1)
                for k in range(KT):
                    add_to_residual(Unit(down + k), k)
                    if n == 2:
                        for t in range(2):
                            m = SQ_F + 2 * k + t
                            dve.wait_ge(sq, m + 1)
                            dst = WK[:, TMP + 2 + t]
                            if k == 0:
                                dve.tensor_copy(dst, WK[:, TMP + t]).then_inc(acc, 1)
                            else:
                                dve.wait_ge(acc, m - 1)
                                dve.tensor_tensor(dst, dst, WK[:, TMP + t], ALU.add).then_inc(acc, 1)

            dve.tensor_tensor(GG[:], vec(V_GF, KT), vec(V_H2, KT), ALU.mult).then_inc(gd, 1)
            dve.wait_ge(gd, GD_PAIR[1] + 8)
            for k in range(KT):
                lo_part(k, XR[:, k], 24 + k + 1, GG[:, k:k + 1])
            U_, V_ = WK[:, TMP + 3], WK[:, 8]
            dve.wait_ge(ss, 4)
            mean_recip(3, 3, U_, D)
            dve.wait_ge(rr, 3)
            chain(dve.scalar_tensor_tensor(V_, one(PA[:, 2:4]), 1.0 / D, U_, ALU.mult, ALU.mult))
            chain(dve.tensor_scalar(V_, V_, EPS, None, ALU.add))
            chain(dve.reciprocal(V_, V_))
            dve.tensor_tensor(V_, V_, U_, ALU.mult).then_inc(rr, 1)
            dve.wait_ge(rs, 4)
            for k in range(KT):
                if k >= 2:
                    dve.wait_ge(av_g, k - 1)
                scaled(Unit(U_AV + k), WK[:, 12 + k % 2])
                add_square(SQ_V + k, k == 0, WK[:, TMP + 2])
                dve.scalar_tensor_tensor(XR[:, k], XR[:, k], vec(V_GF + k), WK[:, 9], ALU.mult, ALU.mult
                                         ).then_inc(xr_scaled, 1)

            def keep(u, first=False):
                if not first:
                    dve.wait_ge(sp_t[u.slot ^ 1], (u.plus(-U_QKV)).turn(16, 0))
                scaled(u, WK[:, 12 + (u.slot ^ 1)])

            for s in range(2):
                dve.wait_ge(av_g, KT)
                keep(Unit(U_QKV + s), True)
            RV = WK[:, TMP + 3]
            mean_recip(5, 5, RV, D)
            for k in range(4):
                keep(Unit(U_QKV + 2 + k))
            dve.wait_ge(rs, 5)
            for g in range(KT):
                dve.scalar_tensor_tensor(WK[:, g], WK[:, g], vec(V_GV + g), RV, ALU.mult, ALU.mult
                                         ).then_inc(avn, 1)
            for g in range(KT):
                dve.wait_ge(mix_mm, g + 1)
                dve.tensor_tensor(WK[:, g].rearrange("p (b t) -> p b t", t=P),
                                  PA[:, 2:4].rearrange("p a (b t) -> p (a b) t", t=P),
                                  WK[:, 11, g * P:(g + 1) * P].unsqueeze(1).to_broadcast([P, NBLK, P]),
                                  ALU.add).then_inc(mixed, 1)
            with dve.Fori(0, 9) as i:
                for s in range(2):
                    keep(Unit(U_QKV + 6 + s, i, 2))
            for s in range(2):
                dve.wait_ge(sp_t[s], 16 * 12)
            for k in range(KT):
                if k >= 2:
                    dve.wait_ge(au_g, k - 1)
                scaled(Unit(U_AU + k), WK[:, 12 + k % 2])
                dve.wait_ge(au_g, k + 1)
                dve.wait_ge(mixed, KT)
                dve.tensor_tensor(WK[:, k], WK[:, k], WK[:, 14 + k % 2], ALU.mult).then_inc(mx_upd, 1)

            dve.wait_ge(tab_in, 64)
            with dve.Fori(0, PAIRS) as j:
                for m in range(4):
                    h, sb = m // 2, m % 2
                    base = 12 * h + 4 * sb
                    u = Unit(U_ATT + m, j, 4)
                    if sb == 0:
                        dve.scalar_tensor_tensor(BH[:], DIST[:], VEC[:, bass.ds(j * 2 + (V_SL + h), 1)],
                                                 LOGM[:], ALU.mult, ALU.add).then_inc(bias, 1)
                        dve.wait_ge(q_hi, 2 * j + h + 1)
                        dve.scalar_tensor_tensor(QS[DH:P], Q2[DH:P], DH ** -0.5, QS[DH:P].bitcast(f32),
                                                 ALU.mult, ALU.subtract).then_inc(q_lo, 1)
                        dve.wait_ge(k_hi, 2 * j + h + 1)
                        dve.tensor_tensor(KL[:], K2[:], KH[:].bitcast(f32), ALU.subtract).then_inc(k_lo, 1)
                        if m == 0:
                            for q in range(2):
                                dve.wait_ge(v_hi, 2 * j + q + 1)
                                blk = VHL[:, :, 4 * q:4 * q + 4].rearrange("p h b d -> p b h d")
                                dve.tensor_tensor(blk[:, :, :, DH:P],
                                                  PA[:, q].rearrange("p (b h d) -> p b h d", h=2, d=DH),
                                                  blk[:, :, :, 0:DH].bitcast(f32), ALU.subtract
                                                  ).then_inc(v_lo, 1)
                        dve.wait_ge(bias, 2 * j + h + 1)
                        dve.sem_inc(turns, 1)

                    def biased(b):
                        i = 4 * sb + b
                        for c in range(sb + 1):
                            c0 = c * HALF
                            w = min(HALF, (i + 1) * P - c0)
                            n = b * (sb + 1) + c
                            if c:
                                dve.wait_ge(ttr, 24 * j + base + n)
                            dve.wait_ge(s_ready, 24 * j + base + n + 1)
                            dve.sem_inc(turns, 1)
                            u0 = S - P - i * P + c0
                            dve.tensor_tensor_reduce(
                                out=PB[:, b, c0:c0 + w], in0=PA[:, n % 3, 0:w], in1=BH[:, u0:u0 + w],
                                scale=-1.0, scalar=(STAT[:, 0, b:b + 1] if c else 3.0e38),
                                op0=ALU.add, op1=ALU.min,
                                accum_out=STAT[:, (1 if c == sb else 0), b:b + 1]).then_inc(ttr, 1)

                    def normed(b):
                        w = (4 * sb + b + 1) * P
                        n = 16 * j + 4 * m + b + 1
                        dve.wait_ge(ex, n)
                        dve.reciprocal(STAT[:, 3, b:b + 1], STAT[:, 2, b:b + 1]).then_inc(rl, 1)
                        dve.wait_ge(rl, n)
                        dve.tensor_scalar(PB[:, b, 0:w], PB[:, b, 0:w], STAT[:, 3, b:b + 1], None, ALU.mult
                                          ).then_inc(pn, 1)

                    for b in range(4):
                        biased(b)
                        if b:
                            normed(b - 1)
                    normed(3)
                    for k in range(4 * sb + 4):
                        lo = max(0, k - 4 * sb) * P
                        dve.wait_ge(ph, 24 * j + base + k + 1)
                        dve.tensor_tensor(PL[:, k % 2, lo:HALF], PA[:, k % 3, lo:HALF],
                                          PH[:, k % 2, lo:HALF].bitcast(f32), ALU.subtract).then_inc(pl, 1)
                    dve.wait_ge(o_half, 4 * j + m + 1)
                    if m == 0:
                        dve.wait_ge(sp_x, 16 * j + 16 * KT)
                    dve.tensor_tensor(Y[h * DH:(h + 1) * DH, sb * HALF:(sb + 1) * HALF], PA[0:DH, 3],
                                      OT[0:DH], ALU.add).then_inc(yh, 1)
                    if m >= 2:
                        dve.wait_ge(g_act, 4 * j + m - 1)
                    scaled(u, WK[:, 12 + u.slot])
                    if m == 0:
                        dve.wait_ge(g_act, 4 * j + 1)
                        dve.wait_ge(mx_in, 16 * j + 16)
                        dve.tensor_tensor(MXL[:], MXL[:], WK[:, 14], ALU.mult).then_inc(ya_up, 1)
                dve.wait_ge(yh, 4 * j + 4)
                dve.wait_ge(g_act, 4 * j + 4)
                dve.tensor_tensor(Y[:], Y[:], SBG[:], ALU.mult).then_inc(yb_up, 1)

            for k in range(KT):
                lo_part(k, WK[:, TMP + k % 2], 32 + k + 1)

            def loaded(n):
                dve.wait_ge(ld[n % 2], 16 * (n // 2 + 1))
                return WK[:, TMP + n % 2]

            for k in range(KT):
                n = LD_YB + 2 * k
                lo_part(k, WK[:, TMP + n % 2], 22 + k + 1, H=MH, L=ML, made=mh, ready=m_ready)
                u = Unit(U_PA + k)
                dve.wait_ge(mm_done, u.c + 1)
                src = loaded(n + 1)
                dve.tensor_tensor(XR[:, k], PD[:, u.slot], src, ALU.mult).then_inc(evac, 1)
            for k in range(KT):
                u = Unit(U_PB + k)
                src = loaded(LD_GB + k)
                dve.wait_ge(mm_done, u.c + 1)
                T = WK[:, TMP + 2]
                dve.tensor_tensor(T, PD[:, u.slot], src, ALU.mult).then_inc(evac, 1)
                dve.wait_ge(evac, u.c + 1)
                dve.tensor_tensor(XR[:, k], XR[:, k], T, ALU.add).then_inc(m1, 1)
                dve.wait_ge(m1, k + 1)
                lo_part(k, XR[:, k], 40 + k + 1)
            for k in range(KT):
                u = Unit(U_WO + k)
                src = loaded(LD_X + k)
                dve.wait_ge(mm_done, u.c + 1)
                dve.tensor_tensor(XR[:, k], PD[:, u.slot], src, ALU.add).then_inc(evac, 1)
                n = SQ_END + k
                add_square(n, k == 0, WK[:, 0], WK[:, 2 + n % 2])
            mean_recip(6, 6, WK[:, 1], D)
            dve.wait_ge(rs, 6)
            for k in range(KT):
                dve.scalar_tensor_tensor(XR[:, k], XR[:, k], vec(V_FIN + k), R[:], ALU.mult, ALU.mult
                                         ).then_inc(fin, 1)


def kernel(**inputs):
    import concourse.bacc as bacc
    from concourse.bass_utils import run_bass_kernel_spmd

    f = {k: np.asarray(v) for k, v in inputs.items()}

    def columns(w):
        k, n = w.shape
        t = w.reshape(k // P, P, n // P, P).transpose(2, 1, 0, 3)
        if k < D:
            t = np.concatenate([t, np.zeros((n // P, P, (D - k) // P, P), w.dtype)], axis=2)
        return t.reshape(n // P, P, KT * P)

    w_in, w2 = f["w_in"][0], f["w_in_2"][0]
    edges = np.cumsum([0, 256, 256, 512, 512, RANK, 512, 512, 512])
    q, k, v, g, a, cb, cc, ch = (w_in[:, edges[i]:edges[i + 1]] for i in range(8))
    a = np.concatenate([a, np.zeros((D, P - RANK), a.dtype)], axis=1)
    conv = np.stack([columns(cc), columns(ch), columns(cb)], axis=1).reshape(12, P, D)
    parts = [columns(a), columns(q), columns(k), columns(v), columns(g), conv, columns(f["w_out"][0])]
    gate, up, down = columns(f["w_ffn_gate"][0]), columns(f["w_ffn_up"][0]), f["w_ffn_down"][0]
    tile = 0
    for _, tiles, _ in FFN:
        parts.append(np.stack([gate[tile:tile + tiles], up[tile:tile + tiles]], axis=1).reshape(2 * tiles, P, D))
        parts.append(columns(down[tile * P:(tile + tiles) * P]))
        tile += tiles
    au, av, agate, q, k, v, bgate, ga, gb = (columns(w2[:, i * D:(i + 1) * D]) for i in range(9))
    parts += [av, np.stack([q, k, v], axis=1).reshape(24, P, D), au,
              np.stack([agate, bgate, ga, gb], axis=1).reshape(32, P, D),
              columns(f["w_proj_a_2"][0]), columns(f["w_proj_b_2"][0]), columns(f["w_out_2"][0])]
    weights = np.concatenate(parts)
    assert weights.shape[0] == UNITS

    def tall(x):
        return x.reshape(-1, P).T

    slopes = -np.exp2(-8.0 * np.arange(1, HEADS + 1) / HEADS).astype(np.float32)
    cw = f["conv_w"][0].reshape(3, 4, P).transpose(2, 1, 0).reshape(P, 12)
    vecs = np.concatenate([tall(f["norm1_g"]), tall(f["b_gate"]), tall(f["gla_norm_g"]), cw, tall(f["norm2_g"]),
                           tall(f["norm_f_g"]), tall(f["g_norm_2"]), tall(f["g_v_2"]), tall(f["g_final_2"]),
                           np.broadcast_to(slopes, (P, HEADS))], axis=1)
    d = np.arange(P)[:, None] + (S - P) - np.arange(S)[None, :]
    count = sum(((d % r == 0) & (d <= w)).astype(np.float64) for w, r in ((128, 1), (512, 4), (2048, 16)))
    count = count * (d >= 0)
    logm = np.where(count > 0, np.log(np.maximum(count, 1)), -1e30).astype(np.float32)
    dist = np.where(count > 0, d, 0).astype(np.float32)

    arrays = {
        "xT": f["x"][0].T.reshape(KT, P, S), "weights": weights, "vecs": vecs, "gate_up": f["w_gate_up"][0],
        "mix_w": f["w_s_2"][0].transpose(2, 0, 1).reshape(P, D),
        "mix_b": np.broadcast_to(f["b_s_2"].reshape(1, D), (P, D)),
        "dist": dist, "logm": logm, "ident": np.eye(P, dtype=np.float32),
    }
    arrays = {k: np.ascontiguousarray(v) for k, v in arrays.items()}
    nc = bacc.Bacc("TRN2", target_bir_lowering=False, num_devices=1)
    aps = [nc.dram_tensor(k, v.shape, mybir.dt.from_np(v.dtype), kind="ExternalInput").ap()
           for k, v in arrays.items()]
    out = nc.dram_tensor("out", (KT, P, S), mybir.dt.float32, kind="ExternalOutput").ap()
    two_blocks(nc, *aps, out)
    r = run_bass_kernel_spmd(nc, [arrays], core_ids=[0])
    return np.ascontiguousarray(np.asarray(r.results[0]["out"]).reshape(D, S).T).reshape(1, S, D)
```

```python
import concourse.bass as bass
from concourse import mybir
from contextlib import ExitStack
import numpy as np

P = 128
D = 1024
S = 1024
KT = D // P
HALF = 512
EPS = 1e-6
GLA_HEADS, DK, DV, CHUNK, RANK = 4, 64, 128, 64, 16
NCH = S // CHUNK
NBLK = S // P
D_FF = 2816
HEADS, DH = 16, 64
PAIRS = HEADS // 2

U_A = 0
U_Q, U_K, U_V, U_G = 1, 3, 5, 9
U_CONV = 13
U_OUT = 25
FFN = [(33, 8, 49), (57, 8, 73), (81, 6, 93)]
U_AV = 101
U_QKV = 109
U_AU = 133
U_ATT = 141
U_PA, U_PB, U_WO = 173, 181, 189
UNITS = 197

V_G1, V_BG, V_GN, V_CW, V_G2, V_GF, V_H2, V_GV, V_FIN, V_SL = 0, 8, 10, 11, 23, 31, 39, 47, 55, 63
VECS = V_SL + HEADS


class Unit:

    def __init__(self, c, reg=None, a=0):
        self.c, self.reg, self.a = c, reg, a

    def plus(self, n):
        return Unit(self.c + n, self.reg, self.a)

    @property
    def slot(self):
        return self.c % 2

    def count(self, n=0):
        return self.c + n if self.reg is None else self.reg * self.a + (self.c + n)

    def turn(self, scale, n):
        k = scale * (self.c // 2 + n)
        return k if self.reg is None else self.reg * (scale * self.a // 2) + k


class Pair:

    def __init__(self, off, reg=None):
        self.off, self.reg = off, reg

    def count(self, per, k):
        k += per * self.off
        return k if self.reg is None else self.reg * per + k

    def unit(self, m):
        c = U_ATT + 4 * self.off + m
        return Unit(c) if self.reg is None else Unit(c, self.reg, 4)

    def index(self, per=1, k=0):
        return self.count(per, k)

    def before(self):
        return Pair(self.off - 1, self.reg)


def after(pair, m):
    return (pair, 1) if m == 1 else (Pair(pair.off + 1, pair.reg), 0)


def steps_before(m):
    return 12 * (m // 2) + 4 * (m % 2)


def chunks_of(m):
    sb = m % 2
    return [(i, c, min(HALF, (i + 1) * P - c)) for i in range(4 * sb, 4 * sb + 4)
            for c in range(0, (i + 1) * P, HALF)]


PE_STEPS = [
    "t0/t1//o0 t2/s0/o1 t3/s1/o2 t4/s2/o3 t5/s3/o4 t6//o5 t7/o6/o7 v0 v1",
    "s0//s1/s2/t0/s3/s4/s5 o0 t1//s6/s7 o1 t2///o2 t3//o3",
]
PE_STEPS = [x.split("/") for x in PE_STEPS]
ACT_STEPS = [
    "O p0 k p1 w p2 p3 e0 p4 e1 a p5 e2 p6 e3 d p7",
    "v0 v1 O e0 w p0 e1 p1 a e2 p2 d e3 p3 q",
]
DVE_STEPS = [
    "O l0 k l1 z l2 r0 l3 r1 n0 l4 r2 n1 l5 r3 n2 l6 m n3 l7",
    "v0 r0 v1 O r1 r2 z n0 l0 r3 r4 n1 l1 r5 m r6 r7 n2 l2 b n3 l3 q",
]
PE_REST = "t0 t1/o0 t2/o1 t3/o2 t4/o3 t5/o4 t6/o5 t7/o6/o7///////".split("/")
REST = "O X0 p0 p1 X1 X2 p2 X3 p3 X4 p4 X5 p5 X6 p6 X7 p7"


def steps(text, before=True, done=True, head=True, first=True):
    for x in text.split():
        kind, n = x[0], int(x[1:] or 0)
        if not ((kind in "topwlzamd" and not before) or (kind == "O" and not done)
                or (kind in "bqk" and not head) or (kind == "v" and not first)):
            yield kind, n


AT_Z = 2
AT_TURN = {5: (0, 1), 6: (2, 3, 4, 5), 7: (6, 7), 8: (8, 9), 9: (10, 11)}
AT_KV = (10, 11)
AT_SCORES = (12, 14, 16, 18)
AT_O = (13, 15, 17, 19)
AT_NORM = (14, 16, 18, 20)
AT_SILU = 12
AT_SPLIT = {21: (0, 1, 2), 22: (3, 4), 23: (5, 6), 24: (7,)}
GD_ALL = 14


def two_blocks(nc, xT, weights, vecs, gate_up, mix_w, mix_b, dist, logm, ident, out):
    f32, f32r = mybir.dt.float32, mybir.dt.float32r
    ALU = mybir.AluOpType
    ACT = mybir.ActivationFunctionType

    ctx = ExitStack()
    with ctx:
        at = {}
        top = (nc.sbuf_base + 63) // 64 * 64

        def place(name, cols, dt=f32, offset=None, rows=P):
            nonlocal top
            shape = [rows] + (list(cols) if isinstance(cols, (list, tuple)) else [cols])
            size = 4 * int(np.prod(shape[1:]))
            if offset is None:
                offset, top = top, top + (size + 63) // 64 * 64
            at[name] = offset
            return nc.alloc_sbuf_tensor_at(name, shape, dt, offset=offset)

        XH = place("x_hi", [KT, S], f32r)
        XL = place("x_lo", [KT, S], f32r)
        WR = place("w_raw", [2, KT, P])
        WH = place("w_hi", [2, KT, P], f32r)
        WL = place("w_lo", [2, KT, P], f32r)
        VEC = place("vectors", VECS)
        IDN = place("identity", P)
        ONES = place("ones", P)
        R = place("rstd", S)
        GG = place("gain_product", KT)
        DEC = place("chunk_decay", [2, NCH])
        STAT = place("softmax_stats", [4, 4])
        WGU = place("gate_up_w", 2 * P, rows=RANK)
        XR = place("residual", [KT, S])
        WK = place("work", [20, S])
        wk, xr = at["work"], at["residual"]
        TMP = 16
        MH = place("m_hi", [8, S], f32r, wk)
        ML = place("m_lo", [8, S], f32r, wk + 8 * 4 * S)
        VTOK = place("gla_v_tokens", [NBLK, GLA_HEADS * DV], f32, xr)
        KS = place("gla_k_s", [2, S], f32, xr + 4 * 4096)
        SC = place("gla_scores", [2, NBLK, P], f32, xr + 4 * 4096)
        KTOK = place("gla_k_tokens", [NBLK, GLA_HEADS * DK], f32, xr + 6 * 4096)
        ST = place("gla_states", [2, NCH, DV], f32, wk + U_V * 4096)
        ZE, ZZ, ZB = ([WK[:, c + j] for j in range(2)] for c in (13, 15, 17))
        RESET, GSQ, GT = WK[:, 19], WK[:, 18], WK[:, 19]
        MIXED = [XR[:, 6], XR[:, 7], WK[:, U_V], WK[:, U_V + 1], WK[:, 13], WK[:, 14], WK[:, 15], WK[:, 19]]
        Q2 = place("att_q", S, f32, xr)
        K2 = place("att_k", S, f32, xr + 4096)
        VT = place("att_v", S, f32, xr + 8192)
        QS = place("att_q_split", S, f32r, xr + 12288)
        KH = place("att_k_hi", S, f32r, xr + 16384)
        KL = place("att_k_lo", S, f32r, xr + 20480)
        VHL = place("att_v_split", [2, NBLK, P], f32r, xr + 24576)
        PB1 = place("att_p_late", [4, S], f32, wk)
        PB0 = place("att_p_early", [4, HALF], f32, wk + 10 * 4096)
        PH = place("att_p_hi", [2, HALF], f32r, wk + 4 * 4096)
        PL = place("att_p_lo", [2, HALF], f32r, wk + 5 * 4096)
        Y = place("att_y", S, f32, wk + 6 * 4096)
        MXL = place("att_mixed", S, f32, wk + 7 * 4096)
        DIST = place("distances", S, f32, wk + 8 * 4096)
        LOGM = place("log_counts", S, f32, wk + 9 * 4096)
        OT = place("att_o_half", HALF, f32, wk + 15 * 4096)
        BH = place("att_bias", S, f32, wk + TMP * 4096)
        SBG = place("att_b_gate", S, f32, wk + 17 * 4096)
        GAB = place("att_gates", [2, S], f32, wk + 18 * 4096)
        WKR = place("work_split", [20, S], f32r, wk)
        MIX_H = [WKR[:, t] for t in (9, 10, 11, 12, 2, 3, 4, 7)]
        MIX_L = [WKR[:, t] for t in (0, 1, U_V, U_V + 1, 13, 14, 15, 19)]
        PBS = [PB0, PB1]

        def psum(name, shape):
            return ctx.enter_context(nc.psum_tensor(name, shape, f32))

        PD = psum("dense", [P, 2, S])
        PA = psum("aux", [P, 4, HALF])

        def dram(name, n):
            return nc.dram_tensor(name, (n, P, S), f32, kind="Internal").ap()

        d_x, d_qkv, d_mix = dram("kept_x", KT), dram("kept_qkv", 3 * KT), dram("kept_mixed", KT)
        d_ya, d_yb = dram("kept_ya", KT), dram("kept_yb", KT)
        d_ga, d_gb = dram("kept_ga", KT), dram("kept_gb", KT)

        def sem(name):
            return ctx.enter_context(nc.semaphore(name))

        x_in = [sem(f"x_in{k}") for k in range(KT)]
        vec_in, tab_in, gat_in = sem("vec_in"), sem("tab_in"), sem("gat_in")
        consts = sem("consts")
        w_raw = [sem("w_raw0"), sem("w_raw1")]
        w_hi, w_lo, mm_done, evac = sem("w_hi"), sem("w_lo"), sem("mm_done"), sem("evac")
        xh, x_ready = sem("xh"), sem("x_ready")
        sq, acc, ss, rr, rs = sem("sq"), sem("acc"), sem("ss"), sem("rr"), sem("rs")
        xr_scaled = sem("xr_scaled")
        cv, conv_out = sem("dve_step"), sem("conv_out")
        s_t, m_t, mh, m_ready = sem("silu_done"), sem("m_t"), sem("mh"), sem("m_ready")
        z_mm, z_abs, z_add, ga, gd = sem("z_mm"), sem("z_abs"), sem("z_add"), sem("gla_act"), sem("gla_dve")
        g_tp, g_tc, kv_mm, st_c = sem("g_tp"), sem("g_tc"), sem("kv_mm"), sem("state_c")
        g_const, sc_mm, sc_cp, sc_sel, o_mm = sem("g_const"), sem("sc_mm"), sem("sc_cp"), sem("sc_sel"), sem("o_mm")
        o_cp, o_sq, o_ss, o_rr, o_rs = sem("o_cp"), sem("o_sq"), sem("o_ss"), sem("o_rr"), sem("o_rs")
        g_silu, g_out = sem("g_silu"), sem("g_out")
        av_t, av_g, avn, v_tp, v_tc, mix_mm, mixed = (sem(n) for n in
            ("av_t", "av_g", "avn", "v_tp", "v_tc", "mix_mm", "mixed"))
        w_sel = sem("w_sel")
        sp_x, sp_mx, sp_t = sem("sp_x"), sem("sp_mx"), [sem("sp_t0"), sem("sp_t1")]
        au_g, mx_upd = sem("au_g"), sem("mx_upd")
        q_in, k_in, v_in, mx_in = sem("q_in"), sem("k_in"), sem("v_in"), sem("mx_in")
        q_hi, k_hi, q_lo, k_lo, bias = sem("q_hi"), sem("k_hi"), sem("q_lo"), sem("k_lo"), sem("bias")
        vt_tp, v_hi, v_lo = sem("vt_tp"), sem("v_hi"), sem("v_lo")
        s_ready, ttr, ex, rl, pn = sem("s_ready"), sem("ttr"), sem("ex"), sem("rl"), sem("pn")
        t_ready, ph, pl, pv, o_half, yh = (sem(n) for n in ("t_ready", "ph", "pl", "pv", "o_half", "yh"))
        g_act, ya_up, yb_up = sem("gate_act"), sem("ya_up"), sem("yb_up")
        gated = sem("gated")
        sp_ya = sem("sp_ya")
        ld = [sem("ld0"), sem("ld1")]
        a_in = [sem(f"y_a_in{t}") for t in range(3)]
        m1 = sem("merged")
        fin, outs = sem("fin"), sem("outs")
        turns = sem("turns")

        def vec(c, n=1):
            return VEC[:, c:c + n]

        def one(t):
            return t.rearrange("p a n -> p (a n)")

        SQ_NORM2, SQ_F, SQ_V, SQ_END = 8, 16, 32, 40
        LD_YB, LD_GB, LD_X = 0, 16, 24

        block = ctx.enter_context(nc.Block())

        def all_stages(engine, stage):
            first, final = Pair(0), Pair(PAIRS - 1)
            stage(first, 0, head=False)
            stage(first, 1, before=(first, 0))
            with engine.Fori(0, PAIRS - 1) as j:
                now, following = Pair(0, j), Pair(1, j)
                stage(now, 2, before=(now, 1), done=(now, 0))
                stage(now, 3, before=(now, 2), done=(now, 1))
                stage(following, 0, before=(now, 3), done=(now, 2))
                stage(following, 1, before=(following, 0), done=(now, 3))
            stage(final, 2, before=(final, 1), done=(final, 0))
            stage(final, 3, before=(final, 2), done=(final, 1), head=False)

        @block.sync
        def _(sp):
            def load(u):
                if u.c >= 2:
                    sp.wait_ge(w_lo, u.count(-1))
                sp.dma_start(WR[:, u.slot].rearrange("p k c -> p (k c)"),
                             weights[u.count()]).then_inc(w_raw[u.slot], 16)

            def loads(c, n):
                if n >= 2:
                    with sp.Fori(0, n // 2) as i:
                        load(Unit(c, i, 2))
                        load(Unit(c + 1, i, 2))
                if n % 2:
                    load(Unit(c + n - 1))

            sp.dma_start(VEC[:], vecs).then_inc(vec_in, 16)
            for k in range(KT):
                sp.dma_start(XR[:, k], xT[k]).then_inc(x_in[k], 16)
                if k < 2:
                    load(Unit(k))
            sp.dma_start(WGU[:], gate_up).then_inc(tab_in, 16)
            sp.dma_start(IDN[:], ident).then_inc(tab_in, 16)
            loads(2, 22)
            sp.wait_ge(o_mm, GLA_HEADS)
            for k in range(KT):
                if k >= 6:
                    sp.wait_ge(x_ready, 8 + k - 6 + 1)
                sp.dma_start(XR[:, k], xT[k]).then_inc(x_in[k], 16)
            loads(24, U_AV + 4 - 24)
            sp.dma_start(WK[:, 10], mix_w).then_inc(gat_in, 16)
            sp.dma_start(WK[:, 11], mix_b).then_inc(gat_in, 16)
            loads(U_AV + 4, U_AU + 2 - U_AV - 4)

            def load_qk(j, h, first):
                if not first:
                    sp.wait_ge(q_lo, 2 * j + h)
                    sp.wait_ge(k_lo, 2 * j + h)
                for t, sm, c in ((Q2, q_in, 0), (K2, k_in, 1)):
                    src = d_qkv[3 * j + c, h * DH:(h + 1) * DH, :]
                    sp.dma_start(t[0:DH], src).then_inc(sm, 16)
                    sp.dma_start(t[DH:P], src).then_inc(sm, 16)

            def load_v(j, first):
                if not first:
                    sp.wait_ge(vt_tp, 2 * j)
                sp.dma_start(VT[:], d_qkv[3 * j + 2]).then_inc(v_in, 16)

            def load_mixed(j):
                sp.wait_ge(sp_ya, 16 * j + 16)
                sp.dma_start(MXL[:], d_mix[j + 1]).then_inc(mx_in, 16)

            sp.wait_ge(mix_mm, KT)
            sp.dma_start(DIST[:], dist).then_inc(tab_in, 16)
            sp.dma_start(LOGM[:], logm).then_inc(tab_in, 16)
            sp.wait_ge(sp_x, 16 * KT)
            for t in range(2):
                sp.wait_ge(sp_t[t], 16 * 12)
            load_qk(0, 0, True)
            load_v(0, True)
            loads(U_AU + 2, 8)
            sp.wait_ge(sp_mx, 16 * KT)
            sp.dma_start(MXL[:], d_mix[0]).then_inc(mx_in, 16)
            with sp.Fori(0, PAIRS - 1) as j:
                load_qk(j, 1, False)
                load(Unit(U_ATT + 2, j, 4))
                load(Unit(U_ATT + 3, j, 4))
                load_v(j + 1, False)
                load_mixed(j)
                load_qk(j + 1, 0, False)
                load(Unit(U_ATT + 4, j, 4))
                load(Unit(U_ATT + 5, j, 4))
            load_qk(PAIRS - 1, 1, False)
            for m in range(4):
                load(Unit(U_ATT + 4 * (PAIRS - 1) + 2 + m))

            sp.wait_ge(sp_ya, 16 * KT)
            sp.wait_ge(q_lo, HEADS)
            sp.wait_ge(k_lo, HEADS)
            sp.wait_ge(vt_tp, 2 * PAIRS)
            for k in range(KT):
                if k >= 3:
                    sp.wait_ge(x_ready, 32 + k - 3 + 1)
                sp.dma_start(XR[:, k % 3], d_ya[k]).then_inc(a_in[k % 3], 16)

            n = 0
            used = []

            def fetch(src, by, count):
                nonlocal n
                if n >= 2:
                    sp.wait_ge(*used[n - 2])
                used.append((by, count))
                sp.dma_start(WK[:, TMP + n % 2], src).then_inc(ld[n % 2], 16)
                n += 1

            sp.wait_ge(sp_x, 16 * 2 * KT)
            for t in range(2):
                sp.wait_ge(sp_t[t], 16 * (12 + KT))
            for k in range(KT):
                fetch(d_yb[k], m_ready, 22 + k + 1)
                load(Unit(U_PA + k + 2))
                fetch(d_ga[k], evac, U_PA + k + 1)
            for k in range(KT):
                load(Unit(U_PB + k + 2))
                fetch(d_gb[k], evac, U_PB + k + 1)
            for k in range(KT):
                if U_WO + k + 2 < UNITS:
                    load(Unit(U_WO + k + 2))
                fetch(d_x[k], evac, U_WO + k + 1)
            for k in range(KT):
                sp.wait_ge(fin, k + 1)
                sp.dma_start(out[k], XR[:, k]).then_inc(outs, 16)
            sp.wait_ge(outs, 16 * KT)

        @block.gpsimd
        def _(pool):
            def split(u):
                pool.wait_ge(w_hi, u.count(1))
                pool.tensor_tensor(WL[:, u.slot], WR[:, u.slot], WH[:, u.slot].bitcast(f32),
                                   ALU.subtract).then_inc(w_lo, 1)

            def splits(c, n):
                if n >= 2:
                    with pool.Fori(0, n // 2) as i:
                        split(Unit(c, i, 2))
                        split(Unit(c + 1, i, 2))
                if n % 2:
                    split(Unit(c + n - 1))

            pool.memset(ONES[:], 1.0).then_inc(consts, 1)
            for u in range(U_OUT + 2):
                split(Unit(u))
                if u == 2:
                    pool.wait_ge(rs, 1)
                    pool.memset(RESET, 1.0).then_inc(g_const, 1)
                    pool.wait_ge(g_const, 1)
                    pool.memset(RESET.rearrange("p (c t) -> p c t", t=CHUNK)[:, :, 0:1], 0.0).then_inc(g_const, 1)
                if u == 10:
                    pool.wait_ge(g_tp, 4)
                    for s in range(2):
                        pool.memset(SC[:, s], 0.0).then_inc(g_const, 1)
                if u - 2 in AT_SCORES:
                    h = AT_SCORES.index(u - 2)
                    pool.wait_ge(sc_cp, h + 1)
                    pool.affine_select(out=SC[:, h % 2], in_=SC[:, h % 2], compare_op=ALU.is_ge, fill=0.0,
                                       base=0, pattern=[[0, NBLK], [1, P]], channel_multiplier=-1
                                       ).then_inc(sc_sel, 1)
            splits(U_OUT + 2, U_AV + 4 - U_OUT - 2)
            pool.wait_ge(gat_in, 32)
            w3 = WK[:, 10].rearrange("p (g t) -> p g t", t=P)
            pool.affine_select(out=w3, in_=w3, compare_op=ALU.is_ge, fill=0.0, base=0,
                               pattern=[[0, KT], [1, P]], channel_multiplier=-1).then_inc(w_sel, 1)
            splits(U_AV + 4, U_ATT + 2 - U_AV - 4)

            def stage(pair, m, before=None, done=None, head=True):
                if m == 1 and done:
                    gate_y(done[0])
                if before:
                    split(pair.unit(m).plus(1))
                if m == 1:
                    pool.wait_ge(gated, pair.count(2, 1))
                    pool.wait_ge(mx_in, pair.count(16, 16))
                    pool.tensor_tensor(MXL[:], MXL[:], WK[:, 14], ALU.mult).then_inc(ya_up, 1)

            def gate_y(pair):
                pool.wait_ge(yh, pair.count(4, 4))
                pool.wait_ge(gated, pair.count(2, 2))
                pool.tensor_tensor(Y[:], Y[:], SBG[:], ALU.mult).then_inc(yb_up, 1)

            all_stages(pool, stage)
            split(Unit(U_PA + 1))
            gate_y(Pair(PAIRS - 1))
            splits(U_PA + 2, UNITS - U_PA - 2)

        @block.tensor
        def _(pe):
            def unit(u, H=XH, L=XL, nk=KT, ready=None, between=None):
                pe.wait_ge(w_hi, u.count(1))
                pe.wait_ge(w_lo, u.count(1))
                if u.c >= 2:
                    pe.wait_ge(evac, u.count(-1))
                for t in range(2):
                    dst = PD[:, u.slot, t * HALF:(t + 1) * HALF]
                    for k in range(nk):
                        if ready and t == 0:
                            pe.wait_ge(ready[0], ready[1] + k + 1)
                        tok = slice(t * HALF, (t + 1) * HALF)
                        hi, lo = (H[k][:, tok], L[k][:, tok]) if isinstance(H, list) else (H[:, k, tok], L[:, k, tok])
                        pe.matmul(dst, WH[:, u.slot, k], hi, start=(k == 0), stop=False)
                        pe.matmul(dst, WH[:, u.slot, k], lo, start=False, stop=False)
                        last = pe.matmul(dst, WL[:, u.slot, k], hi, start=False, stop=(k == nk - 1))
                        if t == 1 and k == nk - 1:
                            last.then_inc(mm_done, 1)
                        if between:
                            between(t * nk + k)

            def units(c, n, **kw):
                if n >= 2:
                    with pe.Fori(0, n // 2) as i:
                        unit(Unit(c, i, 2), **kw)
                        unit(Unit(c + 1, i, 2), **kw)
                if n % 2:
                    unit(Unit(c + n - 1), **kw)

            def column_sums(count, src, bank=0):
                pe.wait_ge(acc, count)
                for t in range(2):
                    last = pe.matmul(PA[:, bank + t], ONES[:], src[:, t * HALF:(t + 1) * HALF],
                                     start=True, stop=True)
                last.then_inc(ss, 1)

            pe.wait_ge(consts, 1)
            unit(Unit(0), ready=(x_ready, 0))
            column_sums(8, WK[:, TMP + 2])

            def gate_logits():
                pe.wait_ge(tab_in, 32)
                pe.wait_ge(evac, 1)
                pe.wait_ge(rr, 1)
                for j in range(2):
                    for t in range(2):
                        last = pe.matmul(PA[:, 2 * j + t], WGU[:, j * P:(j + 1) * P],
                                         WK[0:RANK, 0, t * HALF:(t + 1) * HALF], start=True, stop=True)
                    last.then_inc(z_mm, 1)

            def turn(n):
                if n < 4:
                    src = KS[:, n // 2]
                    pe.wait_ge(gd, 11 + 2 * (n // 2))
                else:
                    src = WK[:, U_V + n // 2 - 2]
                    pe.wait_ge(evac, U_V + n // 2 - 2 + 1)
                if n >= 4:
                    pe.wait_ge(g_tc, n - 3)
                for b in range(4):
                    blk = 4 * (n % 2) + b
                    last = pe.transpose(PA[:, n % 4, b * P:(b + 1) * P], src[:, blk * P:(blk + 1) * P], IDN[:])
                last.then_inc(g_tp, 1)

            def chunk_products(j):
                pe.wait_ge(g_tc, 12)
                if j:
                    pe.wait_ge(st_c, NCH - 1)
                for c in range(NCH):
                    half, blk, col = c % 2, c // 2, (c // 2) % 4 * DV
                    rows = slice(CHUNK * half, CHUNK * (half + 1))
                    for p in range(2):
                        h = 2 * j + p
                        last = pe.matmul(PA[p * DK:(p + 1) * DK, 2 * half + blk // 4, col:col + DV],
                                         KTOK[rows, blk, h * DK:(h + 1) * DK],
                                         VTOK[rows, blk, h * DV:(h + 1) * DV], start=True, stop=True)
                    if c % 8 == 7:
                        last.then_inc(kv_mm, 1)

            def scores(h):
                rows = slice(h % 2 * DK, (h % 2 + 1) * DK)
                if h == 0:
                    pe.wait_ge(st_c, 2 * (NCH - 1))
                    pe.wait_ge(gd, GD_ALL)
                else:
                    pe.wait_ge(sc_cp, h)
                for b in range(NBLK):
                    tok = slice(b * P, (b + 1) * P)
                    last = pe.matmul(PA[:, b // 4, b % 4 * P:(b % 4 + 1) * P], WK[rows, U_K + h // 2, tok],
                                     WK[rows, U_Q + h // 2, tok], start=True, stop=True)
                last.then_inc(sc_mm, 1)

            def outputs(h):
                rows = slice(h % 2 * DK, (h % 2 + 1) * DK)
                pe.wait_ge(sc_sel, h + 1)
                if h:
                    pe.wait_ge(o_rr, h)
                for b in range(NBLK):
                    bank, col = 2 + b // 4, b % 4 * P
                    pe.matmul(PA[:, bank, col:col + P], VTOK[:, b, h * DV:(h + 1) * DV], SC[:, h % 2, b],
                              start=True, stop=False)
                    for c in (2 * b, 2 * b + 1):
                        last = pe.matmul(PA[:, bank, col + c % 2 * CHUNK:col + (c % 2 + 1) * CHUNK],
                                         ST[rows, h // 2, c], WK[rows, U_Q + h // 2, c * CHUNK:(c + 1) * CHUNK],
                                         start=False, stop=(c % 2 == 1))
                last.then_inc(o_mm, 1)

            def norm_sums(h):
                pe.wait_ge(o_sq, h + 1)
                for t in range(2):
                    last = pe.matmul(PA[:, 2 + t], ONES[:], GSQ[:, t * HALF:(t + 1) * HALF],
                                     start=True, stop=True)
                last.then_inc(o_ss, 1)

            for u in range(1, U_OUT):
                unit(Unit(u))
                if u == AT_Z:
                    gate_logits()
                for n in AT_TURN.get(u, ()):
                    turn(n)
                if u in AT_KV:
                    chunk_products(AT_KV.index(u))
                if u in AT_NORM:
                    norm_sums(AT_NORM.index(u))
                if u in AT_SCORES:
                    scores(AT_SCORES.index(u))
                if u in AT_O:
                    outputs(AT_O.index(u))

            unit(Unit(U_OUT), H=MIX_H, L=MIX_L, ready=(x_ready, 8))
            units(U_OUT + 1, 7, H=MIX_H, L=MIX_L)
            for n, (first, tiles, down) in enumerate(FFN):
                if n == 0:
                    unit(Unit(first), ready=(x_ready, 16),
                         between=lambda g: column_sums(16, WK[:, TMP + 2]) if g == 8 else None)
                    unit(Unit(first + 1))
                    units(first + 2, 2 * tiles - 2)
                else:
                    units(first, 2 * tiles)
                unit(Unit(down), H=MH, L=ML, nk=tiles, ready=(m_ready, 8 * n))
                units(down + 1, 7, H=MH, L=ML, nk=tiles)

            def both_sums(g):
                if g == 8:
                    column_sums(31, WK[:, TMP + 2])
                    column_sums(32, WK[:, TMP + 3], 2)

            unit(Unit(U_AV), ready=(x_ready, 24), between=both_sums)
            units(U_AV + 1, 7)
            units(U_QKV, 2)
            column_sums(SQ_V + 8, WK[:, TMP + 2])
            units(U_QKV + 2, 4)

            def gating_transposes(g):
                pe.wait_ge(avn, g + 1)
                if g:
                    pe.wait_ge(v_tc, 2 * g)
                for b in range(NBLK):
                    last = pe.transpose(PA[:, b // 4, b % 4 * P:(b % 4 + 1) * P],
                                        WK[:, g, b * P:(b + 1) * P], IDN[:])
                    if b % 4 == 3:
                        last.then_inc(v_tp, 1)

            def mixing(g):
                pe.wait_ge(v_tc, 2 * g + 2)
                if g:
                    pe.wait_ge(mixed, g)
                for b in range(NBLK):
                    last = pe.matmul(PA[:, 2 + b // 4, b % 4 * P:(b % 4 + 1) * P],
                                     WK[:, 8 + g % 2, b * P:(b + 1) * P], WK[:, 10, g * P:(g + 1) * P],
                                     start=True, stop=True)
                last.then_inc(mix_mm, 1)

            pe.wait_ge(w_sel, 1)
            for g in range(KT):
                gating_transposes(g)
                unit(Unit(U_QKV + 6 + g))
                mixing(g)
            units(U_QKV + 6 + KT, 18 - KT)
            units(U_AU, 8)

            def v_transposes(pair, q):
                if q == 0:
                    pe.wait_ge(v_in, pair.count(16, 16))
                for b in range(4):
                    last = pe.transpose(PA[:, q, b * P:(b + 1) * P],
                                        VT[:, (4 * q + b) * P:(4 * q + b + 1) * P], IDN[:])
                last.then_inc(vt_tp, 1)

            def score_chunk(pair, m, n):
                i, c, w = chunks_of(m)[n]
                base, sb = steps_before(m), m % 2
                bank = 0 if sb and n % 2 else 2
                if n == 0 and sb == 0:
                    pe.wait_ge(q_lo, pair.count(2, m // 2 + 1))
                    pe.wait_ge(k_lo, pair.count(2, m // 2 + 1))
                if m == 1 and n == 1:
                    pe.wait_ge(v_lo, pair.count(2, 1))
                if n >= 1 + sb:
                    pe.wait_ge(ttr, pair.count(24, base + n - sb))
                elif sb and n == 0:
                    pe.wait_ge(ttr, pair.count(24, base))
                dst = PA[:, bank, 0:w]
                pe.matmul(dst, QS[:, i * P:(i + 1) * P], KH[:, c:c + w], start=True, stop=False)
                pe.matmul(dst, QS[:, i * P:(i + 1) * P], KL[:, c:c + w], start=False, stop=True
                          ).then_inc(s_ready, 1)

            def turn_p(pair, m, k):
                base, sb = steps_before(m), m % 2
                bank = k % 2 if sb else 1
                if k == 0:
                    pe.wait_ge(pn, pair.count(16, 4 * m + 4))
                    if m == 0:
                        pe.wait_ge(v_lo, pair.count(2, 2))
                if k >= 1 + sb:
                    pe.wait_ge(pl, pair.count(24, base + k - sb))
                for b in range(max(0, k - 4 * sb), 4):
                    last = pe.transpose(PA[:, bank, b * P:(b + 1) * P], PBS[sb][:, b, k * P:(k + 1) * P],
                                        IDN[:])
                last.then_inc(t_ready, 1)

            def weigh_v(pair, m, k):
                base, sb = steps_before(m), m % 2
                pe.wait_ge(pl, pair.count(24, base + k + 1))
                if k == 0 and (m or pair.reg is not None or pair.off):
                    pe.wait_ge(yh, pair.count(4, m))
                lo = max(0, k - 4 * sb) * P
                dst = PA[:, 3, lo:HALF]
                pe.matmul(dst, VHL[:, m // 2, k], PH[:, k % 2, lo:HALF], start=(k == 0), stop=False)
                pe.matmul(dst, VHL[:, m // 2, k], PL[:, k % 2, lo:HALF], start=False,
                          stop=(k == 4 * sb + 3)).then_inc(pv, 1)

            def stage(pair, m, before=None, **have):
                def between(g):
                    for kind, n in steps(PE_STEPS[m % 2][g], before=bool(before), first=m == 0):
                        if kind == "s":
                            score_chunk(pair, m, n)
                        elif kind == "t":
                            turn_p(*before, n)
                        elif kind == "o":
                            weigh_v(*before, n)
                        else:
                            v_transposes(pair, n)

                unit(pair.unit(m), between=between)

            all_stages(pe, stage)

            def rest(g):
                for kind, k in steps(PE_REST[g]):
                    (turn_p if kind == "t" else weigh_v)(Pair(PAIRS - 1), 3, k)

            unit(Unit(U_PA), ready=(x_ready, 32), between=rest)
            units(U_PA + 1, 7)
            unit(Unit(U_PB), H=MH, L=ML, ready=(m_ready, 22))
            units(U_PB + 1, 7, H=MH, L=ML)
            unit(Unit(U_WO), ready=(x_ready, 40))
            units(U_WO + 1, 7)
            column_sums(SQ_END + 8, WK[:, 0])

        @block.scalar
        def _(act):
            def split(u):
                if u.reg is None and u.c >= UNITS:
                    return
                act.wait_ge(w_raw[u.slot], u.turn(16, 1))
                if u.c >= 2:
                    act.wait_ge(mm_done, u.count(-1))
                act.copy(WH[:, u.slot], WR[:, u.slot]).then_inc(w_hi, 1)

            def splits(c, n):
                if n >= 2:
                    with act.Fori(0, n // 2) as i:
                        split(Unit(c, i, 2))
                        split(Unit(c + 1, i, 2))
                if n % 2:
                    split(Unit(c + n - 1))

            def square(src, n, scale=1.0):
                if n >= 2:
                    act.wait_ge(acc, n - 1)
                act.activation(WK[:, TMP + n % 2], src, ACT.Square, scale=scale).then_inc(sq, 1)

            def root(n, src, dst=R[:]):
                act.wait_ge(rr, n)
                act.activation(dst, src, ACT.Sqrt).then_inc(rs, 1)

            act.wait_ge(vec_in, 16)
            for k in range(KT):
                act.wait_ge(x_in[k], 16)
                act.activation(XH[:, k], XR[:, k], ACT.Copy, scale=vec(V_G1 + k)).then_inc(xh, 1)
                if k < 2:
                    split(Unit(k))
                square(XR[:, k], k)
            root(1, WK[:, TMP + 3])
            split(Unit(2))
            for u in range(1, U_OUT):
                split(Unit(u + 2))
                if u == AT_Z:
                    act.wait_ge(z_mm, 2)
                    for j in range(2):
                        act.activation(ZE[j], one(PA[:, 2 * j:2 * j + 2]), ACT.Abs, bias=vec(V_BG + j)
                                       ).then_inc(z_abs, 1)
                    act.preload_act_table(ACT.Ln)
                    for j in range(2):
                        act.wait_ge(z_abs, j + 1)
                        act.activation(ZE[j], ZE[j], ACT.Exp, scale=-1.0).then_inc(ga, 1)
                    for j in range(2):
                        act.wait_ge(ga, j + 1)
                        act.activation(ZE[j], ZE[j], ACT.Ln, bias=1.0).then_inc(ga, 1)
                if u == AT_Z + 1:
                    for j in range(2):
                        act.wait_ge(gd, 3 + j)
                        act.activation(ZE[j], ZB[j], ACT.Exp, scale=1.0 / 16).then_inc(ga, 1)
                        act.activation(ZZ[j], ZB[j], ACT.Exp, scale=-1.0 / 16).then_inc(ga, 1)
                if u == AT_Z + 2:
                    for j in range(2):
                        act.wait_ge(gd, 7 + 3 * j)
                        act.activation(ZE[j], ZE[j], ACT.Exp, scale=1.0 / 16).then_inc(ga, 1)
                for n in AT_TURN.get(u, ()):
                    act.wait_ge(g_tp, n + 1)
                    blocks = slice(4 * (n % 2), 4 * (n % 2) + 4)
                    i = n // 2
                    dst = (KTOK[:, blocks, i * P:(i + 1) * P] if i < 2 else
                           VTOK[:, blocks, (i - 2) * P:(i - 1) * P])
                    act.copy(dst, PA[:, n % 4].rearrange("p (b f) -> p b f", f=P)).then_inc(g_tc, 1)
                if u == AT_SILU:
                    act.wait_ge(evac, U_G + GLA_HEADS)
                    for h in range(GLA_HEADS):
                        act.activation(WK[:, U_G + h], WK[:, U_G + h], ACT.Silu).then_inc(g_silu, 1)
                if u in AT_NORM:
                    h = AT_NORM.index(u)
                    act.wait_ge(o_rr, h + 1)
                    act.activation(GT, GT, ACT.Sqrt).then_inc(o_rs, 1)
                if u in AT_O:
                    h = AT_O.index(u)
                    act.wait_ge(o_mm, h + 1)
                    act.copy(MIXED[h], one(PA[:, 2:4])).then_inc(o_cp, 1)
                    act.wait_ge(o_cp, h + 1)
                    if h:
                        act.wait_ge(o_ss, h)
                    act.activation(GSQ, MIXED[h], ACT.Square).then_inc(o_sq, 1)

                for k in AT_SPLIT.get(u, ()):
                    if k < 4:
                        act.wait_ge(g_out, k + 1)
                    else:
                        act.wait_ge(conv_out, k - 3)
                    act.copy(MIX_H[k], MIXED[k]).then_inc(xh, 1)

            def hi_part(k, src, scale=None):
                if scale is None:
                    act.copy(XH[:, k], src).then_inc(xh, 1)
                else:
                    act.activation(XH[:, k], src, ACT.Copy, scale=scale).then_inc(xh, 1)

            for k in range(KT):
                split(Unit(U_OUT + k + 2))
                act.wait_ge(evac, U_OUT + k + 1)
                hi_part(k, XR[:, k], vec(V_G2 + k))
                square(XR[:, k], SQ_NORM2 + k)
            root(2, WK[:, TMP + 3])

            act.preload_act_table(ACT.Silu)
            act.wait_ge(gd, GD_ALL + 1)
            for n, (first, tiles, down) in enumerate(FFN):
                with act.Fori(0, tiles) as i:
                    u = Unit(first, i, 2)
                    split(u.plus(2))
                    act.wait_ge(evac, u.count(1))
                    act.activation(WK[:, TMP + 1], WK[:, TMP], ACT.Silu).then_inc(s_t, 1)
                    split(u.plus(3))
                    act.wait_ge(m_t, i + (8 * n + 1))
                    act.copy(MH[:, i], WK[:, TMP + 3]).then_inc(mh, 1)
                if n < 2:
                    splits(down + 2, 8)
                else:
                    for k in range(8):
                        split(Unit(down + 2 + k))
                        act.wait_ge(evac, down + k + 1)
                        hi_part(k, XR[:, k], GG[:, k:k + 1])
                        square(XR[:, k], SQ_F + 2 * k)
                        square(XR[:, k], SQ_F + 2 * k + 1, vec(V_GF + k))

            act.wait_ge(rr, 4)
            act.activation(R[:], WK[:, 8], ACT.Sqrt).then_inc(rs, 1)
            act.activation(WK[:, 9], WK[:, TMP + 3], ACT.Sqrt).then_inc(rs, 1)
            for k in range(KT):
                split(Unit(U_AV + k + 2))
                act.wait_ge(evac, U_AV + k + 1)
                act.activation(WK[:, k], WK[:, 12 + k % 2], ACT.Gelu_apprx_tanh).then_inc(av_g, 1)
                act.wait_ge(av_g, k + 1)
                square(WK[:, k], SQ_V + k)
                act.wait_ge(xr_scaled, k + 1)
                act.dma_start(d_x[k], XR[:, k]).then_inc(sp_x, 16)

            def keep(u, t):
                act.wait_ge(evac, u.count(1))
                act.dma_start(d_qkv[u.count(-U_QKV)], WK[:, 12 + t]).then_inc(sp_t[t], 16)

            def keeps(c, n):
                with act.Fori(0, n // 2) as i:
                    for s in range(2):
                        u = Unit(c + s, i, 2)
                        split(u.plus(2))
                        keep(u, s)

            keeps(U_QKV, 2)
            root(5, WK[:, TMP + 3], WK[:, TMP + 3])
            keeps(U_QKV + 2, 4)
            for g in range(KT):
                if g >= 2:
                    act.wait_ge(mix_mm, g - 1)
                for q in range(2):
                    act.wait_ge(v_tp, 2 * g + q + 1)
                    act.copy(WK[:, 8 + g % 2, q * HALF:(q + 1) * HALF], PA[:, q]).then_inc(v_tc, 1)
                u = Unit(U_QKV + 6 + g)
                split(u.plus(2))
                keep(u, g % 2)
            keeps(U_QKV + 6 + KT, 18 - KT)
            def head_q(pair, h):
                act.wait_ge(q_in, pair.count(64, 32 * h + 32))
                act.activation(QS[:], Q2[:], ACT.Copy, scale=DH ** -0.5).then_inc(q_hi, 1)

            def head_k(pair, h):
                act.wait_ge(k_in, pair.count(64, 32 * h + 32))
                act.copy(KH[:], K2[:]).then_inc(k_hi, 1)

            act.preload_act_table(ACT.Gelu_apprx_tanh)
            for k in range(KT):
                u = Unit(U_AU + k)
                split(u.plus(2))
                act.wait_ge(evac, u.count(1))
                act.activation(WK[:, 14 + k % 2], WK[:, 12 + k % 2], ACT.Gelu_apprx_tanh).then_inc(au_g, 1)
                act.wait_ge(mx_upd, k + 1)
                act.dma_start(d_mix[k], WK[:, k]).then_inc(sp_mx, 16)
                if k == 4:
                    head_q(Pair(0), 0)
                    head_k(Pair(0), 0)

            def exp_block(pair, m, b):
                sb = m % 2
                w = (4 * sb + b + 1) * P
                act.wait_ge(ttr, pair.count(24, steps_before(m) + (b + 1) * (sb + 1)))
                p = PBS[sb][:, b, 0:w]
                act.activation(p, p, ACT.Exp, scale=-1.0, bias=STAT[:, 1, b:b + 1],
                               accum_out=STAT[:, 2, b:b + 1]).then_inc(ex, 1)

            def p_hi(pair, m, k):
                base, sb = steps_before(m), m % 2
                lo = max(0, k - 4 * sb) * P
                bank = k % 2 if sb else 1
                act.wait_ge(t_ready, pair.count(24, base + k + 1))
                if k >= 2:
                    act.wait_ge(pv, pair.count(24, base + k - 1))
                act.copy(PH[:, k % 2, lo:HALF], PA[:, bank, lo:HALF]).then_inc(ph, 1)

            def o_part(pair, m):
                act.wait_ge(pv, pair.count(24, steps_before(m) + 4 + 4 * (m % 2)))
                act.copy(OT[0:DH], PA[DH:P, 3]).then_inc(o_half, 1)

            def gate(pair, m):
                u = pair.unit(m)
                if m >= 2:
                    act.wait_ge(sp_t[m - 2], pair.count(16, 16 * 12))
                dst = (WK[:, 14], SBG[:], GAB[:, 0], GAB[:, 1])[m]
                act.wait_ge(evac, u.count(1))
                act.activation(dst, WK[:, 12 + u.slot], ACT.Tanh, scale=0.5).then_inc(g_act, 1)

            def store(pair, m):
                if m == 0:
                    act.wait_ge(ya_up, pair.count(1, 1))
                    act.dma_start(d_ya[pair.index()], MXL[:]).then_inc(sp_ya, 16)
                elif m >= 2:
                    act.wait_ge(g_act, pair.count(4, m + 1))
                    act.dma_start((d_ga, d_gb)[m - 2][pair.index()], GAB[:, m - 2]).then_inc(sp_t[m - 2], 16)

            def store_y(pair):
                act.wait_ge(yb_up, pair.count(1, 1))
                act.dma_start(d_yb[pair.index()], Y[:]).then_inc(sp_x, 16)

            def stage(pair, m, before=None, done=None, head=True):
                if m == 1 and not done:
                    act.wait_ge(sp_mx, 16 * KT)
                for kind, n in steps(ACT_STEPS[m % 2], bool(before), bool(done), head, m < 2):
                    if kind == "e":
                        exp_block(pair, m, n)
                    elif kind == "p":
                        p_hi(*before, n)
                    elif kind == "O":
                        o_part(*done)
                    elif kind == "q":
                        head_q(*after(pair, m))
                    elif kind == "k":
                        head_k(pair, m // 2)
                    elif kind == "w":
                        split(pair.unit(m).plus(1))
                    elif kind == "a":
                        gate(*before)
                    elif kind == "d":
                        store(*before)
                        if m == 1 and done:
                            store_y(done[0])
                    elif kind == "v" and m == 1:
                        if n == 0 and done:
                            act.wait_ge(pv, pair.count(24, 0))
                        act.wait_ge(vt_tp, pair.count(2, n + 1))
                        act.copy(VHL[:, :, 4 * n:4 * n + 4, 0:DH].rearrange("p h b d -> p b h d"),
                                 PA[:, n].rearrange("p (b h d) -> p b h d", h=2, d=DH)).then_inc(v_hi, 1)

            act.preload_act_table(ACT.Exp)
            all_stages(act, stage)
            final = Pair(PAIRS - 1)
            act.wait_ge(mm_done, U_PA)
            for kind, k in steps(REST):
                if kind == "O":
                    o_part(final, 2)
                elif kind == "p":
                    p_hi(final, 3, k)
                else:
                    act.wait_ge(a_in[k % 3], 16 * (k // 3 + 1))
                    hi_part(k, XR[:, k % 3], 0.5)
            split(Unit(U_PA + 1))
            o_part(final, 3)
            gate(final, 3)
            store(final, 3)
            store_y(final)

            def loaded(n):
                act.wait_ge(ld[n % 2], 16 * (n // 2 + 1))

            for k in range(KT):
                n = LD_YB + 2 * k
                loaded(n)
                if k == 0:
                    for t in range(2):
                        act.wait_ge(sp_t[t], 16 * (12 + KT))
                    act.wait_ge(sp_x, 16 * 2 * KT)
                act.activation(MH[:, k], WK[:, TMP + n % 2], ACT.Copy, scale=0.5).then_inc(mh, 1)
                split(Unit(U_PA + k + 2))
            for k in range(KT):
                split(Unit(U_PB + k + 2))
                act.wait_ge(m1, k + 1)
                hi_part(k, XR[:, k], 0.5)
            for k in range(KT):
                split(Unit(U_WO + k + 2))
                act.wait_ge(evac, U_WO + k + 1)
                n = SQ_END + k
                if k >= 2:
                    act.wait_ge(acc, n - 1)
                act.activation(WK[:, 2 + n % 2], XR[:, k], ACT.Square).then_inc(sq, 1)
            root(6, WK[:, 1])

        @block.vector
        def _(dve):
            def lo_part(k, src, n, scale=None, H=XH, L=XL, made=xh, ready=x_ready):
                dve.wait_ge(made, n)
                if scale is None:
                    dve.tensor_tensor(L[:, k], src, H[:, k].bitcast(f32), ALU.subtract).then_inc(ready, 1)
                else:
                    dve.scalar_tensor_tensor(L[:, k], src, scale, H[:, k].bitcast(f32),
                                             ALU.mult, ALU.subtract).then_inc(ready, 1)

            def add_square(n, first, dst, src=None):
                src = WK[:, TMP + n % 2] if src is None else src
                dve.wait_ge(sq, n + 1)
                if first:
                    dve.tensor_copy(dst, src).then_inc(acc, 1)
                else:
                    dve.wait_ge(acc, n)
                    dve.tensor_tensor(dst, dst, src, ALU.add).then_inc(acc, 1)

            def mean_recip(n_ss, n_rr, dst, width, bank=0):
                dve.wait_ge(ss, n_ss)
                dve.tensor_scalar(dst, one(PA[:, bank:bank + 2]), 1.0 / width, EPS, ALU.mult, ALU.add
                                  ).then_inc(cv, 1)
                nonlocal_cv[0] += 1
                dve.wait_ge(cv, nonlocal_cv[0])
                dve.reciprocal(dst, dst).then_inc(rr, 1)

            nonlocal_cv = [0]

            def chain(ins):
                nonlocal_cv[0] += 1
                ins.then_inc(cv, 1)
                dve.wait_ge(cv, nonlocal_cv[0])

            def scaled(u, dst):
                dve.wait_ge(mm_done, u.count(1))
                return dve.tensor_tensor(dst, PD[:, u.slot], R[:], ALU.mult).then_inc(evac, 1)

            dve.wait_ge(vec_in, 16)
            for k in range(KT):
                lo_part(k, XR[:, k], k + 1, vec(V_G1 + k))
                add_square(k, k == 0, WK[:, TMP + 2])
            mean_recip(1, 1, WK[:, TMP + 3], D)
            dve.wait_ge(rs, 1)
            def gla_gates(stage):
                for j in range(2):
                    q, k = WK[:, U_Q + j], WK[:, U_K + j]
                    E, Z, B = ZE[j], ZZ[j], ZB[j]
                    b3 = B.rearrange("p (c t) -> p c t", t=CHUNK)
                    e3 = E.rearrange("p (c t) -> p c t", t=CHUNK)
                    if stage == 1:
                        dve.wait_ge(ga, 5 + 2 * j)
                        dve.scalar_tensor_tensor(q, q, DK ** -0.5, E, ALU.mult, ALU.mult).then_inc(gd, 1)
                        dve.tensor_copy(DEC[:, j], e3[:, :, CHUNK - 1]).then_inc(gd, 1)
                        dve.wait_ge(gd, 6 + 3 * j)
                        dve.tensor_tensor(e3, b3[:, :, CHUNK - 1:CHUNK].to_broadcast([P, NCH, CHUNK]), b3,
                                          ALU.subtract).then_inc(gd, 1)
                    if stage == 2:
                        dve.wait_ge(ga, 9 + j)
                        dve.tensor_tensor(KS[:, j], k, E, ALU.mult).then_inc(gd, 1)
                        dve.wait_ge(gd, 11 + 2 * j)
                        dve.tensor_tensor(k, k, Z, ALU.mult).then_inc(gd, 1)

            def gla_decays():
                dve.wait_ge(z_abs, 2)
                for j in range(2):
                    dve.tensor_scalar(ZZ[j], one(PA[:, 2 * j:2 * j + 2]), vec(V_BG + j), None, ALU.add
                                      ).then_inc(z_add, 1)
                for j in range(2):
                    dve.wait_ge(ga, 3 + j)
                    dve.wait_ge(z_add, j + 1)
                    dve.scalar_tensor_tensor(ZZ[j], ZZ[j], 0.0, ZE[j], ALU.min, ALU.subtract).then_inc(gd, 1)
                dve.wait_ge(g_const, 2)
                for j in range(2):
                    dve.wait_ge(gd, 1 + j)
                    dve.tensor_tensor_scan(ZB[j], RESET, ZZ[j], 0.0, ALU.mult, ALU.add).then_inc(gd, 1)

            def gla_states(j):
                chain(dve.memset(ST[:, j, 0], 0.0))
                for c in range(NCH - 1):
                    if c % 8 == 0:
                        dve.wait_ge(kv_mm, 2 * j + c // 8 + 1)
                    if c:
                        dve.wait_ge(st_c, (NCH - 1) * j + c)
                    half, blk = c % 2, c // 2
                    dve.scalar_tensor_tensor(ST[:, j, c + 1], ST[:, j, c], DEC[:, j, c:c + 1],
                                             PA[:, 2 * half + blk // 4, blk % 4 * DV:(blk % 4 + 1) * DV],
                                             ALU.mult, ALU.add).then_inc(st_c, 1)

            def gla_scores(h):
                dve.wait_ge(sc_mm, h + 1)
                dve.wait_ge(g_const, 4)
                if h >= 2:
                    dve.wait_ge(o_mm, h - 1)
                ps = PA[:, 0:2].rearrange("p a (b t) -> p (a b) t", t=P)
                for half in range(2):
                    rows = slice(half * CHUNK, (half + 1) * CHUNK)
                    last = dve.tensor_copy(SC[rows, h % 2, :, rows], ps[rows, :, rows])
                last.then_inc(sc_cp, 1)

            def gla_norm(h):
                O = MIXED[h]
                dve.wait_ge(o_ss, h + 1)
                if h:
                    dve.wait_ge(g_out, h)
                chain(dve.tensor_scalar(GT, one(PA[:, 2:4]), 1.0 / DV, EPS, ALU.mult, ALU.add))
                dve.reciprocal(GT, GT).then_inc(o_rr, 1)
                dve.wait_ge(g_silu, GLA_HEADS)
                chain(dve.tensor_tensor(O, O, WK[:, U_G + h], ALU.mult))
                dve.wait_ge(o_rs, h + 1)
                dve.scalar_tensor_tensor(O, O, vec(V_GN), GT, ALU.mult, ALU.mult).then_inc(g_out, 1)

            for u in range(U_OUT):
                T, A = WK[:, TMP], WK[:, TMP + 1]
                c, part = (u - U_CONV) // 3, (u - U_CONV) % 3
                if u < U_CONV:
                    scaled(Unit(u), WK[:, u])
                elif part == 0:
                    if c:
                        dve.wait_ge(conv_out, c)
                    scaled(Unit(u), T)
                elif part == 1:
                    O = MIXED[4 + c]
                    dve.wait_ge(evac, u)
                    dve.wait_ge(mm_done, u + 1)
                    dve.tensor_tensor(T, PD[:, u % 2], T, ALU.mult).then_inc(evac, 1)
                    dve.wait_ge(evac, u + 1)
                    chain(dve.tensor_tensor(A, T, R[:], ALU.mult))
                    w = [vec(V_CW + 3 * c + t) for t in range(3)]
                    chain(dve.tensor_scalar(O, A, w[2], None, ALU.mult))
                    chain(dve.scalar_tensor_tensor(O[:, 1:S], A[:, 0:S - 1], w[1], O[:, 1:S], ALU.mult, ALU.add))
                    chain(dve.scalar_tensor_tensor(O[:, 2:S], A[:, 0:S - 2], w[0], O[:, 2:S], ALU.mult, ALU.add))
                else:
                    O = MIXED[4 + c]
                    scaled(Unit(u), T)
                    dve.wait_ge(evac, u + 1)
                    dve.tensor_tensor(O, T, O, ALU.mult).then_inc(conv_out, 1)
                if u == AT_Z:
                    gla_decays()
                if u in (AT_Z + 1, AT_Z + 2):
                    gla_gates(u - AT_Z)
                if u in AT_KV:
                    gla_states(AT_KV.index(u))
                if u in AT_SCORES:
                    gla_scores(AT_SCORES.index(u))
                if u in AT_NORM:
                    gla_norm(AT_NORM.index(u))
                for k in AT_SPLIT.get(u, ()):
                    dve.wait_ge(xh, 8 + k + 1)
                    dve.tensor_tensor(MIX_L[k], MIXED[k], MIX_H[k].bitcast(f32), ALU.subtract
                                      ).then_inc(x_ready, 1)

            def add_to_residual(u, k):
                dve.wait_ge(mm_done, u.count(1))
                dve.tensor_tensor(XR[:, k], PD[:, u.slot], XR[:, k], ALU.add).then_inc(evac, 1)

            for k in range(KT):
                dve.wait_ge(x_in[k], 32)
                add_to_residual(Unit(U_OUT + k), k)
                lo_part(k, XR[:, k], 16 + k + 1, vec(V_G2 + k))
                add_square(SQ_NORM2 + k, k == 0, WK[:, TMP + 2])
            mean_recip(2, 2, WK[:, TMP + 3], D)
            dve.wait_ge(rs, 2)

            dve.tensor_tensor(GG[:], vec(V_GF, KT), vec(V_H2, KT), ALU.mult).then_inc(gd, 1)
            dve.wait_ge(gd, GD_ALL + 1)

            for n, (first, tiles, down) in enumerate(FFN):
                with dve.Fori(0, tiles) as i:
                    u = Unit(first, i, 2)
                    scaled(u, WK[:, TMP])
                    scaled(u.plus(1), WK[:, TMP + 2])
                    dve.wait_ge(evac, u.count(2))
                    dve.wait_ge(s_t, i + (8 * n + 1))
                    dve.tensor_tensor(WK[:, TMP + 3], WK[:, TMP + 1], WK[:, TMP + 2], ALU.mult).then_inc(m_t, 1)
                    dve.wait_ge(mh, i + (8 * n + 1))
                    dve.tensor_tensor(ML[:, i], WK[:, TMP + 3], MH[:, i].bitcast(f32), ALU.subtract
                                      ).then_inc(m_ready, 1)
                for k in range(KT):
                    add_to_residual(Unit(down + k), k)
                    if n == 2:
                        lo_part(k, XR[:, k], 24 + k + 1, GG[:, k:k + 1])
                        for t in range(2):
                            m = SQ_F + 2 * k + t
                            dve.wait_ge(sq, m + 1)
                            dst = WK[:, TMP + 2 + t]
                            if k == 0:
                                dve.tensor_copy(dst, WK[:, TMP + t]).then_inc(acc, 1)
                            else:
                                dve.wait_ge(acc, m - 1)
                                dve.tensor_tensor(dst, dst, WK[:, TMP + t], ALU.add).then_inc(acc, 1)

            U_, V_ = WK[:, TMP + 3], WK[:, 8]
            dve.wait_ge(ss, 4)
            mean_recip(3, 3, U_, D)
            dve.wait_ge(rr, 3)
            chain(dve.scalar_tensor_tensor(V_, one(PA[:, 2:4]), 1.0 / D, U_, ALU.mult, ALU.mult))
            chain(dve.tensor_scalar(V_, V_, EPS, None, ALU.add))
            chain(dve.reciprocal(V_, V_))
            dve.tensor_tensor(V_, V_, U_, ALU.mult).then_inc(rr, 1)
            dve.wait_ge(rs, 4)
            for k in range(KT):
                if k >= 2:
                    dve.wait_ge(av_g, k - 1)
                scaled(Unit(U_AV + k), WK[:, 12 + k % 2])
                add_square(SQ_V + k, k == 0, WK[:, TMP + 2])
                dve.scalar_tensor_tensor(XR[:, k], XR[:, k], vec(V_GF + k), WK[:, 9], ALU.mult, ALU.mult
                                         ).then_inc(xr_scaled, 1)

            def keep(u, first=False):
                if not first:
                    dve.wait_ge(sp_t[u.slot ^ 1], (u.plus(-U_QKV)).turn(16, 0))
                scaled(u, WK[:, 12 + (u.slot ^ 1)])

            for s in range(2):
                dve.wait_ge(av_g, KT)
                keep(Unit(U_QKV + s), True)
            RV = WK[:, TMP + 3]
            mean_recip(5, 5, RV, D)
            for k in range(4):
                keep(Unit(U_QKV + 2 + k))
            dve.wait_ge(rs, 5)
            for g in range(KT):
                dve.scalar_tensor_tensor(WK[:, g], WK[:, g], vec(V_GV + g), RV, ALU.mult, ALU.mult
                                         ).then_inc(avn, 1)
            for g in range(KT):
                keep(Unit(U_QKV + 6 + g))
                dve.wait_ge(mix_mm, g + 1)
                dve.tensor_tensor(WK[:, g].rearrange("p (b t) -> p b t", t=P),
                                  PA[:, 2:4].rearrange("p a (b t) -> p (a b) t", t=P),
                                  WK[:, 11, g * P:(g + 1) * P].unsqueeze(1).to_broadcast([P, NBLK, P]),
                                  ALU.add).then_inc(mixed, 1)
            with dve.Fori(0, (18 - KT) // 2) as i:
                for s in range(2):
                    keep(Unit(U_QKV + 6 + KT + s, i, 2))
            def head_bias(pair, h):
                dve.scalar_tensor_tensor(BH[:], DIST[:], VEC[:, bass.ds(pair.index(2, V_SL + h), 1)],
                                         LOGM[:], ALU.mult, ALU.add).then_inc(bias, 1)

            def head_q(pair, h):
                dve.wait_ge(q_hi, pair.count(2, h + 1))
                dve.scalar_tensor_tensor(QS[DH:P], Q2[DH:P], DH ** -0.5, QS[DH:P].bitcast(f32),
                                         ALU.mult, ALU.subtract).then_inc(q_lo, 1)

            def head_k(pair, h):
                dve.wait_ge(k_hi, pair.count(2, h + 1))
                dve.tensor_tensor(KL[:], K2[:], KH[:].bitcast(f32), ALU.subtract).then_inc(k_lo, 1)

            for s in range(2):
                dve.wait_ge(sp_t[s], 16 * 12)
            for k in range(KT):
                if k >= 2:
                    dve.wait_ge(au_g, k - 1)
                scaled(Unit(U_AU + k), WK[:, 12 + k % 2])
                dve.wait_ge(au_g, k + 1)
                dve.wait_ge(mixed, KT)
                dve.tensor_tensor(WK[:, k], WK[:, k], WK[:, 14 + k % 2], ALU.mult).then_inc(mx_upd, 1)
                if k == 4:
                    dve.wait_ge(tab_in, 64)
                    head_bias(Pair(0), 0)
                    head_q(Pair(0), 0)
                    head_k(Pair(0), 0)

            def biased(pair, m, n):
                i, c0, w = chunks_of(m)[n]
                base, sb = steps_before(m), m % 2
                b, c = i - 4 * sb, c0 // HALF
                bank = 0 if sb and n % 2 else 2
                if n == 0 and sb == 0:
                    dve.wait_ge(bias, pair.count(2, m // 2 + 1))
                    dve.sem_inc(turns, 1)
                if c:
                    dve.wait_ge(ttr, pair.count(24, base + n))
                dve.wait_ge(s_ready, pair.count(24, base + n + 1))
                dve.sem_inc(turns, 1)
                u0 = S - P - i * P + c0
                dve.tensor_tensor_reduce(
                    out=PBS[sb][:, b, c0:c0 + w], in0=PA[:, bank, 0:w], in1=BH[:, u0:u0 + w],
                    scale=-1.0, scalar=(STAT[:, 0, b:b + 1] if c else 3.0e38), op0=ALU.add, op1=ALU.min,
                    accum_out=STAT[:, (1 if c == sb else 0), b:b + 1]).then_inc(ttr, 1)

            def normed(pair, m, b):
                sb = m % 2
                p = PBS[sb][:, b, 0:(4 * sb + b + 1) * P]
                n = pair.count(16, 4 * m + b + 1)
                dve.wait_ge(ex, n)
                dve.reciprocal(STAT[:, 3, b:b + 1], STAT[:, 2, b:b + 1]).then_inc(rl, 1)
                dve.wait_ge(rl, n)
                dve.tensor_scalar(p, p, STAT[:, 3, b:b + 1], None, ALU.mult).then_inc(pn, 1)

            def p_lo(pair, m, k):
                base, sb = steps_before(m), m % 2
                lo = max(0, k - 4 * sb) * P
                bank = k % 2 if sb else 1
                dve.wait_ge(ph, pair.count(24, base + k + 1))
                dve.tensor_tensor(PL[:, k % 2, lo:HALF], PA[:, bank, lo:HALF],
                                  PH[:, k % 2, lo:HALF].bitcast(f32), ALU.subtract).then_inc(pl, 1)

            def o_out(pair, m):
                h, sb = m // 2, m % 2
                dve.wait_ge(o_half, pair.count(4, m + 1))
                if m == 0:
                    dve.wait_ge(sp_x, pair.count(16, 16 * KT))
                dve.tensor_tensor(Y[h * DH:(h + 1) * DH, sb * HALF:(sb + 1) * HALF], PA[0:DH, 3],
                                  OT[0:DH], ALU.add).then_inc(yh, 1)

            def gate(pair, m):
                if m < 2:
                    T = (WK[:, 14], SBG[:])[m]
                    dve.wait_ge(g_act, pair.count(4, m + 1))
                    dve.scalar_tensor_tensor(T, T, 1.0, WK[:, 12 + pair.unit(m).slot], ALU.add, ALU.mult
                                             ).then_inc(gated, 1)

            def stage(pair, m, before=None, done=None, head=True):
                if m == 1 and not done:
                    dve.wait_ge(sp_mx, 16 * KT)
                for kind, n in steps(DVE_STEPS[m % 2], bool(before), bool(done), head, m < 2):
                    if kind == "r":
                        biased(pair, m, n)
                    elif kind == "n":
                        normed(pair, m, n)
                    elif kind == "l":
                        p_lo(*before, n)
                    elif kind == "O":
                        o_out(*done)
                    elif kind == "b":
                        head_bias(*after(pair, m))
                    elif kind == "q":
                        head_q(*after(pair, m))
                    elif kind == "k":
                        head_k(pair, m // 2)
                    elif kind == "z":
                        u = before[0].unit(before[1])
                        if before[1] >= 2:
                            dve.wait_ge(g_act, before[0].count(4, before[1] - 1))
                        scaled(u, WK[:, 12 + u.slot])
                    elif kind == "m":
                        gate(*before)
                    elif kind == "v" and m == 1:
                        dve.wait_ge(v_hi, pair.count(2, n + 1))
                        blk = VHL[:, :, 4 * n:4 * n + 4].rearrange("p h b d -> p b h d")
                        dve.tensor_tensor(blk[:, :, :, DH:P],
                                          PA[:, n].rearrange("p (b h d) -> p b h d", h=2, d=DH),
                                          blk[:, :, :, 0:DH].bitcast(f32), ALU.subtract).then_inc(v_lo, 1)

            all_stages(dve, stage)
            final = Pair(PAIRS - 1)
            for kind, k in steps(REST):
                if kind == "O":
                    o_out(final, 2)
                elif kind == "p":
                    p_lo(final, 3, k)
                else:
                    lo_part(k, XR[:, k % 3], 32 + k + 1, 0.5)
            dve.wait_ge(g_act, final.count(4, 2))
            scaled(final.unit(3), WK[:, 12 + final.unit(3).slot])
            o_out(final, 3)

            def loaded(n):
                dve.wait_ge(ld[n % 2], 16 * (n // 2 + 1))
                return WK[:, TMP + n % 2]

            for k in range(KT):
                n = LD_YB + 2 * k
                lo_part(k, WK[:, TMP + n % 2], 22 + k + 1, 0.5, H=MH, L=ML, made=mh, ready=m_ready)
                u = Unit(U_PA + k)
                dve.wait_ge(mm_done, u.c + 1)
                src = loaded(n + 1)
                dve.scalar_tensor_tensor(XR[:, k], src, 1.0, PD[:, u.slot], ALU.add, ALU.mult
                                         ).then_inc(evac, 1)
            for k in range(KT):
                u = Unit(U_PB + k)
                src = loaded(LD_GB + k)
                dve.wait_ge(mm_done, u.c + 1)
                T = WK[:, TMP + 2]
                dve.scalar_tensor_tensor(T, src, 1.0, PD[:, u.slot], ALU.add, ALU.mult).then_inc(evac, 1)
                dve.wait_ge(evac, u.c + 1)
                dve.tensor_tensor(XR[:, k], XR[:, k], T, ALU.add).then_inc(m1, 1)
                dve.wait_ge(m1, k + 1)
                lo_part(k, XR[:, k], 40 + k + 1, 0.5)
            for k in range(KT):
                u = Unit(U_WO + k)
                src = loaded(LD_X + k)
                dve.wait_ge(mm_done, u.c + 1)
                dve.tensor_tensor(XR[:, k], PD[:, u.slot], src, ALU.add).then_inc(evac, 1)
                n = SQ_END + k
                add_square(n, k == 0, WK[:, 0], WK[:, 2 + n % 2])
            mean_recip(6, 6, WK[:, 1], D)
            dve.wait_ge(rs, 6)
            for k in range(KT):
                dve.scalar_tensor_tensor(XR[:, k], XR[:, k], vec(V_FIN + k), R[:], ALU.mult, ALU.mult
                                         ).then_inc(fin, 1)


def kernel(**inputs):
    import concourse.bacc as bacc
    from concourse.bass_utils import run_bass_kernel_spmd

    f = {k: np.asarray(v) for k, v in inputs.items()}

    def columns(w):
        k, n = w.shape
        t = w.reshape(k // P, P, n // P, P).transpose(2, 1, 0, 3)
        if k < D:
            t = np.concatenate([t, np.zeros((n // P, P, (D - k) // P, P), w.dtype)], axis=2)
        return t.reshape(n // P, P, KT * P)

    w_in, w2 = f["w_in"][0], f["w_in_2"][0]
    edges = np.cumsum([0, 256, 256, 512, 512, RANK, 512, 512, 512])
    q, k, v, g, a, cb, cc, ch = (w_in[:, edges[i]:edges[i + 1]] for i in range(8))
    a = np.concatenate([a, np.zeros((D, P - RANK), a.dtype)], axis=1)
    conv = np.stack([columns(cc), columns(ch), columns(cb)], axis=1).reshape(12, P, D)
    parts = [columns(a), columns(q), columns(k), columns(v), columns(g), conv, columns(f["w_out"][0])]
    gate, up, down = columns(f["w_ffn_gate"][0]), columns(f["w_ffn_up"][0]), f["w_ffn_down"][0]
    tile = 0
    for _, tiles, _ in FFN:
        parts.append(np.stack([gate[tile:tile + tiles], up[tile:tile + tiles]], axis=1).reshape(2 * tiles, P, D))
        parts.append(columns(down[tile * P:(tile + tiles) * P]))
        tile += tiles
    au, av, agate, q, k, v, bgate, ga, gb = (columns(w2[:, i * D:(i + 1) * D]) for i in range(9))
    parts += [av, np.stack([q, k, v], axis=1).reshape(24, P, D), au,
              np.stack([agate, bgate, ga, gb], axis=1).reshape(32, P, D),
              columns(f["w_proj_a_2"][0]), columns(f["w_proj_b_2"][0]), columns(f["w_out_2"][0])]
    weights = np.concatenate(parts)
    assert weights.shape[0] == UNITS

    def tall(x):
        return x.reshape(-1, P).T

    slopes = -np.exp2(-8.0 * np.arange(1, HEADS + 1) / HEADS).astype(np.float32)
    cw = f["conv_w"][0].reshape(3, 4, P).transpose(2, 1, 0).reshape(P, 12)
    vecs = np.concatenate([tall(f["norm1_g"]), tall(f["b_gate"]), tall(f["gla_norm_g"]), cw, tall(f["norm2_g"]),
                           tall(f["norm_f_g"]), tall(f["g_norm_2"]), tall(f["g_v_2"]), tall(f["g_final_2"]),
                           np.broadcast_to(slopes, (P, HEADS))], axis=1)
    d = np.arange(P)[:, None] + (S - P) - np.arange(S)[None, :]
    count = sum(((d % r == 0) & (d <= w)).astype(np.float64) for w, r in ((128, 1), (512, 4), (2048, 16)))
    count = count * (d >= 0)
    logm = np.where(count > 0, np.log(np.maximum(count, 1)), -1e30).astype(np.float32)
    dist = np.where(count > 0, d, 0).astype(np.float32)

    arrays = {
        "xT": f["x"][0].T.reshape(KT, P, S), "weights": weights, "vecs": vecs, "gate_up": f["w_gate_up"][0],
        "mix_w": f["w_s_2"][0].transpose(2, 0, 1).reshape(P, D),
        "mix_b": np.broadcast_to(f["b_s_2"].reshape(1, D), (P, D)),
        "dist": dist, "logm": logm, "ident": np.eye(P, dtype=np.float32),
    }
    arrays = {k: np.ascontiguousarray(v) for k, v in arrays.items()}
    nc = bacc.Bacc("TRN2", target_bir_lowering=False, num_devices=1)
    aps = [nc.dram_tensor(k, v.shape, mybir.dt.from_np(v.dtype), kind="ExternalInput").ap()
           for k, v in arrays.items()]
    out = nc.dram_tensor("out", (KT, P, S), mybir.dt.float32, kind="ExternalOutput").ap()
    two_blocks(nc, *aps, out)
    r = run_bass_kernel_spmd(nc, [arrays], core_ids=[0])
    return np.ascontiguousarray(np.asarray(r.results[0]["out"]).reshape(D, S).T).reshape(1, S, D)
```

```python
import concourse.bass as bass
from concourse import mybir
from contextlib import ExitStack
import numpy as np

P = 128
D = 1024
S = 1024
KT = D // P
HALF = 512
EPS = 1e-6
GLA_HEADS, DK, DV, CHUNK, RANK = 4, 64, 128, 64, 16
NCH = S // CHUNK
NBLK = S // P
D_FF = 2816
HEADS, DH = 16, 64
PAIRS = HEADS // 2

U_A = 0
U_Q, U_K, U_V, U_G = 1, 3, 5, 9
U_CONV = 13
U_OUT = 25
FFN = [(33, 8, 49), (57, 8, 73), (81, 6, 93)]
U_AV = 101
U_QKV = 109
U_AU = 133
U_ATT = 141
U_PA, U_PB, U_WO = 173, 181, 189
UNITS = 197

V_G1, V_BG, V_GN, V_CW, V_G2, V_GF, V_H2, V_GV, V_FIN, V_SL = 0, 8, 10, 11, 23, 31, 39, 47, 55, 63
VECS = V_SL + HEADS


class Unit:

    def __init__(self, c, reg=None, a=0):
        self.c, self.reg, self.a = c, reg, a

    def plus(self, n):
        return Unit(self.c + n, self.reg, self.a)

    @property
    def slot(self):
        return self.c % 2

    def count(self, n=0):
        return self.c + n if self.reg is None else self.reg * self.a + (self.c + n)

    def turn(self, scale, n):
        k = scale * (self.c // 2 + n)
        return k if self.reg is None else self.reg * (scale * self.a // 2) + k


class Pair:

    def __init__(self, off, reg=None):
        self.off, self.reg = off, reg

    def count(self, per, k):
        k += per * self.off
        return k if self.reg is None else self.reg * per + k

    def unit(self, m):
        c = U_ATT + 4 * self.off + m
        return Unit(c) if self.reg is None else Unit(c, self.reg, 4)

    def index(self, per=1, k=0):
        return self.count(per, k)


def after(pair, m):
    return (pair, 1) if m == 1 else (Pair(pair.off + 1, pair.reg), 0)


def steps_before(m):
    return 12 * (m // 2) + 4 * (m % 2)


def chunks_of(m):
    sb = m % 2
    return [(i, c, min(HALF, (i + 1) * P - c)) for i in range(4 * sb, 4 * sb + 4)
            for c in range(0, (i + 1) * P, HALF)]


PE_STEPS = [
    "t0/t1//o0 t2/s0/o1 t3/s1/o2 t4/s2/o3 t5/s3/o4 t6//o5 t7/o6/o7 v0 v1",
    "s0//s1/s2/t0/s3/s4/s5 o0 t1//s6/s7 o1 t2///o2 t3//o3",
]
PE_STEPS = [x.split("/") for x in PE_STEPS]
ACT_STEPS = [
    "O p0 k p1 w p2 p3 e0 p4 e1 a p5 e2 p6 e3 d p7",
    "v0 v1 O e0 w p0 e1 p1 a e2 p2 y e3 p3 q d",
]
DVE_STEPS = [
    "O l0 k l1 z l2 r0 l3 r1 n0 l4 r2 n1 l5 r3 n2 l6 m n3 l7",
    "v0 r0 v1 O r1 r2 z n0 l0 r3 r4 n1 l1 r5 m r6 r7 l2 n2 b l3 n3 q",
]
PE_REST = "t0 t1//o0 t2//o1 t3//o2 t4//o3 t5//o4 t6//o5 t7//o6//o7//".split("/")
REST = "X0 O p0 X1 p1 w z X2 p2 X3 p3 X4 p4 X5 p5 X6 p6 X7 p7"


def steps(text, before=True, done=True, head=True, first=True):
    for x in text.split():
        kind, n = x[0], int(x[1:] or 0)
        if not ((kind in "topwlzamd" and not before) or (kind in "Oy" and not done)
                or (kind in "bqk" and not head) or (kind == "v" and not first)):
            yield kind, n


AT_Z = 3
AT_TURN = {6: (0, 1, 2, 3), 7: (4, 5, 6, 7), 8: (8, 9), 9: (10, 11)}
AT_KV = (10, 11)
AT_SCORES = (12, 14, 16, 18)
AT_O = (13, 15, 17, 19)
AT_NORM = (14, 16, 18, 20)
AT_SILU = 12
AT_SPLIT = {21: (0, 1, 2), 22: (3, 4), 23: (5, 6), 24: (7,)}
GD_ALL = 14

ENDED_BY_DVE, ENDED_BY_ACT = (0, 1, 2, 4, 5, 7), (3, 6)


def two_blocks(nc, xT, weights, vecs, gate_up, mix_w, mix_b, dist, logm, ident, out):
    f32, f32r = mybir.dt.float32, mybir.dt.float32r
    ALU = mybir.AluOpType
    ACT = mybir.ActivationFunctionType

    ctx = ExitStack()
    with ctx:
        at = {}
        top = (nc.sbuf_base + 63) // 64 * 64

        def place(name, cols, dt=f32, offset=None, rows=P):
            nonlocal top
            shape = [rows] + (list(cols) if isinstance(cols, (list, tuple)) else [cols])
            size = 4 * int(np.prod(shape[1:]))
            if offset is None:
                offset, top = top, top + (size + 63) // 64 * 64
            at[name] = offset
            return nc.alloc_sbuf_tensor_at(name, shape, dt, offset=offset)

        XH = place("x_hi", [KT, S], f32r)
        XL = place("x_lo", [KT, S], f32r)
        WR = place("w_raw", [2, KT, P])
        WH = place("w_hi", [2, KT, P], f32r)
        WL = place("w_lo", [2, KT, P], f32r)
        VEC = place("vectors", VECS)
        IDN = place("identity", P)
        ONES = place("ones", P)
        R = place("rstd", S)
        RT = place("rstd_tokens", [4, NBLK])
        GG = place("gain_product", KT)
        DEC = place("chunk_decay", [2, NCH])
        STAT = place("softmax_stats", [4, 4])
        WGU = place("gate_up_w", 2 * P, rows=RANK)
        XR = place("residual", [KT, S])
        WK = place("work", [20, S])
        wk, xr = at["work"], at["residual"]
        TMP = 16
        MH = place("m_hi", [8, S], f32r, wk)
        ML = place("m_lo", [8, S], f32r, wk + 8 * 4 * S)
        VTOK = place("gla_v_tokens", [NBLK, GLA_HEADS * DV], f32, xr)
        KS = place("gla_k_s", [2, S], f32, xr + 4 * 4096)
        SC = place("gla_scores", [2, NBLK, P], f32, xr + 4 * 4096)
        KTOK = place("gla_k_tokens", [NBLK, GLA_HEADS * DK], f32, xr + 6 * 4096)
        ST = place("gla_states", [2, NCH, DV], f32, wk + U_V * 4096)
        ZE, ZZ, ZB = ([WK[:, c + j] for j in range(2)] for c in (13, 15, 17))
        RESET, GSQ, GT = WK[:, 19], WK[:, 18], WK[:, 19]
        MIXED = [XR[:, 6], XR[:, 7], WK[:, U_V], WK[:, U_V + 1], WK[:, 13], WK[:, 14], WK[:, 15], WK[:, 19]]
        Q2 = place("att_q", S, f32, xr)
        K2 = place("att_k", S, f32, xr + 4096)
        VT = place("att_v", S, f32, xr + 8192)
        QS = place("att_q_split", S, f32r, xr + 12288)
        KH = place("att_k_hi", S, f32r, xr + 16384)
        KL = place("att_k_lo", S, f32r, xr + 20480)
        VHL = place("att_v_split", [2, NBLK, P], f32r, xr + 24576)
        PB1 = place("att_p_late", [4, S], f32, wk)
        PB0 = place("att_p_early", [4, HALF], f32, wk + 10 * 4096)
        PH = place("att_p_hi", [2, HALF], f32r, wk + 4 * 4096)
        PL = place("att_p_lo", [2, HALF], f32r, wk + 5 * 4096)
        Y = place("att_y", S, f32, wk + 6 * 4096)
        MXL = place("att_mixed", S, f32, wk + 7 * 4096)
        DIST = place("distances", S, f32, wk + 8 * 4096)
        LOGM = place("log_counts", S, f32, wk + 9 * 4096)
        OT = place("att_o_half", HALF, f32, wk + 15 * 4096)
        BH = place("att_bias", S, f32, wk + TMP * 4096)
        SBG = place("att_b_gate", S, f32, wk + 17 * 4096)
        GAB = place("att_gates", [2, S], f32, wk + 18 * 4096)
        WKR = place("work_split", [20, S], f32r, wk)
        MIX_H = [WKR[:, t] for t in (9, 10, 11, 12, 2, 3, 4, 7)]
        MIX_L = [WKR[:, t] for t in (0, 1, U_V, U_V + 1, 13, 14, 15, 19)]
        PBS = [PB0, PB1]

        def psum(name, shape):
            return ctx.enter_context(nc.psum_tensor(name, shape, f32))

        PD = psum("dense", [P, 2, S])
        PA = psum("aux", [P, 4, HALF])

        def dram(name, n):
            return nc.dram_tensor(name, (n, P, S), f32, kind="Internal").ap()

        d_x, d_qkv, d_mix = dram("kept_x", KT), dram("kept_qkv", 3 * KT), dram("kept_mixed", KT)
        d_ya, d_yb = dram("kept_ya", KT), dram("kept_yb", KT)
        d_ga, d_gb = dram("kept_ga", KT), dram("kept_gb", KT)

        def sem(name):
            return ctx.enter_context(nc.semaphore(name))

        x_in = [sem(f"x_in{k}") for k in range(KT)]
        vec_in, tab_in, gat_in = sem("vec_in"), sem("tab_in"), sem("gat_in")
        consts = sem("consts")
        w_raw = [sem("w_raw0"), sem("w_raw1")]
        w_hi, w_lo, mm_done = sem("w_hi"), sem("w_lo"), sem("mm_done")
        evac, last_half = sem("evac"), sem("last_half")
        x_hi_made, x_ready, m_hi_made = sem("x_hi_made"), sem("x_ready"), sem("m_hi_made")
        m_ready = sem("m_ready")
        squared, squares_added, sums_done = sem("squared"), sem("squares_added"), sem("sums_done")
        recip_done, root_done = sem("recip_done"), sem("root_done")
        diagonal_done, spread_done, rstd_there = sem("diagonal_done"), sem("spread_done"), sem("rstd_there")
        a_there, dve_step, conv_out = sem("a_there"), sem("dve_step"), sem("conv_out")
        silu_done, m_made = sem("silu_done"), sem("m_made")
        z_mm, z_abs, z_add = sem("z_mm"), sem("z_abs"), sem("z_add")
        gla_act, gla_dve, gla_turned = sem("gla_act"), sem("gla_dve"), sem("gla_turned")
        gla_turned_out = sem("gla_turned_out")
        gla_consts, kv_done, state_done = sem("gla_consts"), sem("kv_done"), sem("state_done")
        scores_done, scores_out, scores_masked = sem("scores_done"), sem("scores_out"), sem("scores_masked")
        o_done, o_out_done, o_squared = sem("o_done"), sem("o_out_done"), sem("o_squared")
        o_summed, o_mean_done, o_recip = sem("o_summed"), sem("o_mean_done"), sem("o_recip")
        o_rstd, g_silu, o_gated = sem("o_rstd"), sem("g_silu"), sem("o_gated")
        av_gelu, av_normed, av_turned = sem("av_gelu"), sem("av_normed"), sem("av_turned")
        av_turned_out = sem("av_turned_out")
        mix_w_masked, mix_done, mixed = sem("mix_w_masked"), sem("mix_done"), sem("mixed")
        au_gelu, mixed_gated, xr_scaled = sem("au_gelu"), sem("mixed_gated"), sem("xr_scaled")
        stored_x, stored_mixed, stored_ya = sem("stored_x"), sem("stored_mixed"), sem("stored_ya")
        stored_ring = [sem("stored_ring0"), sem("stored_ring1")]
        q_in, k_in, v_in = sem("q_in"), sem("k_in"), sem("v_in")
        mixed_in, q_hi, k_hi = sem("mixed_in"), sem("q_hi"), sem("k_hi")
        q_lo, k_lo, bias = sem("q_lo"), sem("k_lo"), sem("bias")
        v_turned, v_hi, v_lo = sem("v_turned"), sem("v_hi"), sem("v_lo")
        att_scores, biased_done, p_exp = sem("att_scores"), sem("biased_done"), sem("p_exp")
        sum_recip, p_normed = sem("sum_recip"), sem("p_normed")
        p_turned, ph_made, pl_made = sem("p_turned"), sem("ph_made"), sem("pl_made")
        pv_done, o_half, y_half = sem("pv_done"), sem("o_half"), sem("y_half")
        gate_act, gated, ya_gated = sem("gate_act"), sem("gated"), sem("ya_gated")
        yb_gated = sem("yb_gated")
        ring_in = [sem("ring_in0"), sem("ring_in1")]
        ya_in = [sem(f"ya_in{t}") for t in range(3)]
        merged, fin_dve, fin_pool = sem("merged"), sem("fin_dve"), sem("fin_pool")
        fin_act, outs = sem("fin_act"), sem("outs")
        turns = sem("turns")

        def vec(c, n=1):
            return VEC[:, c:c + n]

        def one(t):
            return t.rearrange("p a n -> p (a n)")

        SQ_NORM2, SQ_F, SQ_V, SQ_END = 8, 16, 32, 40
        LD_GA, LD_GB, LD_X = 0, 16, 24

        block = ctx.enter_context(nc.Block())

        def all_stages(engine, stage):
            first, final = Pair(0), Pair(PAIRS - 1)
            stage(first, 0, head=False)
            stage(first, 1, before=(first, 0))
            with engine.Fori(0, PAIRS - 1) as j:
                now, following = Pair(0, j), Pair(1, j)
                stage(now, 2, before=(now, 1), done=(now, 0))
                stage(now, 3, before=(now, 2), done=(now, 1))
                stage(following, 0, before=(now, 3), done=(now, 2))
                stage(following, 1, before=(following, 0), done=(now, 3))
            stage(final, 2, before=(final, 1), done=(final, 0))
            stage(final, 3, before=(final, 2), done=(final, 1), head=False)

        @block.sync
        def _(sp):
            def load(u):
                if u.c >= 2:
                    sp.wait_ge(w_lo, u.count(-1))
                sp.dma_start(WR[:, u.slot].rearrange("p k c -> p (k c)"),
                             weights[u.count()]).then_inc(w_raw[u.slot], 16)

            def loads(c, n):
                if n >= 2:
                    with sp.Fori(0, n // 2) as i:
                        load(Unit(c, i, 2))
                        load(Unit(c + 1, i, 2))
                if n % 2:
                    load(Unit(c + n - 1))

            sp.dma_start(VEC[:], vecs).then_inc(vec_in, 16)
            load(Unit(0))
            for k in range(KT):
                sp.dma_start(XR[:, k], xT[k]).then_inc(x_in[k], 16)
                if k == 3:
                    load(Unit(1))
            sp.dma_start(WGU[:], gate_up).then_inc(tab_in, 16)
            sp.dma_start(IDN[:], ident).then_inc(tab_in, 16)
            loads(2, 22)
            sp.wait_ge(o_done, GLA_HEADS)
            for k in range(KT):
                if k == 6:
                    loads(24, 2)
                if k >= 6:
                    sp.wait_ge(x_ready, 8 + k - 6 + 1)
                sp.dma_start(XR[:, k], xT[k]).then_inc(x_in[k], 16)
            loads(26, U_AV + 4 - 26)
            sp.dma_start(WK[:, 10], mix_w).then_inc(gat_in, 16)
            sp.dma_start(WK[:, 11], mix_b).then_inc(gat_in, 16)
            loads(U_AV + 4, U_AU + 2 - U_AV - 4)

            def load_qk(j, h, first):
                if not first:
                    sp.wait_ge(q_lo, 2 * j + h)
                    sp.wait_ge(k_lo, 2 * j + h)
                for t, sm, c in ((Q2, q_in, 0), (K2, k_in, 1)):
                    src = d_qkv[3 * j + c, h * DH:(h + 1) * DH, :]
                    sp.dma_start(t[0:DH], src).then_inc(sm, 16)
                    sp.dma_start(t[DH:P], src).then_inc(sm, 16)

            def load_v(j, first):
                if not first:
                    sp.wait_ge(v_turned, 2 * j)
                sp.dma_start(VT[:], d_qkv[3 * j + 2]).then_inc(v_in, 16)

            def load_mixed(j):
                sp.wait_ge(stored_ya, 16 * j + 16)
                sp.dma_start(MXL[:], d_mix[j + 1]).then_inc(mixed_in, 16)

            sp.wait_ge(mix_done, KT)
            sp.dma_start(DIST[:], dist).then_inc(tab_in, 16)
            sp.dma_start(LOGM[:], logm).then_inc(tab_in, 16)
            sp.wait_ge(stored_x, 16 * KT)
            for t in range(2):
                sp.wait_ge(stored_ring[t], 16 * 12)
            load_qk(0, 0, True)
            load_v(0, True)
            loads(U_AU + 2, 8)
            sp.wait_ge(stored_mixed, 16 * KT)
            sp.dma_start(MXL[:], d_mix[0]).then_inc(mixed_in, 16)
            with sp.Fori(0, PAIRS - 1) as j:
                load_qk(j, 1, False)
                load(Unit(U_ATT + 2, j, 4))
                load(Unit(U_ATT + 3, j, 4))
                load_v(j + 1, False)
                load_mixed(j)
                load_qk(j + 1, 0, False)
                load(Unit(U_ATT + 4, j, 4))
                load(Unit(U_ATT + 5, j, 4))
            load_qk(PAIRS - 1, 1, False)
            for m in range(4):
                load(Unit(U_ATT + 4 * (PAIRS - 1) + 2 + m))

            sp.wait_ge(stored_ya, 16 * KT)
            sp.wait_ge(q_lo, HEADS)
            sp.wait_ge(k_lo, HEADS)
            sp.wait_ge(v_turned, 2 * PAIRS)
            for k in range(KT):
                if k >= 3:
                    sp.wait_ge(x_ready, 32 + k - 3 + 1)
                sp.dma_start(XR[:, k % 3], d_ya[k]).then_inc(ya_in[k % 3], 16)

            n = 0
            used = []

            def fetch(src, by, count):
                nonlocal n
                if n >= 2:
                    sp.wait_ge(*used[n - 2])
                used.append((by, count))
                sp.dma_start(WK[:, TMP + n % 2], src).then_inc(ring_in[n % 2], 16)
                n += 1

            load(Unit(U_PA + 2))
            sp.wait_ge(stored_ring[0], 16 * (12 + KT))
            for k in range(KT):
                fetch(d_ga[k], evac, U_PA + k + 1)
                if k == 0:
                    sp.wait_ge(stored_x, 16 * 2 * KT)
                fetch(d_yb[k], m_ready, 22 + k + 1)
                load(Unit(U_PA + k + 3))
            sp.wait_ge(stored_ring[1], 16 * (12 + KT))
            for k in range(KT):
                load(Unit(U_PB + k + 3))
                fetch(d_gb[k], evac, U_PB + k + 1)
            for k in range(KT):
                if U_WO + k + 3 < UNITS:
                    load(Unit(U_WO + k + 3))
                fetch(d_x[k], evac, U_WO + k + 1)
            for t in range(2):
                tok = slice(t * HALF, (t + 1) * HALF)
                for k in range(KT):
                    if k in ENDED_BY_ACT:
                        sp.wait_ge(fin_act, len(ENDED_BY_ACT) * t + ENDED_BY_ACT.index(k) + 1)
                    else:
                        sp.wait_ge(fin_dve, ENDED_BY_DVE.index(k) + len(ENDED_BY_DVE) * t + 1)
                    sp.dma_start(out[k][:, tok], XR[:, k, tok]).then_inc(outs, 16)
            sp.wait_ge(outs, 16 * 2 * KT)

        @block.gpsimd
        def _(pool):
            def split(u):
                pool.wait_ge(w_hi, u.count(1))
                pool.tensor_tensor(WL[:, u.slot], WR[:, u.slot], WH[:, u.slot].bitcast(f32),
                                   ALU.subtract).then_inc(w_lo, 1)

            def splits(c, n):
                if n >= 2:
                    with pool.Fori(0, n // 2) as i:
                        split(Unit(c, i, 2))
                        split(Unit(c + 1, i, 2))
                if n % 2:
                    split(Unit(c + n - 1))

            pool.memset(ONES[:], 1.0).then_inc(consts, 1)
            for u in range(U_OUT + 2):
                split(Unit(u))
                if u == 3:
                    pool.wait_ge(rstd_there, 1)
                    pool.memset(RESET, 1.0).then_inc(gla_consts, 1)
                    pool.wait_ge(gla_consts, 1)
                    pool.memset(RESET.rearrange("p (c t) -> p c t", t=CHUNK)[:, :, 0:1], 0.0).then_inc(gla_consts, 1)
                if u == 10:
                    pool.wait_ge(gla_turned, 4)
                    for s in range(2):
                        pool.memset(SC[:, s], 0.0).then_inc(gla_consts, 1)
                if u - 2 in AT_SCORES:
                    h = AT_SCORES.index(u - 2)
                    pool.wait_ge(scores_out, h + 1)
                    pool.affine_select(out=SC[:, h % 2], in_=SC[:, h % 2], compare_op=ALU.is_ge, fill=0.0,
                                       base=0, pattern=[[0, NBLK], [1, P]], channel_multiplier=-1
                                       ).then_inc(scores_masked, 1)
            splits(U_OUT + 2, U_AV + 4 - U_OUT - 2)
            pool.wait_ge(gat_in, 32)
            w3 = WK[:, 10].rearrange("p (g t) -> p g t", t=P)
            pool.affine_select(out=w3, in_=w3, compare_op=ALU.is_ge, fill=0.0, base=0,
                               pattern=[[0, KT], [1, P]], channel_multiplier=-1).then_inc(mix_w_masked, 1)
            splits(U_AV + 4, U_ATT + 2 - U_AV - 4)

            def stage(pair, m, before=None, done=None, head=True):
                if m == 1 and done:
                    gate_y(done[0])
                if before:
                    split(pair.unit(m).plus(1))
                if m == 1:
                    pool.wait_ge(gated, pair.count(2, 1))
                    pool.wait_ge(mixed_in, pair.count(16, 16))
                    pool.tensor_tensor(MXL[:], MXL[:], WK[:, 14], ALU.mult).then_inc(ya_gated, 1)

            def gate_y(pair):
                pool.wait_ge(y_half, pair.count(4, 4))
                pool.wait_ge(gated, pair.count(2, 2))
                pool.tensor_tensor(Y[:], Y[:], SBG[:], ALU.mult).then_inc(yb_gated, 1)

            all_stages(pool, stage)
            split(Unit(U_PA + 1))
            gate_y(Pair(PAIRS - 1))
            splits(U_PA + 2, UNITS - U_PA - 2)
            for t in range(2):
                pool.wait_ge(rstd_there, 6 + t)
                for k in ENDED_BY_ACT:
                    dst = XR[:, k, t * HALF:(t + 1) * HALF]
                    pool.tensor_tensor(dst, dst, R[:, t * HALF:(t + 1) * HALF], ALU.mult).then_inc(fin_pool, 1)

        @block.tensor
        def _(pe):
            def unit(u, H=XH, L=XL, nk=KT, ready=None, between=None, half=None):
                pe.wait_ge(w_hi, u.count(1))
                pe.wait_ge(w_lo, u.count(1))
                if u.c >= 2:
                    pe.wait_ge(evac, u.count(-1))
                order = [(t, k) for t in range(2) for k in range(nk)]
                if ready:
                    order = [(t, k) for k in range(nk) for t in range(2)]
                for g, (t, k) in enumerate(order):
                    dst = PD[:, u.slot, t * HALF:(t + 1) * HALF]
                    if ready and t == 0:
                        pe.wait_ge(ready[0], ready[1] + k + 1)
                    tok = slice(t * HALF, (t + 1) * HALF)
                    hi, lo = (H[k][:, tok], L[k][:, tok]) if isinstance(H, list) else (H[:, k, tok], L[:, k, tok])
                    pe.matmul(dst, WH[:, u.slot, k], hi, start=(k == 0), stop=False)
                    pe.matmul(dst, WH[:, u.slot, k], lo, start=False, stop=False)
                    last = pe.matmul(dst, WL[:, u.slot, k], hi, start=False, stop=(k == nk - 1))
                    if t == 1 and k == nk - 1:
                        last.then_inc(mm_done, 1)
                    elif half is not None and k == nk - 1:
                        last.then_inc(half, 1)
                    if between:
                        between(g)

            def units(c, n, **kw):
                if n >= 2:
                    with pe.Fori(0, n // 2) as i:
                        unit(Unit(c, i, 2), **kw)
                        unit(Unit(c + 1, i, 2), **kw)
                if n % 2:
                    unit(Unit(c + n - 1), **kw)

            def token_sums(count, src, bank=0, blocks=range(NBLK)):
                pe.wait_ge(squares_added, count)
                for b in blocks:
                    last = pe.matmul(PA[:, bank, b:b + 1], src[:, b * P:(b + 1) * P], ONES[:, 0:1],
                                     start=True, stop=True)
                last.then_inc(sums_done, 1)

            def spread(n, diagonals, bank=0, halves=range(2)):
                pe.wait_ge(diagonal_done, n)
                for t in halves:
                    last = pe.matmul(PA[:, bank + t], ONES[:], diagonals[:, t * HALF:(t + 1) * HALF],
                                     start=True, stop=True)
                last.then_inc(spread_done, 1)

            pe.wait_ge(consts, 1)
            unit(Unit(0), ready=(x_ready, 0))

            def gate_logits():
                pe.wait_ge(tab_in, 32)
                pe.wait_ge(a_there, 1)
                for j in range(2):
                    for t in range(2):
                        last = pe.matmul(PA[:, 2 * j + t], WGU[:, j * P:(j + 1) * P],
                                         WK[0:RANK, 0, t * HALF:(t + 1) * HALF], start=True, stop=True)
                    last.then_inc(z_mm, 1)

            def turn(n):
                if n < 4:
                    src = KS[:, n // 2]
                    pe.wait_ge(gla_dve, 11 + 2 * (n // 2))
                else:
                    src = WK[:, U_V + n // 2 - 2]
                    pe.wait_ge(evac, U_V + n // 2 - 2 + 1)
                if n >= 4:
                    pe.wait_ge(gla_turned_out, n - 3)
                for b in range(4):
                    blk = 4 * (n % 2) + b
                    last = pe.transpose(PA[:, n % 4, b * P:(b + 1) * P], src[:, blk * P:(blk + 1) * P], IDN[:])
                last.then_inc(gla_turned, 1)

            def chunk_products(j):
                pe.wait_ge(gla_turned_out, 12)
                if j:
                    pe.wait_ge(state_done, NCH - 1)
                for c in range(NCH):
                    half, blk, col = c % 2, c // 2, (c // 2) % 4 * DV
                    rows = slice(CHUNK * half, CHUNK * (half + 1))
                    for p in range(2):
                        h = 2 * j + p
                        last = pe.matmul(PA[p * DK:(p + 1) * DK, 2 * half + blk // 4, col:col + DV],
                                         KTOK[rows, blk, h * DK:(h + 1) * DK],
                                         VTOK[rows, blk, h * DV:(h + 1) * DV], start=True, stop=True)
                    if c % 8 == 7:
                        last.then_inc(kv_done, 1)

            def scores(h):
                rows = slice(h % 2 * DK, (h % 2 + 1) * DK)
                if h == 0:
                    pe.wait_ge(state_done, 2 * (NCH - 1))
                    pe.wait_ge(gla_dve, GD_ALL)
                else:
                    pe.wait_ge(scores_out, h)
                for b in range(NBLK):
                    tok = slice(b * P, (b + 1) * P)
                    last = pe.matmul(PA[:, b // 4, b % 4 * P:(b % 4 + 1) * P], WK[rows, U_K + h // 2, tok],
                                     WK[rows, U_Q + h // 2, tok], start=True, stop=True)
                last.then_inc(scores_done, 1)

            def outputs(h):
                rows = slice(h % 2 * DK, (h % 2 + 1) * DK)
                pe.wait_ge(scores_masked, h + 1)
                if h:
                    pe.wait_ge(o_mean_done, h)
                for b in range(NBLK):
                    bank, col = 2 + b // 4, b % 4 * P
                    pe.matmul(PA[:, bank, col:col + P], VTOK[:, b, h * DV:(h + 1) * DV], SC[:, h % 2, b],
                              start=True, stop=False)
                    for c in (2 * b, 2 * b + 1):
                        last = pe.matmul(PA[:, bank, col + c % 2 * CHUNK:col + (c % 2 + 1) * CHUNK],
                                         ST[rows, h // 2, c], WK[rows, U_Q + h // 2, c * CHUNK:(c + 1) * CHUNK],
                                         start=False, stop=(c % 2 == 1))
                last.then_inc(o_done, 1)

            def norm_sums(h):
                pe.wait_ge(o_squared, h + 1)
                for t in range(2):
                    last = pe.matmul(PA[:, 2 + t], ONES[:], GSQ[:, t * HALF:(t + 1) * HALF],
                                     start=True, stop=True)
                last.then_inc(o_summed, 1)

            def norm1(u, g):
                if (u, g) == (1, 15):
                    token_sums(8, WK[:, TMP + 2])
                if (u, g) == (2, 10):
                    spread(1, WK[:, TMP + 3])

            for u in range(1, U_OUT):
                unit(Unit(u), between=lambda g: norm1(u, g))
                if u == AT_Z:
                    gate_logits()
                for n in AT_TURN.get(u, ()):
                    turn(n)
                if u in AT_KV:
                    chunk_products(AT_KV.index(u))
                if u in AT_NORM:
                    norm_sums(AT_NORM.index(u))
                if u in AT_SCORES:
                    scores(AT_SCORES.index(u))
                if u in AT_O:
                    outputs(AT_O.index(u))

            def norm2(g):
                if g == 8:
                    token_sums(16, WK[:, TMP + 2])
                if g == 15:
                    spread(2, WK[:, TMP + 3])

            unit(Unit(U_OUT), H=MIX_H, L=MIX_L, ready=(x_ready, 8))
            units(U_OUT + 1, 7, H=MIX_H, L=MIX_L)
            for n, (first, tiles, down) in enumerate(FFN):
                if n == 0:
                    unit(Unit(first), ready=(x_ready, 16), between=norm2)
                    unit(Unit(first + 1))
                    units(first + 2, 2 * tiles - 2)
                else:
                    units(first, 2 * tiles)
                unit(Unit(down), H=MH, L=ML, nk=tiles, ready=(m_ready, 8 * n))
                units(down + 1, 7, H=MH, L=ML, nk=tiles)

            def both_norms(g):
                if g == 8:
                    token_sums(31, WK[:, TMP + 2])
                    token_sums(32, WK[:, TMP + 3], 2)
                if g == 15:
                    spread(3, WK[:, 8])
                    spread(4, WK[:, TMP + 3], 2)

            unit(Unit(U_AV), ready=(x_ready, 24), between=both_norms)
            units(U_AV + 1, 7)
            units(U_QKV, 2)
            token_sums(SQ_V + 8, WK[:, TMP + 2])
            unit(Unit(U_QKV + 2))
            spread(5, WK[:, 8])
            units(U_QKV + 3, 3)

            def gating_transposes(g):
                pe.wait_ge(av_normed, g + 1)
                if g:
                    pe.wait_ge(av_turned_out, 2 * g)
                for b in range(NBLK):
                    last = pe.transpose(PA[:, b // 4, b % 4 * P:(b % 4 + 1) * P],
                                        WK[:, g, b * P:(b + 1) * P], IDN[:])
                    if b % 4 == 3:
                        last.then_inc(av_turned, 1)

            def mixing(g):
                pe.wait_ge(av_turned_out, 2 * g + 2)
                if g:
                    pe.wait_ge(mixed, g)
                for b in range(NBLK):
                    last = pe.matmul(PA[:, 2 + b // 4, b % 4 * P:(b % 4 + 1) * P],
                                     WK[:, 8 + g % 2, b * P:(b + 1) * P], WK[:, 10, g * P:(g + 1) * P],
                                     start=True, stop=True)
                last.then_inc(mix_done, 1)

            pe.wait_ge(mix_w_masked, 1)
            for g in range(KT):
                gating_transposes(g)
                unit(Unit(U_QKV + 6 + g))
                mixing(g)
            units(U_QKV + 6 + KT, 18 - KT)
            units(U_AU, 8)

            def v_transposes(pair, q):
                if q == 0:
                    pe.wait_ge(v_in, pair.count(16, 16))
                for b in range(4):
                    last = pe.transpose(PA[:, q, b * P:(b + 1) * P],
                                        VT[:, (4 * q + b) * P:(4 * q + b + 1) * P], IDN[:])
                last.then_inc(v_turned, 1)

            def score_chunk(pair, m, n):
                i, c, w = chunks_of(m)[n]
                base, sb = steps_before(m), m % 2
                bank = 0 if sb and n % 2 else 2
                if n == 0 and sb == 0:
                    pe.wait_ge(q_lo, pair.count(2, m // 2 + 1))
                    pe.wait_ge(k_lo, pair.count(2, m // 2 + 1))
                if m == 1 and n == 1:
                    pe.wait_ge(v_lo, pair.count(2, 1))
                if n >= 1 + sb:
                    pe.wait_ge(biased_done, pair.count(24, base + n - sb))
                elif sb and n == 0:
                    pe.wait_ge(biased_done, pair.count(24, base))
                dst = PA[:, bank, 0:w]
                pe.matmul(dst, QS[:, i * P:(i + 1) * P], KH[:, c:c + w], start=True, stop=False)
                pe.matmul(dst, QS[:, i * P:(i + 1) * P], KL[:, c:c + w], start=False, stop=True
                          ).then_inc(att_scores, 1)

            def turn_p(pair, m, k):
                base, sb = steps_before(m), m % 2
                bank = k % 2 if sb else 1
                if k == 0:
                    pe.wait_ge(p_normed, pair.count(16, 4 * m + 4))
                    if m == 0:
                        pe.wait_ge(v_lo, pair.count(2, 2))
                if k >= 1 + sb:
                    pe.wait_ge(pl_made, pair.count(24, base + k - sb))
                for b in range(max(0, k - 4 * sb), 4):
                    last = pe.transpose(PA[:, bank, b * P:(b + 1) * P], PBS[sb][:, b, k * P:(k + 1) * P],
                                        IDN[:])
                last.then_inc(p_turned, 1)

            def weigh_v(pair, m, k):
                base, sb = steps_before(m), m % 2
                pe.wait_ge(pl_made, pair.count(24, base + k + 1))
                if k == 0 and (m or pair.reg is not None or pair.off):
                    pe.wait_ge(y_half, pair.count(4, m))
                lo = max(0, k - 4 * sb) * P
                dst = PA[:, 3, lo:HALF]
                pe.matmul(dst, VHL[:, m // 2, k], PH[:, k % 2, lo:HALF], start=(k == 0), stop=False)
                pe.matmul(dst, VHL[:, m // 2, k], PL[:, k % 2, lo:HALF], start=False,
                          stop=(k == 4 * sb + 3)).then_inc(pv_done, 1)

            def stage(pair, m, before=None, **have):
                def between(g):
                    for kind, n in steps(PE_STEPS[m % 2][g], before=bool(before), first=m == 0):
                        if kind == "s":
                            score_chunk(pair, m, n)
                        elif kind == "t":
                            turn_p(*before, n)
                        elif kind == "o":
                            weigh_v(*before, n)
                        else:
                            v_transposes(pair, n)

                unit(pair.unit(m), between=between)

            all_stages(pe, stage)

            def rest(g):
                for kind, k in steps(PE_REST[g + 1]):
                    (turn_p if kind == "t" else weigh_v)(Pair(PAIRS - 1), 3, k)

            rest(-1)
            unit(Unit(U_PA), ready=(x_ready, 32), between=rest)
            units(U_PA + 1, 7)
            unit(Unit(U_PB), H=MH, L=ML, ready=(m_ready, 22))
            units(U_PB + 1, 7, H=MH, L=ML)
            unit(Unit(U_WO), ready=(x_ready, 40))
            units(U_WO + 1, 6)
            def last_sums(t):
                pe.wait_ge(squares_added, SQ_END + KT - 1)
                pe.wait_ge(squared, SQ_END + KT + t)
                for b in range(4 * t, 4 * t + 4):
                    tok = slice(b * P, (b + 1) * P)
                    pe.matmul(PA[:, 2 * t, b:b + 1], WK[:, 0, tok], ONES[:, 0:1], start=True, stop=False)
                    last = pe.matmul(PA[:, 2 * t, b:b + 1], WK[:, 2 + (KT - 1) % 2, tok], ONES[:, 0:1],
                                     start=False, stop=True)
                last.then_inc(sums_done, 1)

            def first_norm(g):
                if g == 11:
                    last_sums(0)
                if g == 15:
                    spread(6, WK[:, 1], 0, range(1))

            unit(Unit(U_WO + 7), half=last_half, between=first_norm)
            last_sums(1)
            spread(7, WK[:, 1], 0, range(1, 2))

        @block.scalar
        def _(act):
            def split(u):
                if u.reg is None and u.c >= UNITS:
                    return
                act.wait_ge(w_raw[u.slot], u.turn(16, 1))
                if u.c >= 2:
                    act.wait_ge(mm_done, u.count(-1))
                act.copy(WH[:, u.slot], WR[:, u.slot]).then_inc(w_hi, 1)

            def splits(c, n):
                if n >= 2:
                    with act.Fori(0, n // 2) as i:
                        split(Unit(c, i, 2))
                        split(Unit(c + 1, i, 2))
                if n % 2:
                    split(Unit(c + n - 1))

            def square(src, n, scale=1.0):
                if n >= 2:
                    act.wait_ge(squares_added, n - 1)
                act.activation(WK[:, TMP + n % 2], src, ACT.Square, scale=scale).then_inc(squared, 1)

            def root(n, cols=slice(0, NBLK)):
                act.wait_ge(recip_done, n)
                act.activation(RT[:, n % 4, cols], RT[:, n % 4, cols], ACT.Sqrt).then_inc(root_done, 1)

            def rstd(n, dst=R[:], bank=0):
                act.wait_ge(spread_done, n)
                act.copy(dst, one(PA[:, bank:bank + 2])).then_inc(rstd_there, 1)

            act.preload_act_table(ACT.Sqrt)
            split(Unit(0))
            act.wait_ge(vec_in, 16)
            for k in range(KT):
                act.wait_ge(x_in[k], 16)
                act.activation(XH[:, k], XR[:, k], ACT.Copy, scale=vec(V_G1 + k)).then_inc(x_hi_made, 1)
                if k == 3:
                    split(Unit(1))
            for k in range(KT):
                square(XR[:, k], k)
            split(Unit(2))
            root(1)
            for u in range(1, U_OUT):
                split(Unit(u + 2))
                if u == 1:
                    rstd(1)
                if u == AT_Z:
                    act.wait_ge(z_mm, 2)
                    for j in range(2):
                        act.activation(ZE[j], one(PA[:, 2 * j:2 * j + 2]), ACT.Abs, bias=vec(V_BG + j)
                                       ).then_inc(z_abs, 1)
                    act.preload_act_table(ACT.Ln)
                    for j in range(2):
                        act.wait_ge(z_abs, j + 1)
                        act.activation(ZE[j], ZE[j], ACT.Exp, scale=-1.0).then_inc(gla_act, 1)
                    for j in range(2):
                        act.wait_ge(gla_act, j + 1)
                        act.activation(ZE[j], ZE[j], ACT.Ln, bias=1.0).then_inc(gla_act, 1)
                if u == AT_Z + 1:
                    for j in range(2):
                        act.wait_ge(gla_dve, 3 + j)
                        act.activation(ZE[j], ZB[j], ACT.Exp, scale=1.0 / 16).then_inc(gla_act, 1)
                        act.activation(ZZ[j], ZB[j], ACT.Exp, scale=-1.0 / 16).then_inc(gla_act, 1)
                if u == AT_Z + 2:
                    for j in range(2):
                        act.wait_ge(gla_dve, 7 + 3 * j)
                        act.activation(ZE[j], ZE[j], ACT.Exp, scale=1.0 / 16).then_inc(gla_act, 1)
                for n in AT_TURN.get(u, ()):
                    act.wait_ge(gla_turned, n + 1)
                    blocks = slice(4 * (n % 2), 4 * (n % 2) + 4)
                    i = n // 2
                    dst = (KTOK[:, blocks, i * P:(i + 1) * P] if i < 2 else
                           VTOK[:, blocks, (i - 2) * P:(i - 1) * P])
                    act.copy(dst, PA[:, n % 4].rearrange("p (b f) -> p b f", f=P)).then_inc(gla_turned_out, 1)
                if u == AT_SILU:
                    act.wait_ge(evac, U_G + GLA_HEADS)
                    for h in range(GLA_HEADS):
                        act.activation(WK[:, U_G + h], WK[:, U_G + h], ACT.Silu).then_inc(g_silu, 1)
                if u - 1 in AT_NORM:
                    h = AT_NORM.index(u - 1)
                    act.wait_ge(o_recip, h + 1)
                    act.activation(GT, GT, ACT.Sqrt).then_inc(o_rstd, 1)
                if u in AT_O:
                    h = AT_O.index(u)
                    act.wait_ge(o_done, h + 1)
                    act.copy(MIXED[h], one(PA[:, 2:4])).then_inc(o_out_done, 1)
                    act.wait_ge(o_out_done, h + 1)
                    if h:
                        act.wait_ge(o_summed, h)
                    act.activation(GSQ, MIXED[h], ACT.Square).then_inc(o_squared, 1)
                for k in AT_SPLIT.get(u, ()):
                    if k < 4:
                        act.wait_ge(o_gated, k + 1)
                    else:
                        act.wait_ge(conv_out, k - 3)
                    act.copy(MIX_H[k], MIXED[k]).then_inc(x_hi_made, 1)

            def hi_part(k, src, scale=None):
                if scale is None:
                    act.copy(XH[:, k], src).then_inc(x_hi_made, 1)
                else:
                    act.activation(XH[:, k], src, ACT.Copy, scale=scale).then_inc(x_hi_made, 1)

            for k in range(KT):
                split(Unit(U_OUT + k + 2))
                act.wait_ge(evac, U_OUT + k + 1)
                hi_part(k, XR[:, k], vec(V_G2 + k))
                square(XR[:, k], SQ_NORM2 + k)
            root(2)
            rstd(2)

            act.preload_act_table(ACT.Silu)
            act.wait_ge(gla_dve, GD_ALL + 1)
            for n, (first, tiles, down) in enumerate(FFN):
                with act.Fori(0, tiles) as i:
                    u = Unit(first, i, 2)
                    split(u.plus(2))
                    act.wait_ge(evac, u.count(1))
                    act.activation(WK[:, TMP + 1], WK[:, TMP], ACT.Silu).then_inc(silu_done, 1)
                    split(u.plus(3))
                    act.wait_ge(m_made, i + (8 * n + 1))
                    act.copy(MH[:, i], WK[:, TMP + 3]).then_inc(m_hi_made, 1)
                if n < 2:
                    splits(down + 2, 8)
                else:
                    for k in range(8):
                        split(Unit(down + 2 + k))
                        act.wait_ge(evac, down + k + 1)
                        hi_part(k, XR[:, k], GG[:, k:k + 1])
                        square(XR[:, k], SQ_F + 2 * k)
                        square(XR[:, k], SQ_F + 2 * k + 1, vec(V_GF + k))

            act.wait_ge(recip_done, 4)
            root(3)
            root(4)
            rstd(3, WK[:, 9])
            rstd(4, bank=2)
            for k in range(KT):
                split(Unit(U_AV + k + 2))
                act.wait_ge(evac, U_AV + k + 1)
                act.activation(WK[:, k], WK[:, 12 + k % 2], ACT.Gelu_apprx_tanh).then_inc(av_gelu, 1)
                act.wait_ge(av_gelu, k + 1)
                square(WK[:, k], SQ_V + k)
                act.wait_ge(xr_scaled, k + 1)
                act.dma_start(d_x[k], XR[:, k]).then_inc(stored_x, 16)

            def keep(u, t):
                act.wait_ge(evac, u.count(1))
                act.dma_start(d_qkv[u.count(-U_QKV)], WK[:, 12 + t]).then_inc(stored_ring[t], 16)

            def keeps(c, n):
                with act.Fori(0, n // 2) as i:
                    for s in range(2):
                        u = Unit(c + s, i, 2)
                        split(u.plus(2))
                        keep(u, s)

            keeps(U_QKV, 2)
            root(5)
            keeps(U_QKV + 2, 2)
            rstd(5, WK[:, TMP + 3])
            keeps(U_QKV + 4, 2)
            for g in range(KT):
                if g >= 2:
                    act.wait_ge(mix_done, g - 1)
                for q in range(2):
                    act.wait_ge(av_turned, 2 * g + q + 1)
                    act.copy(WK[:, 8 + g % 2, q * HALF:(q + 1) * HALF], PA[:, q]).then_inc(av_turned_out, 1)
                u = Unit(U_QKV + 6 + g)
                split(u.plus(2))
                keep(u, g % 2)
            keeps(U_QKV + 6 + KT, 18 - KT)
            def head_q(pair, h):
                act.wait_ge(q_in, pair.count(64, 32 * h + 32))
                act.activation(QS[:], Q2[:], ACT.Copy, scale=DH ** -0.5).then_inc(q_hi, 1)

            def head_k(pair, h):
                act.wait_ge(k_in, pair.count(64, 32 * h + 32))
                act.copy(KH[:], K2[:]).then_inc(k_hi, 1)

            act.preload_act_table(ACT.Gelu_apprx_tanh)
            for k in range(KT):
                u = Unit(U_AU + k)
                split(u.plus(2))
                act.wait_ge(evac, u.count(1))
                act.activation(WK[:, 14 + k % 2], WK[:, 12 + k % 2], ACT.Gelu_apprx_tanh).then_inc(au_gelu, 1)
                act.wait_ge(mixed_gated, k + 1)
                act.dma_start(d_mix[k], WK[:, k]).then_inc(stored_mixed, 16)
                if k == 4:
                    head_q(Pair(0), 0)
                    head_k(Pair(0), 0)

            def exp_block(pair, m, b):
                sb = m % 2
                w = (4 * sb + b + 1) * P
                act.wait_ge(biased_done, pair.count(24, steps_before(m) + (b + 1) * (sb + 1)))
                p = PBS[sb][:, b, 0:w]
                act.activation(p, p, ACT.Exp, scale=-1.0, bias=STAT[:, 1, b:b + 1],
                               accum_out=STAT[:, 2, b:b + 1]).then_inc(p_exp, 1)

            def p_hi(pair, m, k):
                base, sb = steps_before(m), m % 2
                lo = max(0, k - 4 * sb) * P
                bank = k % 2 if sb else 1
                act.wait_ge(p_turned, pair.count(24, base + k + 1))
                if k >= 2:
                    act.wait_ge(pv_done, pair.count(24, base + k - 1))
                act.copy(PH[:, k % 2, lo:HALF], PA[:, bank, lo:HALF]).then_inc(ph_made, 1)

            def o_part(pair, m):
                act.wait_ge(pv_done, pair.count(24, steps_before(m) + 4 + 4 * (m % 2)))
                act.copy(OT[0:DH], PA[DH:P, 3]).then_inc(o_half, 1)

            def gate(pair, m):
                u = pair.unit(m)
                if m >= 2:
                    act.wait_ge(stored_ring[m - 2], pair.count(16, 16 * 12))
                dst = (WK[:, 14], SBG[:], GAB[:, 0], GAB[:, 1])[m]
                act.wait_ge(evac, u.count(1))
                act.activation(dst, WK[:, 12 + u.slot], ACT.Tanh, scale=0.5).then_inc(gate_act, 1)

            def store(pair, m):
                if m == 0:
                    act.wait_ge(ya_gated, pair.count(1, 1))
                    act.dma_start(d_ya[pair.index()], MXL[:]).then_inc(stored_ya, 16)
                elif m >= 2:
                    act.wait_ge(gate_act, pair.count(4, m + 1))
                    act.dma_start((d_ga, d_gb)[m - 2][pair.index()], GAB[:, m - 2]).then_inc(stored_ring[m - 2], 16)

            def store_y(pair):
                act.wait_ge(yb_gated, pair.count(1, 1))
                act.dma_start(d_yb[pair.index()], Y[:]).then_inc(stored_x, 16)

            def stage(pair, m, before=None, done=None, head=True):
                if m == 1 and not done:
                    act.wait_ge(stored_mixed, 16 * KT)
                for kind, n in steps(ACT_STEPS[m % 2], bool(before), bool(done), head, m < 2):
                    if kind == "e":
                        exp_block(pair, m, n)
                    elif kind == "p":
                        p_hi(*before, n)
                    elif kind == "O":
                        o_part(*done)
                    elif kind == "q":
                        head_q(*after(pair, m))
                    elif kind == "k":
                        head_k(pair, m // 2)
                    elif kind == "w":
                        split(pair.unit(m).plus(1))
                    elif kind == "a":
                        gate(*before)
                    elif kind == "d":
                        store(*before)
                    elif kind == "y" and m == 1:
                        store_y(done[0])
                    elif kind == "v" and m == 1:
                        if n == 0 and done:
                            act.wait_ge(pv_done, pair.count(24, 0))
                        act.wait_ge(v_turned, pair.count(2, n + 1))
                        act.copy(VHL[:, :, 4 * n:4 * n + 4, 0:DH].rearrange("p h b d -> p b h d"),
                                 PA[:, n].rearrange("p (b h d) -> p b h d", h=2, d=DH)).then_inc(v_hi, 1)

            act.preload_act_table(ACT.Exp)
            all_stages(act, stage)
            final = Pair(PAIRS - 1)
            act.wait_ge(mm_done, U_PA)
            for kind, k in steps(REST):
                if kind == "O":
                    o_part(final, 2)
                elif kind == "p":
                    p_hi(final, 3, k)
                elif kind == "w":
                    split(Unit(U_PA + 1))
                elif kind == "X":
                    act.wait_ge(ya_in[k % 3], 16 * (k // 3 + 1))
                    hi_part(k, XR[:, k % 3], 0.5)
            o_part(final, 3)
            gate(final, 3)
            store(final, 3)
            split(Unit(U_PA + 2))
            store_y(final)

            def loaded(n):
                act.wait_ge(ring_in[n % 2], 16 * (n // 2 + 1))

            def gains(t):
                for i, k in enumerate(ENDED_BY_ACT):
                    dst = XR[:, k, t * HALF:(t + 1) * HALF]
                    act.wait_ge(fin_pool, len(ENDED_BY_ACT) * t + i + 1)
                    act.activation(dst, dst, ACT.Copy, scale=vec(V_FIN + k)).then_inc(fin_act, 1)

            for k in range(KT):
                n = LD_GA + 2 * k + 1
                if k:
                    split(Unit(U_PA + k + 2))
                loaded(n)
                if k == 0:
                    for t in range(2):
                        act.wait_ge(stored_ring[t], 16 * (12 + KT))
                    act.wait_ge(stored_x, 16 * 2 * KT)
                act.activation(MH[:, k], WK[:, TMP + n % 2], ACT.Copy, scale=0.5).then_inc(m_hi_made, 1)
            for k in range(KT):
                split(Unit(U_PB + k + 2))
                act.wait_ge(merged, k + 1)
                hi_part(k, XR[:, k], 0.5)
            for k in range(KT):
                split(Unit(U_WO + k + 2))
                n = SQ_END + k
                if k >= 2:
                    act.wait_ge(squares_added, n - 1)
                if k < KT - 1:
                    act.wait_ge(evac, U_WO + k + 1)
                    act.activation(WK[:, 2 + n % 2], XR[:, k], ACT.Square).then_inc(squared, 1)
            act.preload_act_table(ACT.Sqrt)
            for t in range(2):
                tok = slice(t * HALF, (t + 1) * HALF)
                act.wait_ge(evac, U_WO + KT + t)
                act.activation(WK[:, 2 + n % 2, tok], XR[:, KT - 1, tok], ACT.Square).then_inc(squared, 1)
                root(6 + t, slice(4 * t, 4 * t + 4))
                if t:
                    gains(0)
                act.wait_ge(spread_done, 6 + t)
                act.copy(R[:, tok], PA[:, t]).then_inc(rstd_there, 1)
            gains(1)

        @block.vector
        def _(dve):
            def lo_part(k, src, n, scale=None, H=XH, L=XL, made=x_hi_made, ready=x_ready):
                dve.wait_ge(made, n)
                if scale is None:
                    dve.tensor_tensor(L[:, k], src, H[:, k].bitcast(f32), ALU.subtract).then_inc(ready, 1)
                else:
                    dve.scalar_tensor_tensor(L[:, k], src, scale, H[:, k].bitcast(f32),
                                             ALU.mult, ALU.subtract).then_inc(ready, 1)

            def add_square(n, first, dst, src=None):
                src = WK[:, TMP + n % 2] if src is None else src
                dve.wait_ge(squared, n + 1)
                if first:
                    dve.tensor_copy(dst, src).then_inc(squares_added, 1)
                else:
                    dve.wait_ge(squares_added, n)
                    dve.tensor_tensor(dst, dst, src, ALU.add).then_inc(squares_added, 1)

            def mean_recip(n, width=D, bank=0, cols=slice(0, NBLK)):
                dst = RT[:, n % 4, cols]
                dve.wait_ge(sums_done, n)
                chain(dve.tensor_scalar(dst, PA[:, bank, cols], 1.0 / width, EPS, ALU.mult, ALU.add))
                dve.reciprocal(dst, dst).then_inc(recip_done, 1)

            def diagonals(n, dst, blocks=range(NBLK)):
                dve.wait_ge(root_done, n)
                b0, b1 = blocks[0], blocks[-1] + 1
                dve.tensor_tensor(dst[:, b0 * P:b1 * P].rearrange("p (b t) -> p b t", t=P),
                                  IDN[:].unsqueeze(1).to_broadcast([P, b1 - b0, P]),
                                  RT[:, n % 4, b0:b1].unsqueeze(2).to_broadcast([P, b1 - b0, P]),
                                  ALU.mult).then_inc(diagonal_done, 1)

            in_row = [0]

            def chain(ins):
                in_row[0] += 1
                ins.then_inc(dve_step, 1)
                dve.wait_ge(dve_step, in_row[0])

            def scaled(u, dst):
                dve.wait_ge(mm_done, u.count(1))
                return dve.tensor_tensor(dst, PD[:, u.slot], R[:], ALU.mult).then_inc(evac, 1)

            dve.wait_ge(vec_in, 16)
            for k in range(KT):
                lo_part(k, XR[:, k], k + 1, vec(V_G1 + k))
            for k in range(KT):
                add_square(k, k == 0, WK[:, TMP + 2])

            def raw(u):
                dve.wait_ge(mm_done, u + 1)
                dve.tensor_copy(WK[:, u], PD[:, u]).then_inc(evac, 1)

            raw(0)
            mean_recip(1)
            dve.wait_ge(tab_in, 32)
            diagonals(1, WK[:, TMP + 3])
            raw(1)
            dve.wait_ge(evac, 2)
            dve.wait_ge(rstd_there, 1)
            for u in range(2):
                dve.tensor_tensor(WK[:, u], WK[:, u], R[:], ALU.mult).then_inc(a_there, 1)
            def gla_gates(stage):
                for j in range(2):
                    q, k = WK[:, U_Q + j], WK[:, U_K + j]
                    E, Z, B = ZE[j], ZZ[j], ZB[j]
                    b3 = B.rearrange("p (c t) -> p c t", t=CHUNK)
                    e3 = E.rearrange("p (c t) -> p c t", t=CHUNK)
                    if stage == 1:
                        dve.wait_ge(gla_act, 5 + 2 * j)
                        dve.scalar_tensor_tensor(q, q, DK ** -0.5, E, ALU.mult, ALU.mult).then_inc(gla_dve, 1)
                        dve.tensor_copy(DEC[:, j], e3[:, :, CHUNK - 1]).then_inc(gla_dve, 1)
                        dve.wait_ge(gla_dve, 6 + 3 * j)
                        dve.tensor_tensor(e3, b3[:, :, CHUNK - 1:CHUNK].to_broadcast([P, NCH, CHUNK]), b3,
                                          ALU.subtract).then_inc(gla_dve, 1)
                    if stage == 2:
                        dve.wait_ge(gla_act, 9 + j)
                        dve.tensor_tensor(KS[:, j], k, E, ALU.mult).then_inc(gla_dve, 1)
                        dve.wait_ge(gla_dve, 11 + 2 * j)
                        dve.tensor_tensor(k, k, Z, ALU.mult).then_inc(gla_dve, 1)

            def gla_decays():
                dve.wait_ge(z_abs, 2)
                for j in range(2):
                    dve.tensor_scalar(ZZ[j], one(PA[:, 2 * j:2 * j + 2]), vec(V_BG + j), None, ALU.add
                                      ).then_inc(z_add, 1)
                for j in range(2):
                    dve.wait_ge(gla_act, 3 + j)
                    dve.wait_ge(z_add, j + 1)
                    dve.scalar_tensor_tensor(ZZ[j], ZZ[j], 0.0, ZE[j], ALU.min, ALU.subtract).then_inc(gla_dve, 1)
                dve.wait_ge(gla_consts, 2)
                for j in range(2):
                    dve.wait_ge(gla_dve, 1 + j)
                    dve.tensor_tensor_scan(ZB[j], RESET, ZZ[j], 0.0, ALU.mult, ALU.add).then_inc(gla_dve, 1)

            def gla_states(j):
                chain(dve.memset(ST[:, j, 0], 0.0))
                for c in range(NCH - 1):
                    if c % 8 == 0:
                        dve.wait_ge(kv_done, 2 * j + c // 8 + 1)
                    if c:
                        dve.wait_ge(state_done, (NCH - 1) * j + c)
                    half, blk = c % 2, c // 2
                    dve.scalar_tensor_tensor(ST[:, j, c + 1], ST[:, j, c], DEC[:, j, c:c + 1],
                                             PA[:, 2 * half + blk // 4, blk % 4 * DV:(blk % 4 + 1) * DV],
                                             ALU.mult, ALU.add).then_inc(state_done, 1)

            def gla_scores(h):
                dve.wait_ge(scores_done, h + 1)
                dve.wait_ge(gla_consts, 4)
                if h >= 2:
                    dve.wait_ge(o_done, h - 1)
                ps = PA[:, 0:2].rearrange("p a (b t) -> p (a b) t", t=P)
                for half in range(2):
                    rows = slice(half * CHUNK, (half + 1) * CHUNK)
                    last = dve.tensor_copy(SC[rows, h % 2, :, rows], ps[rows, :, rows])
                last.then_inc(scores_out, 1)

            def gla_norm(h):
                dve.wait_ge(o_summed, h + 1)
                if h:
                    dve.wait_ge(o_gated, h)
                dve.tensor_scalar(GT, one(PA[:, 2:4]), 1.0 / DV, EPS, ALU.mult, ALU.add).then_inc(o_mean_done, 1)

            def gla_gate(h):
                O = MIXED[h]
                dve.wait_ge(o_mean_done, h + 1)
                dve.reciprocal(GT, GT).then_inc(o_recip, 1)
                dve.wait_ge(g_silu, GLA_HEADS)
                chain(dve.tensor_tensor(O, O, WK[:, U_G + h], ALU.mult))
                dve.wait_ge(o_rstd, h + 1)
                dve.scalar_tensor_tensor(O, O, vec(V_GN), GT, ALU.mult, ALU.mult).then_inc(o_gated, 1)

            for u in range(U_OUT):
                T, A = WK[:, TMP], WK[:, TMP + 1]
                c, part = (u - U_CONV) // 3, (u - U_CONV) % 3
                if u < 2:
                    continue
                if u < U_CONV:
                    scaled(Unit(u), WK[:, u])
                elif part == 0:
                    if c:
                        dve.wait_ge(conv_out, c)
                    scaled(Unit(u), T)
                elif part == 1:
                    O = MIXED[4 + c]
                    dve.wait_ge(evac, u)
                    dve.wait_ge(mm_done, u + 1)
                    dve.tensor_tensor(T, PD[:, u % 2], T, ALU.mult).then_inc(evac, 1)
                    dve.wait_ge(evac, u + 1)
                    chain(dve.tensor_tensor(A, T, R[:], ALU.mult))
                    w = [vec(V_CW + 3 * c + t) for t in range(3)]
                    chain(dve.tensor_scalar(O, A, w[2], None, ALU.mult))
                    chain(dve.scalar_tensor_tensor(O[:, 1:S], A[:, 0:S - 1], w[1], O[:, 1:S], ALU.mult, ALU.add))
                    chain(dve.scalar_tensor_tensor(O[:, 2:S], A[:, 0:S - 2], w[0], O[:, 2:S], ALU.mult, ALU.add))
                else:
                    O = MIXED[4 + c]
                    scaled(Unit(u), T)
                    dve.wait_ge(evac, u + 1)
                    dve.tensor_tensor(O, T, O, ALU.mult).then_inc(conv_out, 1)
                if u == AT_Z:
                    gla_decays()
                if u in (AT_Z + 1, AT_Z + 2):
                    gla_gates(u - AT_Z)
                if u in AT_KV:
                    gla_states(AT_KV.index(u))
                if u in AT_SCORES:
                    gla_scores(AT_SCORES.index(u))
                if u in AT_NORM:
                    gla_norm(AT_NORM.index(u))
                if u - 1 in AT_NORM:
                    gla_gate(AT_NORM.index(u - 1))
                for k in AT_SPLIT.get(u, ()):
                    dve.wait_ge(x_hi_made, 8 + k + 1)
                    dve.tensor_tensor(MIX_L[k], MIXED[k], MIX_H[k].bitcast(f32), ALU.subtract
                                      ).then_inc(x_ready, 1)

            def add_to_residual(u, k):
                dve.wait_ge(mm_done, u.count(1))
                dve.tensor_tensor(XR[:, k], PD[:, u.slot], XR[:, k], ALU.add).then_inc(evac, 1)

            for k in range(KT):
                dve.wait_ge(x_in[k], 32)
                add_to_residual(Unit(U_OUT + k), k)
                lo_part(k, XR[:, k], 16 + k + 1, vec(V_G2 + k))
                add_square(SQ_NORM2 + k, k == 0, WK[:, TMP + 2])
            mean_recip(2)
            diagonals(2, WK[:, TMP + 3])
            dve.wait_ge(rstd_there, 2)

            dve.tensor_tensor(GG[:], vec(V_GF, KT), vec(V_H2, KT), ALU.mult).then_inc(gla_dve, 1)
            dve.wait_ge(gla_dve, GD_ALL + 1)

            for n, (first, tiles, down) in enumerate(FFN):
                with dve.Fori(0, tiles) as i:
                    u = Unit(first, i, 2)
                    scaled(u, WK[:, TMP])
                    scaled(u.plus(1), WK[:, TMP + 2])
                    dve.wait_ge(evac, u.count(2))
                    dve.wait_ge(silu_done, i + (8 * n + 1))
                    dve.tensor_tensor(WK[:, TMP + 3], WK[:, TMP + 1], WK[:, TMP + 2], ALU.mult).then_inc(m_made, 1)
                    dve.wait_ge(m_hi_made, i + (8 * n + 1))
                    dve.tensor_tensor(ML[:, i], WK[:, TMP + 3], MH[:, i].bitcast(f32), ALU.subtract
                                      ).then_inc(m_ready, 1)
                for k in range(KT):
                    add_to_residual(Unit(down + k), k)
                    if n == 2:
                        lo_part(k, XR[:, k], 24 + k + 1, GG[:, k:k + 1])
                        for t in range(2):
                            m = SQ_F + 2 * k + t
                            dve.wait_ge(squared, m + 1)
                            dst = WK[:, TMP + 2 + t]
                            if k == 0:
                                dve.tensor_copy(dst, WK[:, TMP + t]).then_inc(squares_added, 1)
                            else:
                                dve.wait_ge(squares_added, m - 1)
                                dve.tensor_tensor(dst, dst, WK[:, TMP + t], ALU.add).then_inc(squares_added, 1)

            mean_recip(3)
            V, U = RT[:, 0], RT[:, 3]
            dve.wait_ge(sums_done, 4)
            dve.wait_ge(recip_done, 3)
            chain(dve.scalar_tensor_tensor(V, PA[:, 2, 0:NBLK], 1.0 / D, U, ALU.mult, ALU.mult))
            chain(dve.tensor_scalar(V, V, EPS, None, ALU.add))
            chain(dve.reciprocal(V, V))
            chain(dve.tensor_tensor(V, V, U, ALU.mult))
            dve.sem_inc(recip_done, 1)
            diagonals(3, WK[:, 8])
            diagonals(4, WK[:, TMP + 3])
            dve.wait_ge(rstd_there, 4)
            for k in range(KT):
                if k >= 2:
                    dve.wait_ge(av_gelu, k - 1)
                scaled(Unit(U_AV + k), WK[:, 12 + k % 2])
                add_square(SQ_V + k, k == 0, WK[:, TMP + 2])
                dve.scalar_tensor_tensor(XR[:, k], XR[:, k], vec(V_GF + k), WK[:, 9], ALU.mult, ALU.mult
                                         ).then_inc(xr_scaled, 1)

            def keep(u, first=False):
                if not first:
                    dve.wait_ge(stored_ring[u.slot ^ 1], (u.plus(-U_QKV)).turn(16, 0))
                scaled(u, WK[:, 12 + (u.slot ^ 1)])

            for s in range(2):
                dve.wait_ge(av_gelu, KT)
                keep(Unit(U_QKV + s), True)
            RV = WK[:, TMP + 3]
            mean_recip(5)
            diagonals(5, WK[:, 8])
            for k in range(2):
                keep(Unit(U_QKV + 2 + k))
            dve.wait_ge(rstd_there, 5)
            for g in range(KT):
                dve.scalar_tensor_tensor(WK[:, g], WK[:, g], vec(V_GV + g), RV, ALU.mult, ALU.mult
                                         ).then_inc(av_normed, 1)
            for k in range(2):
                keep(Unit(U_QKV + 4 + k))
            for g in range(KT):
                keep(Unit(U_QKV + 6 + g))
                dve.wait_ge(mix_done, g + 1)
                dve.tensor_tensor(WK[:, g].rearrange("p (b t) -> p b t", t=P),
                                  PA[:, 2:4].rearrange("p a (b t) -> p (a b) t", t=P),
                                  WK[:, 11, g * P:(g + 1) * P].unsqueeze(1).to_broadcast([P, NBLK, P]),
                                  ALU.add).then_inc(mixed, 1)
            with dve.Fori(0, (18 - KT) // 2) as i:
                for s in range(2):
                    keep(Unit(U_QKV + 6 + KT + s, i, 2))
            def head_bias(pair, h):
                dve.scalar_tensor_tensor(BH[:], DIST[:], VEC[:, bass.ds(pair.index(2, V_SL + h), 1)],
                                         LOGM[:], ALU.mult, ALU.add).then_inc(bias, 1)

            def head_q(pair, h):
                dve.wait_ge(q_hi, pair.count(2, h + 1))
                dve.scalar_tensor_tensor(QS[DH:P], Q2[DH:P], DH ** -0.5, QS[DH:P].bitcast(f32),
                                         ALU.mult, ALU.subtract).then_inc(q_lo, 1)

            def head_k(pair, h):
                dve.wait_ge(k_hi, pair.count(2, h + 1))
                dve.tensor_tensor(KL[:], K2[:], KH[:].bitcast(f32), ALU.subtract).then_inc(k_lo, 1)

            for s in range(2):
                dve.wait_ge(stored_ring[s], 16 * 12)
            for k in range(KT):
                if k >= 2:
                    dve.wait_ge(au_gelu, k - 1)
                scaled(Unit(U_AU + k), WK[:, 12 + k % 2])
                dve.wait_ge(au_gelu, k + 1)
                dve.wait_ge(mixed, KT)
                dve.tensor_tensor(WK[:, k], WK[:, k], WK[:, 14 + k % 2], ALU.mult).then_inc(mixed_gated, 1)
                if k == 4:
                    dve.wait_ge(tab_in, 64)
                    head_bias(Pair(0), 0)
                    head_q(Pair(0), 0)
                    head_k(Pair(0), 0)

            def biased(pair, m, n):
                i, c0, w = chunks_of(m)[n]
                base, sb = steps_before(m), m % 2
                b, c = i - 4 * sb, c0 // HALF
                bank = 0 if sb and n % 2 else 2
                if n == 0 and sb == 0:
                    dve.wait_ge(bias, pair.count(2, m // 2 + 1))
                    dve.sem_inc(turns, 1)
                if c:
                    dve.wait_ge(biased_done, pair.count(24, base + n))
                dve.wait_ge(att_scores, pair.count(24, base + n + 1))
                dve.sem_inc(turns, 1)
                u0 = S - P - i * P + c0
                dve.tensor_tensor_reduce(
                    out=PBS[sb][:, b, c0:c0 + w], in0=PA[:, bank, 0:w], in1=BH[:, u0:u0 + w],
                    scale=-1.0, scalar=(STAT[:, 0, b:b + 1] if c else 3.0e38), op0=ALU.add, op1=ALU.min,
                    accum_out=STAT[:, (1 if c == sb else 0), b:b + 1]).then_inc(biased_done, 1)

            def normed(pair, m, b):
                sb = m % 2
                p = PBS[sb][:, b, 0:(4 * sb + b + 1) * P]
                n = pair.count(16, 4 * m + b + 1)
                dve.wait_ge(p_exp, n)
                dve.reciprocal(STAT[:, 3, b:b + 1], STAT[:, 2, b:b + 1]).then_inc(sum_recip, 1)
                dve.wait_ge(sum_recip, n)
                dve.tensor_scalar(p, p, STAT[:, 3, b:b + 1], None, ALU.mult).then_inc(p_normed, 1)

            def p_lo(pair, m, k):
                base, sb = steps_before(m), m % 2
                lo = max(0, k - 4 * sb) * P
                bank = k % 2 if sb else 1
                dve.wait_ge(ph_made, pair.count(24, base + k + 1))
                dve.tensor_tensor(PL[:, k % 2, lo:HALF], PA[:, bank, lo:HALF],
                                  PH[:, k % 2, lo:HALF].bitcast(f32), ALU.subtract).then_inc(pl_made, 1)

            def o_out(pair, m):
                h, sb = m // 2, m % 2
                dve.wait_ge(o_half, pair.count(4, m + 1))
                if m == 0:
                    dve.wait_ge(stored_x, pair.count(16, 16 * KT))
                dve.tensor_tensor(Y[h * DH:(h + 1) * DH, sb * HALF:(sb + 1) * HALF], PA[0:DH, 3],
                                  OT[0:DH], ALU.add).then_inc(y_half, 1)

            def gate(pair, m):
                if m < 2:
                    T = (WK[:, 14], SBG[:])[m]
                    dve.wait_ge(gate_act, pair.count(4, m + 1))
                    dve.scalar_tensor_tensor(T, T, 1.0, WK[:, 12 + pair.unit(m).slot], ALU.add, ALU.mult
                                             ).then_inc(gated, 1)

            def stage(pair, m, before=None, done=None, head=True):
                if m == 1 and not done:
                    dve.wait_ge(stored_mixed, 16 * KT)
                for kind, n in steps(DVE_STEPS[m % 2], bool(before), bool(done), head, m < 2):
                    if kind == "r":
                        biased(pair, m, n)
                    elif kind == "n":
                        normed(pair, m, n)
                    elif kind == "l":
                        p_lo(*before, n)
                    elif kind == "O":
                        o_out(*done)
                    elif kind == "b":
                        head_bias(*after(pair, m))
                    elif kind == "q":
                        head_q(*after(pair, m))
                    elif kind == "k":
                        head_k(pair, m // 2)
                    elif kind == "z":
                        u = before[0].unit(before[1])
                        if before[1] >= 2:
                            dve.wait_ge(gate_act, before[0].count(4, before[1] - 1))
                        scaled(u, WK[:, 12 + u.slot])
                    elif kind == "m":
                        gate(*before)
                    elif kind == "v" and m == 1:
                        dve.wait_ge(v_hi, pair.count(2, n + 1))
                        blk = VHL[:, :, 4 * n:4 * n + 4].rearrange("p h b d -> p b h d")
                        dve.tensor_tensor(blk[:, :, :, DH:P],
                                          PA[:, n].rearrange("p (b h d) -> p b h d", h=2, d=DH),
                                          blk[:, :, :, 0:DH].bitcast(f32), ALU.subtract).then_inc(v_lo, 1)

            all_stages(dve, stage)
            final = Pair(PAIRS - 1)
            for kind, k in steps(REST):
                if kind == "O":
                    o_out(final, 2)
                elif kind == "p":
                    p_lo(final, 3, k)
                elif kind == "z":
                    dve.wait_ge(gate_act, final.count(4, 2))
                    scaled(final.unit(3), WK[:, 12 + final.unit(3).slot])
                elif kind == "X":
                    lo_part(k, XR[:, k % 3], 32 + k + 1, 0.5)
            o_out(final, 3)

            def loaded(n):
                dve.wait_ge(ring_in[n % 2], 16 * (n // 2 + 1))
                return WK[:, TMP + n % 2]

            for k in range(KT):
                n = LD_GA + 2 * k + 1
                u = Unit(U_PA + k)
                dve.wait_ge(mm_done, u.c + 1)
                src = loaded(n - 1)
                dve.scalar_tensor_tensor(XR[:, k], src, 1.0, PD[:, u.slot], ALU.add, ALU.mult
                                         ).then_inc(evac, 1)
                lo_part(k, WK[:, TMP + n % 2], 22 + k + 1, 0.5, H=MH, L=ML, made=m_hi_made, ready=m_ready)
            for k in range(KT):
                u = Unit(U_PB + k)
                src = loaded(LD_GB + k)
                dve.wait_ge(mm_done, u.c + 1)
                T = WK[:, TMP + 2]
                dve.scalar_tensor_tensor(T, src, 1.0, PD[:, u.slot], ALU.add, ALU.mult).then_inc(evac, 1)
                dve.wait_ge(evac, u.c + 1)
                dve.tensor_tensor(XR[:, k], XR[:, k], T, ALU.add).then_inc(merged, 1)
                dve.wait_ge(merged, k + 1)
                lo_part(k, XR[:, k], 40 + k + 1, 0.5)
            for k in range(KT):
                u = Unit(U_WO + k)
                src = loaded(LD_X + k)
                if k < KT - 1:
                    dve.wait_ge(mm_done, u.c + 1)
                    dve.tensor_tensor(XR[:, k], PD[:, u.slot], src, ALU.add).then_inc(evac, 1)
                    add_square(SQ_END + k, k == 0, WK[:, 0], WK[:, 2 + k % 2])

            def ended(t, tiles):
                tok = slice(t * HALF, (t + 1) * HALF)
                for k in tiles:
                    dve.scalar_tensor_tensor(XR[:, k, tok], XR[:, k, tok], vec(V_FIN + k), R[:, tok],
                                             ALU.mult, ALU.mult).then_inc(fin_dve, 1)

            for t in range(2):
                tok = slice(t * HALF, (t + 1) * HALF)
                if t:
                    dve.wait_ge(mm_done, UNITS)
                else:
                    dve.wait_ge(last_half, 1)
                dve.tensor_tensor(XR[:, k, tok], PD[:, u.slot, tok], src[:, tok], ALU.add).then_inc(evac, 1)
                if t:
                    ended(0, ENDED_BY_DVE[:1])
                if t:
                    ended(0, ENDED_BY_DVE[1:2])
                mean_recip(6 + t, bank=2 * t, cols=slice(4 * t, 4 * t + 4))
                diagonals(6 + t, WK[:, 1], range(4 * t, 4 * t + 4))
                if t:
                    ended(0, ENDED_BY_DVE[2:])
                dve.wait_ge(rstd_there, 6 + t)
            ended(1, ENDED_BY_DVE)


def kernel(**inputs):
    import concourse.bacc as bacc
    from concourse.bass_utils import run_bass_kernel_spmd

    f = {k: np.asarray(v) for k, v in inputs.items()}

    def columns(w):
        k, n = w.shape
        t = w.reshape(k // P, P, n // P, P).transpose(2, 1, 0, 3)
        if k < D:
            t = np.concatenate([t, np.zeros((n // P, P, (D - k) // P, P), w.dtype)], axis=2)
        return t.reshape(n // P, P, KT * P)

    w_in, w2 = f["w_in"][0], f["w_in_2"][0]
    edges = np.cumsum([0, 256, 256, 512, 512, RANK, 512, 512, 512])
    q, k, v, g, a, cb, cc, ch = (w_in[:, edges[i]:edges[i + 1]] for i in range(8))
    a = np.concatenate([a, np.zeros((D, P - RANK), a.dtype)], axis=1)
    conv = np.stack([columns(cc), columns(ch), columns(cb)], axis=1).reshape(12, P, D)
    parts = [columns(a), columns(q), columns(k), columns(v), columns(g), conv, columns(f["w_out"][0])]
    gate, up, down = columns(f["w_ffn_gate"][0]), columns(f["w_ffn_up"][0]), f["w_ffn_down"][0]
    tile = 0
    for _, tiles, _ in FFN:
        parts.append(np.stack([gate[tile:tile + tiles], up[tile:tile + tiles]], axis=1).reshape(2 * tiles, P, D))
        parts.append(columns(down[tile * P:(tile + tiles) * P]))
        tile += tiles
    au, av, agate, q, k, v, bgate, ga, gb = (columns(w2[:, i * D:(i + 1) * D]) for i in range(9))
    parts += [av, np.stack([q, k, v], axis=1).reshape(24, P, D), au,
              np.stack([agate, bgate, ga, gb], axis=1).reshape(32, P, D),
              columns(f["w_proj_a_2"][0]), columns(f["w_proj_b_2"][0]), columns(f["w_out_2"][0])]
    weights = np.concatenate(parts)
    assert weights.shape[0] == UNITS

    def tall(x):
        return x.reshape(-1, P).T

    slopes = -np.exp2(-8.0 * np.arange(1, HEADS + 1) / HEADS).astype(np.float32)
    cw = f["conv_w"][0].reshape(3, 4, P).transpose(2, 1, 0).reshape(P, 12)
    vecs = np.concatenate([tall(f["norm1_g"]), tall(f["b_gate"]), tall(f["gla_norm_g"]), cw, tall(f["norm2_g"]),
                           tall(f["norm_f_g"]), tall(f["g_norm_2"]), tall(f["g_v_2"]), tall(f["g_final_2"]),
                           np.broadcast_to(slopes, (P, HEADS))], axis=1)
    d = np.arange(P)[:, None] + (S - P) - np.arange(S)[None, :]
    count = sum(((d % r == 0) & (d <= w)).astype(np.float64) for w, r in ((128, 1), (512, 4), (2048, 16)))
    count = count * (d >= 0)
    logm = np.where(count > 0, np.log(np.maximum(count, 1)), -1e30).astype(np.float32)
    dist = np.where(count > 0, d, 0).astype(np.float32)

    arrays = {
        "xT": f["x"][0].T.reshape(KT, P, S), "weights": weights, "vecs": vecs, "gate_up": f["w_gate_up"][0],
        "mix_w": f["w_s_2"][0].transpose(2, 0, 1).reshape(P, D),
        "mix_b": np.broadcast_to(f["b_s_2"].reshape(1, D), (P, D)),
        "dist": dist, "logm": logm, "ident": np.eye(P, dtype=np.float32),
    }
    arrays = {k: np.ascontiguousarray(v) for k, v in arrays.items()}
    nc = bacc.Bacc("TRN2", target_bir_lowering=False, num_devices=1)
    aps = [nc.dram_tensor(k, v.shape, mybir.dt.from_np(v.dtype), kind="ExternalInput").ap()
           for k, v in arrays.items()]
    out = nc.dram_tensor("out", (KT, P, S), mybir.dt.float32, kind="ExternalOutput").ap()
    two_blocks(nc, *aps, out)
    r = run_bass_kernel_spmd(nc, [arrays], core_ids=[0])
    return np.ascontiguousarray(np.asarray(r.results[0]["out"]).reshape(D, S).T).reshape(1, S, D)
```
